# Optimizing a Trainium2 kernel written in Bass

```python
import jax, jax.numpy as jnp
from jax import lax
import numpy as np

D_MODEL = 1024
BATCH = 1
SEQ = 512
DEPTH = 2
DEC_BATCH = 1
DEC_SEQ = 256
PAST_LEN = 128

GRID_W = 64
NORM_EPS = 1e-6
GLA_HEADS = 4
GLA_DK = 64
GLA_DV = 128
GLA_RANK = 16
GLA_GATE_NORM = 16.0
GLA_CHUNK = 64
FNET_GROUPS = 4
FNET_GW = 128
ATTN_HEADS = 8
KV_HEADS = 2
HEAD_DIM = 128
ROPE_THETA = 10000.0
Q_BLOCK = 128
FFN_HIDDEN = -(-8 * D_MODEL // (3 * 256)) * 256
AB_IN = 2 * GLA_HEADS * GLA_DK + 2 * GLA_HEADS * GLA_DV + 2 * GLA_RANK + FNET_GROUPS * FNET_GW
AB_OUT = GLA_HEADS * GLA_DV + FNET_GROUPS * FNET_GW
C_IN = (ATTN_HEADS + 2 * KV_HEADS) * HEAD_DIM

kernel_name = 'hybrid_gla_fnet_axial_gqa_encoder'

def rms_norm(x, gain):
    xf = x.astype(jnp.float32)
    y = xf * lax.rsqrt(jnp.mean(xf * xf, axis=-1, keepdims=True) + NORM_EPS)
    return (y * gain.astype(jnp.float32)).astype(x.dtype)

def gla_direction(q, k, v, g):
    b_, s_, h_, dk = q.shape
    dv = v.shape[-1]
    n = s_ // GLA_CHUNK
    qc = q.reshape(b_, n, GLA_CHUNK, h_, dk)
    kc = k.reshape(b_, n, GLA_CHUNK, h_, dk)
    vc = v.reshape(b_, n, GLA_CHUNK, h_, dv)
    gc = g.reshape(b_, n, GLA_CHUNK, h_, dk)
    bcum = jnp.cumsum(gc, axis=2)
    q_in = qc * jnp.exp(bcum)
    k_in = kc * jnp.exp(-bcum)
    lower = jnp.tril(jnp.ones((GLA_CHUNK, GLA_CHUNK), dtype=bool))
    att = jnp.where(lower, jnp.einsum('bnihd,bnjhd->bnhij', q_in, k_in), 0.0)
    o_intra = jnp.einsum('bnhij,bnjhe->bnihe', att, vc)
    b_last = bcum[:, :, -1]
    d_state = jnp.einsum('bnjhd,bnjhe->bnhde', kc * jnp.exp(b_last[:, :, None] - bcum), vc)

    def step(state, inp):
        ds, dec = inp
        return dec[..., None] * state + ds, state

    init = jnp.zeros((b_, h_, dk, dv), jnp.float32)
    _, s_prev = lax.scan(step, init, (jnp.moveaxis(d_state, 1, 0), jnp.moveaxis(jnp.exp(b_last), 1, 0)))
    s_prev = jnp.moveaxis(s_prev, 0, 1)
    o_inter = jnp.einsum('bnihd,bnhde->bnihe', q_in, s_prev)
    return (o_intra + o_inter).reshape(b_, s_, h_, dv)

def ab_mixer(x, norm_g, w_in, up_f, bias_f, up_b, bias_b, out_g, w_out):
    b_, s_, _ = x.shape
    f32 = jnp.float32
    h = rms_norm(x, norm_g)
    sizes = [GLA_HEADS * GLA_DK, GLA_HEADS * GLA_DK, GLA_HEADS * GLA_DV, GLA_HEADS * GLA_DV, GLA_RANK, GLA_RANK]
    cuts = [int(c) for c in np.cumsum(sizes)]
    q, k, v, r, lf, lb, f = jnp.split(h @ w_in, cuts, axis=-1)
    q = q.astype(f32).reshape(b_, s_, GLA_HEADS, GLA_DK) * (GLA_DK ** -0.5)
    k = k.astype(f32).reshape(b_, s_, GLA_HEADS, GLA_DK)
    v = v.astype(f32).reshape(b_, s_, GLA_HEADS, GLA_DV)
    g_f = (jax.nn.log_sigmoid(lf.astype(f32) @ up_f.astype(f32) + bias_f.astype(f32)) / GLA_GATE_NORM).reshape(b_, s_, GLA_HEADS, GLA_DK)
    g_b = (jax.nn.log_sigmoid(lb.astype(f32) @ up_b.astype(f32) + bias_b.astype(f32)) / GLA_GATE_NORM).reshape(b_, s_, GLA_HEADS, GLA_DK)
    o_f = gla_direction(q, k, v, g_f)
    o_b = jnp.flip(gla_direction(jnp.flip(q, 1), jnp.flip(k, 1), jnp.flip(v, 1), jnp.flip(g_b, 1)), 1)
    o = rms_norm(o_f + o_b, out_g).reshape(b_, s_, GLA_HEADS * GLA_DV) * jax.nn.silu(r.astype(f32))
    fg = f.astype(f32).reshape(b_, s_, FNET_GROUPS, FNET_GW)
    fo = jnp.real(jnp.fft.fft2(fg, axes=(1, 3), norm='ortho')).reshape(b_, s_, FNET_GROUPS * FNET_GW)
    mixed = jnp.concatenate([o, fo], axis=-1).astype(x.dtype) @ w_out
    return x + mixed

def axial_angles(s_):
    rows = s_ // GRID_W
    row_idx = jnp.repeat(jnp.arange(rows), GRID_W).astype(jnp.float32)
    col_idx = jnp.tile(jnp.arange(GRID_W), rows).astype(jnp.float32)
    half = HEAD_DIM // 2
    inv = ROPE_THETA ** (-jnp.arange(0, half, 2, dtype=jnp.float32) / half)
    return row_idx[:, None] * inv[None, :], col_idx[:, None] * inv[None, :]

def rope_rotate(x, ang):
    m = ang.shape[-1]
    x1, x2 = x[..., :m], x[..., m:]
    c = jnp.cos(ang)[:, None, :]
    s = jnp.sin(ang)[:, None, :]
    return jnp.concatenate([x1 * c - x2 * s, x2 * c + x1 * s], axis=-1)

def apply_axial_rope(x, ang_row, ang_col):
    half = HEAD_DIM // 2
    xf = x.astype(jnp.float32)
    out = jnp.concatenate([rope_rotate(xf[..., :half], ang_row), rope_rotate(xf[..., half:], ang_col)], axis=-1)
    return out.astype(x.dtype)

def c_mixer(x, norm_g, w_in, qn_g, kn_g, w_out):
    b_, s_, _ = x.shape
    h = rms_norm(x, norm_g)
    q, k, v = jnp.split(h @ w_in, [ATTN_HEADS * HEAD_DIM, (ATTN_HEADS + KV_HEADS) * HEAD_DIM], axis=-1)
    q = rms_norm(q.reshape(b_, s_, ATTN_HEADS, HEAD_DIM), qn_g)
    k = rms_norm(k.reshape(b_, s_, KV_HEADS, HEAD_DIM), kn_g)
    v = v.reshape(b_, s_, KV_HEADS, HEAD_DIM)
    ang_row, ang_col = axial_angles(s_)
    q = apply_axial_rope(q, ang_row, ang_col)
    k = apply_axial_rope(k, ang_row, ang_col)
    group = ATTN_HEADS // KV_HEADS
    nblk = s_ // Q_BLOCK
    qb = jnp.moveaxis(q.reshape(b_, nblk, Q_BLOCK, KV_HEADS, group, HEAD_DIM), 1, 0)
    scale = HEAD_DIM ** -0.5

    def block(qblk):
        sc = jnp.einsum('bqkgd,bskd->bkgqs', qblk, k).astype(jnp.float32) * scale
        pr = jax.nn.softmax(sc, axis=-1).astype(v.dtype)
        return jnp.einsum('bkgqs,bskd->bqkgd', pr, v)

    o = lax.map(block, qb)
    o = jnp.moveaxis(o, 0, 1).reshape(b_, s_, ATTN_HEADS * HEAD_DIM)
    return x + o @ w_out

def swiglu_ffn(x, norm_g, w_gate, w_up, w_down):
    h = rms_norm(x, norm_g)
    return x + (jax.nn.silu(h @ w_gate) * (h @ w_up)) @ w_down

def trunk(x, ab_norm, ab_w_in, gla_up_f, gla_bias_f, gla_up_b, gla_bias_b, gla_out_norm, ab_w_out,
          c_norm, c_w_in, c_q_norm, c_k_norm, c_w_out, ffn_norm, ffn_w_gate, ffn_w_up, ffn_w_down):
    for i in range(DEPTH):
        j = i // 2
        if i % 2 == 0:
            x = ab_mixer(x, ab_norm[j], ab_w_in[j], gla_up_f[j], gla_bias_f[j], gla_up_b[j], gla_bias_b[j],
                         gla_out_norm[j], ab_w_out[j])
        else:
            x = c_mixer(x, c_norm[j], c_w_in[j], c_q_norm[j], c_k_norm[j], c_w_out[j])
        x = swiglu_ffn(x, ffn_norm[i], ffn_w_gate[i], ffn_w_up[i], ffn_w_down[i])
    return x

def setup_inputs(seed: int = 0) -> dict:
    key = jax.random.key(seed)
    ks = jax.random.split(key, 24)
    ne = (DEPTH + 1) // 2
    no = DEPTH // 2
    f32 = jnp.float32

    def nrm(k, shape, scale):
        return jax.random.normal(k, shape, f32) * scale

    def gain(k, shape):
        return 1.0 + 0.01 * jax.random.normal(k, shape, f32)

    return {
        'x_prompt': nrm(ks[0], (BATCH, SEQ, D_MODEL), 1.0),
        'x_sample': nrm(ks[1], (DEC_BATCH, DEC_SEQ, D_MODEL), 1.0),
        'ab_norm': gain(ks[2], (ne, D_MODEL)),
        'ab_w_in': nrm(ks[3], (ne, D_MODEL, AB_IN), D_MODEL ** -0.5),
        'gla_up_f': nrm(ks[4], (ne, GLA_RANK, GLA_HEADS * GLA_DK), GLA_RANK ** -0.5),
        'gla_bias_f': nrm(ks[5], (ne, GLA_HEADS * GLA_DK), 0.1),
        'gla_up_b': nrm(ks[6], (ne, GLA_RANK, GLA_HEADS * GLA_DK), GLA_RANK ** -0.5),
        'gla_bias_b': nrm(ks[7], (ne, GLA_HEADS * GLA_DK), 0.1),
        'gla_out_norm': gain(ks[8], (ne, GLA_DV)),
        'ab_w_out': nrm(ks[9], (ne, AB_OUT, D_MODEL), AB_OUT ** -0.5),
        'c_norm': gain(ks[10], (no, D_MODEL)),
        'c_w_in': nrm(ks[11], (no, D_MODEL, C_IN), D_MODEL ** -0.5),
        'c_q_norm': gain(ks[12], (no, HEAD_DIM)),
        'c_k_norm': gain(ks[13], (no, HEAD_DIM)),
        'c_w_out': nrm(ks[14], (no, ATTN_HEADS * HEAD_DIM, D_MODEL), (ATTN_HEADS * HEAD_DIM) ** -0.5),
        'ffn_norm': gain(ks[15], (DEPTH, D_MODEL)),
        'ffn_w_gate': nrm(ks[16], (DEPTH, D_MODEL, FFN_HIDDEN), D_MODEL ** -0.5),
        'ffn_w_up': nrm(ks[17], (DEPTH, D_MODEL, FFN_HIDDEN), D_MODEL ** -0.5),
        'ffn_w_down': nrm(ks[18], (DEPTH, FFN_HIDDEN, D_MODEL), FFN_HIDDEN ** -0.5),
    }

def reference(x_prompt, x_sample, ab_norm, ab_w_in, gla_up_f, gla_bias_f, gla_up_b, gla_bias_b, gla_out_norm,
              ab_w_out, c_norm, c_w_in, c_q_norm, c_k_norm, c_w_out, ffn_norm, ffn_w_gate, ffn_w_up, ffn_w_down):
    y_prompt = trunk(x_prompt, ab_norm, ab_w_in, gla_up_f, gla_bias_f, gla_up_b, gla_bias_b, gla_out_norm, ab_w_out,
                     c_norm, c_w_in, c_q_norm, c_k_norm, c_w_out, ffn_norm, ffn_w_gate, ffn_w_up, ffn_w_down)
    y_sample = trunk(x_sample, ab_norm, ab_w_in, gla_up_f, gla_bias_f, gla_up_b, gla_bias_b, gla_out_norm, ab_w_out,
                     c_norm, c_w_in, c_q_norm, c_k_norm, c_w_out, ffn_norm, ffn_w_gate, ffn_w_up, ffn_w_down)
    return (y_prompt, y_sample)


_drawn_inputs = setup_inputs


def setup_inputs(seed=0):
    import zlib

    import numpy as np

    out = dict(_drawn_inputs(seed))
    spreads = {}
    factors = {'ab_norm': 5.455,
     'gla_bias_f': 4.393,
     'gla_bias_b': 4.549,
     'gla_out_norm': 8.0,
     'c_norm': 8.0,
     'c_q_norm': 23.482,
     'c_k_norm': 8.0,
     'ffn_norm': 5.987}
    for name, (base, spread) in spreads.items():
        noise = np.random.default_rng([zlib.crc32(name.encode()), seed]).standard_normal(out[name].shape)
        drawn = base * np.exp(spread * noise) if base else spread * noise
        out[name] = __import__('jax').numpy.asarray(drawn.astype(out[name].dtype))
    for name, factor in factors.items():
        out[name] = (out[name] * factor).astype(out[name].dtype)
    return out
```

```python
from contextlib import ExitStack

import numpy as np

import concourse.bass as bass
import concourse.mybir as mybir
from concourse.alu_op_type import AluOpType as ALU

ACT = mybir.ActivationFunctionType
F32 = mybir.dt.float32
F32R = mybir.dt.float32r
AX = mybir.AxisListType

P = 128
D = 1024
KT = D // P
SEQ, DEC = 512, 256
TOK = SEQ + DEC
TT = TOK // P
HALF = TOK // 2
HT = TT // 2
EPS = 1e-6
HEADS, DK, DV, RANK, CHUNK = 4, 64, 128, 16, 64
NCH = TOK // CHUNK
GATE_NORM = 16.0
FG, FW = 4, 128
AH, KVH, HD = 8, 2, 128
FFN = 2816
FT = FFN // P
CHUNKS = (8, 8, 6)
assert sum(CHUNKS) == FT
ROPE_THETA, GRID_W = 10000.0, 64
SLOT = KT * P

C_Q, C_K, C_V = 0, HEADS * DK, 2 * HEADS * DK
C_R = C_V + HEADS * DV
C_L = C_R + HEADS * DV
C_F = C_L + 2 * RANK
AB_UNITS = ([("l", 0, C_L)] + [("q", j, C_Q + P * j) for j in range(2)] + [("k", j, C_K + P * j) for j in range(2)]
            + [("v", j, C_V + P * j) for j in range(4)] + [("r", j, C_R + P * j) for j in range(4)]
            + [("f", j, C_F + P * j) for j in range(4)])
C_UNITS = ([("k", j, (AH + j) * HD) for j in range(KVH)] + [("v", j, (AH + KVH + j) * HD) for j in range(KVH)]
           + [("q", j, j * HD) for j in range(AH)])
QK = [(n, kind, j) for n, (kind, j, _) in enumerate(C_UNITS) if kind != "v"]

SEGMENTS = [("load", KT), ("ab", len(AB_UNITS)), ("fnet", 6), ("ab_out", KT)]
for _l in range(2):
    if _l:
        SEGMENTS += [("c", len(C_UNITS)), ("c_out", KT)]
    for _c, _t in enumerate(CHUNKS):
        SEGMENTS += [(f"gate_up{_l}{_c}", 2 * _t), (f"down{_l}{_c}", KT)]
SEGMENTS += [("store", KT)]
BASE, _n = {}, 0
for _name, _k in SEGMENTS:
    BASE[_name] = _n
    _n += _k
N_WEIGHTS = BASE["store"] - KT
FNET_END = BASE["ab_out"]

CHAIN = {"ab": 0, "o": 1, "ffn0": 1 + HEADS, "c": 2 + HEADS, "qk": 3 + HEADS, "ffn1": 3 + HEADS + len(QK)}

COL = {"ab": 0, "ffn0": KT, "c": 2 * KT, "ffn1": 3 * KT, "out": 4 * KT, "qn": 4 * KT + 1, "kn": 4 * KT + 2,
       "bias": 4 * KT + 3, "eps": 4 * KT + 7}
N_COL = 4 * KT + 8

SEQS = ((0, SEQ // CHUNK), (SEQ // CHUNK, NCH))
STATES = ([(c, c + 1, c == a) for a, b in SEQS for c in range(a, b - 1)],
          [(c, c - 1, c == b - 1) for a, b in SEQS for c in range(b - 1, a, -1)])
NS = len(STATES[0])
FIRSTS = ({a for a, _ in SEQS}, {b - 1 for _, b in SEQS})

STEPS, ITEMS = [], []
for _h in range(AH):
    for _s, _len in ((0, SEQ), (SEQ, DEC)):
        for _q in range(_len // P):
            STEPS.append((len(ITEMS), _h, _s, _len, _q, _q == _len // P - 1))
        ITEMS.append((_h, _s, _len))


def reads(n):
    return n + 1 - max(0, min(n + 1, FNET_END) - BASE["fnet"])


def trunk_kernel(nc, x_prompt, x_sample, ab_w_in, ab_w_out, c_w_in, c_w_out, w_gate, w_up, w_down,
                 columns, up_pad, tables, rope, dft, y_prompt, y_sample):
    ctx = ExitStack()
    with ctx:
        place = [-(-nc.sbuf_base // 32) * 32]

        def at(name, shape, offset, dt=F32):
            return nc.alloc_sbuf_tensor_at(name, [P, *shape], dt, offset=offset)

        def fresh(nbytes):
            place[0] += -(-nbytes // 32) * 32
            return place[0] - -(-nbytes // 32) * 32

        KB3 = TOK * 4
        x = at("x", [KT, TOK], fresh(KT * KB3))
        A = fresh(2 * KT * KB3)
        B = fresh(2 * KT * KB3)
        Dreg = fresh(32768)
        Treg = fresh(6 * KB3)
        raw = at("w_raw", [2, KT, P], fresh(2 * SLOT * 4))
        whi = at("w_hi", [2, KT, P], fresh(2 * SLOT * 4), F32R)
        wlo = at("w_lo", [2, KT, P], fresh(2 * SLOT * 4), F32R)
        rstd = at("rstd", [2, HALF], fresh(KB3))
        sumsq = at("sumsq", [TOK], fresh(KB3))
        tab = at("tab", [4, P], fresh(4 * P * 4))
        cols = at("cols", [N_COL], fresh(N_COL * 4))
        upw = at("upw", [4, P], fresh(4 * P * 4))
        ones = at("ones", [2], fresh(32))
        root = at("root", [2, TT], fresh(64))
        inv = at("inv", [2, TT], fresh(64))
        inv_tok = at("inv_tok", [TT], fresh(32))
        dec = at("dec", [4, NCH], fresh(4 * NCH * 4))
        negmax = at("negmax", [2, 2], fresh(32))
        expsum = at("expsum", [2, 2], fresh(32))
        assert place[0] <= nc.sbuf_usable_end, (place[0], nc.sbuf_usable_end)
        ident, mask, rot = tab[:, 0, :], tab[:, 1:3, :], tab[:, 3, :]

        pairA = at("pair_a", [KT, 2, TOK], A, F32R)
        pairB = at("pair_b", [KT, 2, TOK], B, F32R)
        T = [at(f"t{j}", [TOK], Treg + j * KB3) for j in range(6)]
        x_tok = at("x_tok", [TT, D], B)
        y_tok = at("y_tok", [TT, D], A)
        gcum = at("gcum", [4, TOK], B)
        q_ab = at("q_ab", [2, TOK], B + 4 * KB3)
        k_ab = at("k_ab", [2, TOK], B + 6 * KB3)
        v_ab = at("v_ab", [TT, HEADS * DV], B + 8 * KB3)
        r_ab = at("r_ab", [4, TOK], B + 12 * KB3)
        f_ab = at("f_ab", [FG, TOK], Dreg)
        o_ab = at("o_ab", [HEADS, TOK], Dreg + 4 * KB3)
        reset = at("reset", [2, TOK], Dreg + 8 * KB3)
        ranks = T[0]
        qpad = at("qpad", [HEADS, TOK], A)
        kin = at("kin", [2, TOK], A + 4 * KB3)
        kintok = at("kintok", [2, TT, 2, P], A + 6 * KB3)
        state = at("state", [NCH, 2, P], A + 10 * KB3)
        fpair = at("fpair", [2, 2, TOK], Dreg + 4 * KB3, F32R)
        wave = at("wave", [2, FG, TT, 2 * FW], A, F32R)
        kpair = at("kpair", [KVH, 2, TOK], Dreg, F32R)
        v_c = at("v_c", [TT, KVH * HD], Dreg + 4 * KB3)
        ropes = at("ropes", [2, TOK], Dreg + 6 * KB3)
        probs = [at(f"probs{j}", [SEQ], Treg + j * SEQ * 4) for j in range(3)]
        probsT = [at("probs_t0", [4, SEQ], Treg + 2 * KB3), at("probs_t1", [4, SEQ], Dreg + 6 * KB3)]

        unit_ps = ctx.enter_context(nc.psum_tensor("unit_ps", [P, 2, 2, 512], F32))
        misc_ps = ctx.enter_context(nc.psum_tensor("misc_ps", [P, 4, 512], F32))

        def ups(n):
            return unit_ps[:, n % 2, :, 0:HALF]

        def two(ap):
            return ap.rearrange("p (a b) -> p a b", a=2)

        def sem(name):
            return ctx.enter_context(nc.semaphore(name))

        x_landed = [sem(f"x_landed{j}") for j in range(2)]
        tables_landed = sem("tables_landed")
        rope_landed = sem("rope_landed")
        weights_landed = [sem(f"weights_landed{j}") for j in range(2)]
        hi_split, lo_split = sem("hi_split"), sem("lo_split")
        unit_done, unit_read = sem("unit_done"), sem("unit_read")
        h_hi, h_lo = sem("h_hi"), sem("h_lo")
        sq_ready, sq_summed, sum_zeroed = sem("sq_ready"), sem("sq_summed"), sem("sum_zeroed")
        colsum_done, root_done, inv_done = sem("colsum_done"), sem("root_done"), sem("inv_done")
        bc_done, bc_read = sem("bc_done"), sem("bc_read")
        const_ready = sem("const_ready")
        reset_ready, inv_copied = sem("reset_ready"), sem("inv_copied")
        z_done, z_read, log_ready, log_step = sem("z_done"), sem("z_read"), sem("log_ready"), sem("log_step")
        gate_ready, gate_summed = sem("gate_ready"), sem("gate_summed")
        r_silu = sem("r_silu")
        pad_zeroed = sem("pad_zeroed")
        exp_pos, exp_neg, decay_ready = sem("exp_pos"), sem("exp_neg"), sem("decay_ready")
        q_gated, k_gated = sem("q_gated"), sem("k_gated")
        kT_done, kT_read = sem("kT_done"), sem("kT_read")
        kv_done, kv_added, state_sum = sem("kv_done"), sem("kv_added"), sem("state_sum")
        att_done, att_masked = sem("att_done"), sem("att_masked")
        o_done, o_read = sem("o_done"), sem("o_read")
        osq_ready, o_gated = sem("osq_ready"), sem("o_gated")
        mixed_hi, mixed_lo = sem("mixed_hi"), sem("mixed_lo")
        f_hi, f_lo = sem("f_hi"), sem("f_lo")
        wave_done, wave_hi, wave_lo = sem("wave_done"), sem("wave_hi"), sem("wave_lo")
        y_done = sem("y_done")
        silu_done, prod_done, act_hi, act_lo = sem("silu_done"), sem("prod_done"), sem("act_hi"), sem("act_lo")
        qk_sq, qk_gain, rot_done, rot_read = sem("qk_sq"), sem("qk_gain"), sem("rot_done"), sem("rot_read")
        qk_cos, qk_sum, qk_hi, qk_lo = sem("qk_cos"), sem("qk_sum"), sem("qk_hi"), sem("qk_lo")
        s_done, s_max, s_neg, s_exp, s_inv, s_norm = (sem("s_done"), sem("s_max"), sem("s_neg"), sem("s_exp"),
                                                      sem("s_inv"), sem("s_norm"))
        pT_done, pT_read, pv_done, pv_hi, pv_lo = (sem("pT_done"), sem("pT_read"), sem("pv_done"), sem("pv_hi"),
                                                   sem("pv_lo"))
        y_stored = sem("y_stored")

        def wave_product(eng, i):
            if i < FG * HT - 1:
                eng.wait_ge(wave_done, i + 1)
            else:
                eng.wait_ge(unit_done, BASE["fnet"] + 1)

        def token_product(eng, part, g):
            if g < FG - 1:
                eng.wait_ge(y_done, (FG - 1) * part + g + 1)
            else:
                eng.wait_ge(unit_done, BASE["fnet"] + 5 + part)

        block = ctx.enter_context(nc.Block())

        @block.sync
        def _(sp):
            sp.dma_start(x_tok[:, 0:SEQ // P, :], x_prompt.rearrange("(m p) d -> p m d", p=P)).then_inc(x_landed[0], 16)
            sp.dma_start(x_tok[:, SEQ // P:, :], x_sample.rearrange("(m p) d -> p m d", p=P)).then_inc(x_landed[1], 16)

            def weights(w, src, kt, slot=None):
                s = w % 2 if slot is None else slot
                if slot is not None or w >= 2:
                    sp.wait_ge(lo_split, w - 1)
                sp.dma_start(raw[:, s, 0:kt, :], src.rearrange("(k p) n -> p k n", p=P)).then_inc(weights_landed[s], 16)

            def columns_of(w0, mat, count, kt):
                with sp.Fori(0, count // 2) as i:
                    for s in range(2):
                        weights(w0 + s + 2 * i, mat[:, bass.ds((2 * i + s) * P, P)], kt, slot=(w0 + s) % 2)

            for n, (_, _, c) in enumerate(AB_UNITS):
                weights(n, ab_w_in[:, c:c + P], KT)
            for j in range(6):
                w = BASE["fnet"] - KT + j
                sp.wait_ge(lo_split, w - 1)
                sp.dma_start(raw[:, w % 2, :, :], dft[j].rearrange("p (k n) -> p k n", k=KT)).then_inc(
                    weights_landed[w % 2], 16)
            columns_of(BASE["ab_out"] - KT, ab_w_out, KT, KT)
            for layer in range(2):
                if layer:
                    for n, (_, _, c) in enumerate(C_UNITS):
                        weights(BASE["c"] - KT + n, c_w_in[:, c:c + P], KT)
                    columns_of(BASE["c_out"] - KT, c_w_out, KT, KT)
                first = 0
                for c, tiles in enumerate(CHUNKS):
                    w0 = BASE[f"gate_up{layer}{c}"] - KT
                    with sp.Fori(0, tiles) as i:
                        for s, mat in enumerate((w_gate, w_up)):
                            weights(w0 + s + 2 * i, mat[layer][:, bass.ds((first + i) * P, P)], KT, slot=(w0 + s) % 2)
                    columns_of(BASE[f"down{layer}{c}"] - KT, w_down[layer][first * P:(first + tiles) * P, :], KT, tiles)
                    first += tiles
            for n in range(KT):
                sp.wait_ge(unit_read, reads(BASE["store"] + n))
                sl = slice(n * P, (n + 1) * P)
                sp.dma_start(y_prompt[:, sl].rearrange("(m p) d -> p m d", p=P),
                             y_tok[:, 0:SEQ // P, sl]).then_inc(y_stored, 16)
                sp.dma_start(y_sample[:, sl].rearrange("(m p) d -> p m d", p=P),
                             y_tok[:, SEQ // P:, sl]).then_inc(y_stored, 16)
            sp.wait_ge(y_stored, 32 * KT)

        @block.tensor
        def _(pe):
            def product3(out, w_hi, w_lo, m_hi, m_lo, start, stop):
                pe.matmul(out, w_hi, m_hi, start=start, stop=False)
                pe.matmul(out, w_hi, m_lo, start=False, stop=False)
                return pe.matmul(out, w_lo, m_hi, start=False, stop=stop)

            def linear(n, slot, pair, kt, waits, middle=None):
                pe.wait_ge(lo_split, n - KT + 1)
                pe.wait_ge(unit_read, waits[2])
                pe.wait_ge(waits[0], waits[1] - 1)
                for k in range(kt):
                    if k == kt - 1:
                        pe.wait_ge(waits[0], waits[1])
                    for h in range(2):
                        last = product3(unit_ps[:, slot, h, 0:HALF], whi[:, slot, k, :], wlo[:, slot, k, :],
                                        pair[:, k, 0, h * HALF:(h + 1) * HALF], pair[:, k, 1, h * HALF:(h + 1) * HALF],
                                        k == 0, k == kt - 1)
                last.then_inc(unit_done, 1)

            def linear_tokens(n, pair, waits):
                slot = n % 2
                pe.wait_ge(lo_split, n - KT + 1)
                pe.wait_ge(unit_read, waits[2])
                pe.wait_ge(waits[0], waits[1])
                for m in range(TT):
                    out = unit_ps[:, slot, m // HT, (m % HT) * P:(m % HT + 1) * P]
                    for k in range(KT):
                        last = product3(out, pair[:, k, 0, m * P:(m + 1) * P], pair[:, k, 1, m * P:(m + 1) * P],
                                        whi[:, slot, k, :], wlo[:, slot, k, :], k == 0, k == KT - 1)
                last.then_inc(unit_done, 1)

            def column_sums(g, squares):
                for m in range(TT):
                    last = pe.matmul(misc_ps[:, 0, 2 * m:2 * m + 2], squares[:, m * P:(m + 1) * P], ones[:, :],
                                     start=True, stop=True)
                last.then_inc(colsum_done, 1)

            def broadcast(g):
                pe.wait_ge(inv_done, g + 1)
                if g:
                    pe.wait_ge(bc_read, g)
                for m in range(TT):
                    last = pe.matmul(misc_ps[:, 1 + m // HT, (m % HT) * P:(m % HT + 1) * P],
                                     inv[:, g % 2, m:m + 1].to_broadcast([P, P]), ident, start=True, stop=True)
                last.then_inc(bc_done, 1)

            def trunk_norm(g, r):
                pe.wait_ge(sq_summed, KT * (r + 1))
                column_sums(g, sumsq)
                broadcast(g)

            pe.wait_ge(tables_landed, 48)
            pe.wait_ge(const_ready, 1)
            pe.wait_ge(x_landed[0], 16)
            pe.wait_ge(x_landed[1], 16)
            for n in range(KT):
                if n >= 2:
                    pe.wait_ge(unit_read, reads(n - 2))
                for m in range(TT):
                    last = pe.transpose(unit_ps[:, n % 2, m // HT, (m % HT) * P:(m % HT + 1) * P],
                                        x_tok[:, m, n * P:(n + 1) * P], ident)
                last.then_inc(unit_done, 1)

            for j, (kind, _, _) in enumerate(AB_UNITS):
                n = BASE["ab"] + j
                waits = (h_lo, KT, reads(n - 2))
                if kind == "v":
                    linear_tokens(n, pairA, waits)
                else:
                    linear(n, n % 2, pairA, KT, waits)
                if j == 0:
                    trunk_norm(CHAIN["ab"], 0)
                if j in (2, 3):
                    pe.wait_ge(unit_read, reads(BASE["ab"]))
                    pe.wait_ge(bc_read, 1)
                    for t in range(2):
                        dt = 2 * (j - 2) + t
                        if dt >= 2:
                            pe.wait_ge(z_read, dt - 1)
                        for h in range(2):
                            last = pe.matmul(misc_ps[:, 2 * t + h, 0:HALF], upw[0:2 * RANK, dt, :],
                                             ranks[0:2 * RANK, h * HALF:(h + 1) * HALF], start=True, stop=True)
                        last.then_inc(z_done, 1)

            for d in range(2):
                for t in range(2):
                    dt = 2 * d + t
                    pe.wait_ge(k_gated, dt + 1)
                    if dt == 0:
                        pe.wait_ge(z_read, 4)
                    elif t == 1:
                        pe.wait_ge(kT_read, dt)
                    else:
                        pe.wait_ge(state_sum, NS)
                    for m in range(TT):
                        last = pe.transpose(misc_ps[:, m // HT, (m % HT) * P:(m % HT + 1) * P],
                                            kin[:, t, m * P:(m + 1) * P], ident)
                    last.then_inc(kT_done, 1)
                pe.wait_ge(kT_read, 2 * d + 2)
                for i, (c, _, _) in enumerate(STATES[d]):
                    if i >= 2:
                        pe.wait_ge(state_sum, NS * d + i - 1)
                    for t in range(2):
                        for e in range(2):
                            last = pe.matmul(misc_ps[e * DK:(e + 1) * DK, i % 2, t * P:(t + 1) * P],
                                             kintok[:, t, c // 2, c % 2, e * DK:(e + 1) * DK],
                                             v_ab[:, c // 2, (2 * t + e) * DV:(2 * t + e + 1) * DV],
                                             start=True, stop=True)
                    last.then_inc(kv_done, 1)

                def scores(m):
                    if d or m:
                        pe.wait_ge(att_masked, TT * d + m)
                    for h in range(HEADS):
                        last = pe.matmul(misc_ps[:, 2, h * P:(h + 1) * P], kin[:, h // 2, m * P:(m + 1) * P],
                                         qpad[:, h, m * P:(m + 1) * P], start=True, stop=True)
                    last.then_inc(att_done, 1)

                pe.wait_ge(q_gated, 2 * d + 2)
                pe.wait_ge(state_sum, NS * (d + 1))
                scores(0)
                for m in range(TT):
                    if m + 1 < TT:
                        scores(m + 1)
                    pe.wait_ge(att_masked, TT * d + m + 1)
                    if d or m:
                        pe.wait_ge(o_read, TT * d + m)
                    for h in range(HEADS):
                        inter = [c for c in (2 * m, 2 * m + 1) if c not in FIRSTS[d]]
                        last = pe.matmul(misc_ps[:, 3, h * P:(h + 1) * P], v_ab[:, m, h * DV:(h + 1) * DV],
                                         T[m % 2][:, h * P:(h + 1) * P], start=True, stop=not inter)
                        for c in inter:
                            o = (c % 2) * CHUNK
                            last = pe.matmul(misc_ps[:, 3, h * P + o:h * P + o + CHUNK], state[:, c, h // 2, :],
                                             qpad[:, h, c * CHUNK:(c + 1) * CHUNK], start=False, stop=c == inter[-1])
                    last.then_inc(o_done, 1)

            for h in range(HEADS):
                g = CHAIN["o"] + h
                pe.wait_ge(osq_ready, h + 1)
                if h:
                    pe.wait_ge(root_done, g)
                column_sums(g, T[2 + h % 2])
                if h:
                    broadcast(g - 1)
            broadcast(CHAIN["o"] + HEADS - 1)

            n = BASE["fnet"]
            pe.wait_ge(lo_split, n - KT + 1)
            pe.wait_ge(bc_read, CHAIN["o"] + HEADS)
            for i in range(FG * HT):
                g, b = i // HT, i % 4
                pe.wait_ge(f_lo, g + 1)
                if i >= 4:
                    pe.wait_ge(wave_lo, i - 3)
                for m in (2 * (i % HT), 2 * (i % HT) + 1):
                    last = product3(misc_ps[:, b, (m % 2) * 2 * FW:(m % 2 + 1) * 2 * FW],
                                    fpair[:, g % 2, 0, m * P:(m + 1) * P], fpair[:, g % 2, 1, m * P:(m + 1) * P],
                                    whi[:, n % 2, 0:2, :], wlo[:, n % 2, 0:2, :], True, True)
                last.then_inc(unit_done if i == FG * HT - 1 else wave_done, 1)
            pe.wait_ge(wave_lo, FG * HT)
            for j in range(4):
                n = BASE["fnet"] + 1 + j
                pe.wait_ge(lo_split, n - KT + 1)
                for g in range(FG):
                    for kk in range(2):
                        k = 2 * j + kk
                        part, m = k // 4, k % 4
                        last = product3(misc_ps[:, g, :], wave[:, 0, g, m, part * FW:(part + 1) * FW],
                                        wave[:, 1, g, m, part * FW:(part + 1) * FW],
                                        whi[:, n % 2, 4 * kk:4 * kk + 4, :], wlo[:, n % 2, 4 * kk:4 * kk + 4, :],
                                        k == 0, k == 7)
                    if j == 3 and g < FG - 1:
                        last.then_inc(y_done, 1)
                last.then_inc(unit_done, 1)
            n = BASE["fnet"] + 5
            pe.wait_ge(lo_split, n - KT + 1)
            for g in range(FG):
                pe.wait_ge(mixed_lo, HEADS + g + 1)
                for k in range(4):
                    part, m = k // 2, SEQ // P + k % 2
                    last = product3(misc_ps[:, g, 0:DEC], wave[:, 0, g, m, part * FW:(part + 1) * FW],
                                    wave[:, 1, g, m, part * FW:(part + 1) * FW],
                                    whi[:, n % 2, 2 * k:2 * k + 2, :], wlo[:, n % 2, 2 * k:2 * k + 2, :],
                                    k == 0, k == 3)
                if g < FG - 1:
                    last.then_inc(y_done, 1)
            last.then_inc(unit_done, 1)

            def out_projection(seg, pair, ready, count, kt):
                n0 = BASE[seg]
                with pe.Fori(0, KT // 2) as i:
                    for s in range(2):
                        linear(n0 + s + 2 * i, (n0 + s) % 2, pair, kt, (ready, count, reads(n0 + s - 2) + 2 * i))

            def ffn(layer, g, r, pair, acts):
                done = FT * layer
                for c, tiles in enumerate(CHUNKS):
                    n0 = BASE[f"gate_up{layer}{c}"]

                    def gate_up(i, between=None):
                        for s in range(2):
                            linear(n0 + s + 2 * i, (n0 + s) % 2, pair, KT,
                                   (h_lo, KT * (r + 1), reads(n0 + s - 2) + 2 * i))
                            if s == 0 and between:
                                between()

                    gate_up(0, (lambda: trunk_norm(g, r)) if c == 0 else None)
                    with pe.Fori(1, tiles) as i:
                        gate_up(i)
                    done += tiles
                    out_projection(f"down{layer}{c}", acts, act_lo, done, tiles)

            out_projection("ab_out", pairB, mixed_lo, HEADS + 2 * FG, KT)
            ffn(0, CHAIN["ffn0"], 1, pairA, pairB)

            qk_index = {n: i for i, (n, _, _) in enumerate(QK)}

            sums_issued = [0]
            turns_issued = [0]

            def head_sums(i):
                g = CHAIN["qk"] + i
                pe.wait_ge(qk_sq, i + 1)
                pe.wait_ge(root_done, g)
                if turns_issued[0]:
                    pe.wait_ge(rot_read, turns_issued[0])
                column_sums(g, T[1])
                sums_issued[0] = i + 1

            def head_rotation(i):
                broadcast(CHAIN["qk"] + i)
                pe.wait_ge(qk_gain, i + 1)
                pe.wait_ge(root_done, CHAIN["qk"] + sums_issued[0])
                for h, b in enumerate((3, 0)):
                    last = pe.matmul(misc_ps[:, b, 0:HALF], rot, T[2 + i % 2][:, h * HALF:(h + 1) * HALF],
                                     start=True, stop=True)
                last.then_inc(rot_done, 1)
                turns_issued[0] = i + 1

            for j, (kind, _, _) in enumerate(C_UNITS):
                n = BASE["c"] + j
                waits = (h_lo, KT * 3, reads(n - 2))
                if kind == "v":
                    linear_tokens(n, pairA, waits)
                else:
                    linear(n, n % 2, pairA, KT, waits)
                if j == 0:
                    trunk_norm(CHAIN["c"], 2)
                if j - 1 in qk_index:
                    head_sums(qk_index[j - 1])
                if j - 2 in qk_index:
                    head_rotation(qk_index[j - 2])
            head_sums(len(QK) - 1)
            head_rotation(len(QK) - 2)
            head_rotation(len(QK) - 1)

            def attention_scores(j):
                a, h, s0, ln, qt, _ = STEPS[j]
                if j >= 2:
                    pe.wait_ge(s_exp, j - 1)
                q = slice(s0 + qt * P, s0 + (qt + 1) * P)
                kv = h // (AH // KVH)
                last = product3(misc_ps[:, j % 2, 0:ln], pairB[:, h, 0, q], pairB[:, h, 1, q],
                                kpair[:, kv, 0, s0:s0 + ln], kpair[:, kv, 1, s0:s0 + ln], True, True)
                last.then_inc(s_done, 1)

            def values(a):
                h, s0, ln = ITEMS[a]
                kv = h // (AH // KVH)
                steps = sum(n // P for _, _, n in ITEMS[:a + 1])
                pe.wait_ge(pT_read, steps)
                if a >= 2:
                    pe.wait_ge(pv_lo, a - 1)
                for m in range(ln // P):
                    last = pe.matmul(unit_ps[:, 0, a % 2, 0:ln], v_c[:, s0 // P + m, kv * HD:(kv + 1) * HD],
                                     probsT[a % 2][:, m, 0:ln], start=m == 0, stop=m == ln // P - 1)
                last.then_inc(pv_done, 1)

            pe.wait_ge(qk_lo, len(QK))
            pe.wait_ge(unit_read, reads(BASE["c_out"] - 1))
            attention_scores(0)
            attention_scores(1)
            for j, (a, h, s0, ln, qt, _) in enumerate(STEPS):
                pe.wait_ge(s_norm, j + 1)
                if j >= 2:
                    pe.wait_ge(pT_read, j - 1)
                for m in range(ln // P):
                    last = pe.transpose(misc_ps[:, 2 + j % 2, m * P:(m + 1) * P],
                                        probs[j % 3][:, m * P:(m + 1) * P], ident)
                last.then_inc(pT_done, 1)
                if j + 2 < len(STEPS):
                    attention_scores(j + 2)
                if qt == 0 and a:
                    values(a - 1)
            values(len(ITEMS) - 1)
            pe.wait_ge(pv_lo, len(ITEMS))
            out_projection("c_out", pairA, pv_lo, len(ITEMS), KT)
            ffn(1, CHAIN["ffn1"], 3, pairB, pairA)

            for f in range(KT):
                n = BASE["store"] + f
                pe.wait_ge(unit_read, max(reads(n - 2), reads(BASE["store"] - KT + f)))
                for m in range(TT):
                    last = pe.transpose(unit_ps[:, n % 2, m // HT, (m % HT) * P:(m % HT + 1) * P],
                                        x[:, f, m * P:(m + 1) * P], ident)
                last.then_inc(unit_done, 1)

        @block.scalar
        def _(act):
            act.dma_start(tab[:, :, :], tables.rearrange("p (a b) -> p a b", a=4)).then_inc(tables_landed, 16)
            act.dma_start(cols[:, :], columns).then_inc(tables_landed, 16)
            act.dma_start(upw[0:2 * RANK, :, :], up_pad.rearrange("p (a b) -> p a b", a=4)).then_inc(tables_landed, 16)

            def split_hi(w, slot=None, turn=None):
                s = w % 2 if slot is None else slot
                act.wait_ge(weights_landed[s], 16 * ((w // 2 if turn is None else turn) + 1))
                if slot is not None or w >= 2:
                    act.wait_ge(unit_done, w - 2 + KT + 1)
                act.activation(whi[:, s, :, :], raw[:, s, :, :], ACT.Copy).then_inc(hi_split, 1)

            def ahead(n):
                if n - KT + 2 < N_WEIGHTS:
                    split_hi(n - KT + 2)

            def ahead_loop(n0, s, i):
                w = n0 - KT + 2 + s
                split_hi(w + 2 * i, slot=w % 2, turn=w // 2 + i)

            def finish(f, n_read, r, gain, pair, tile):
                if not isinstance(f, int) or f:
                    act.wait_ge(sq_summed, f)
                act.wait_ge(unit_read, n_read)
                act.activation(pair[:, tile, 0, :], x[:, tile, :], ACT.Copy,
                               scale=cols[:, bass.ds(COL[gain] + tile, 1)] if not isinstance(tile, int)
                               else cols[:, COL[gain] + tile:COL[gain] + tile + 1]).then_inc(h_hi, 1)
                act.activation(T[2][:, :], x[:, tile, :], ACT.Square).then_inc(sq_ready, 1)

            def root_of(g, width):
                act.wait_ge(colsum_done, g + 1)
                act.activation(root[:, g % 2, :], misc_ps[:, 0, 0:2 * TT:2], ACT.Sqrt, scale=1.0 / width,
                               bias=cols[:, COL["eps"]:COL["eps"] + 1]).then_inc(root_done, 1)

            act.wait_ge(tables_landed, 48)
            split_hi(0)
            split_hi(1)
            for f in range(KT):
                finish(f, reads(f), 0, "ab", pairA, f)
            root_of(CHAIN["ab"], D)
            for j, (kind, k, _) in enumerate(AB_UNITS):
                n = BASE["ab"] + j
                ahead(n)
                if j in (2, 3):
                    for dt in (2 * (j - 2), 2 * (j - 2) + 1):
                        t = T[3 + dt % 2]
                        act.wait_ge(z_read, dt + 1)
                        if dt >= 2:
                            act.wait_ge(gate_ready, dt - 1)
                        act.activation(t[:, :], gcum[:, dt, :], ACT.Abs).then_inc(log_step, 1)
                        act.wait_ge(log_step, 2 * dt + 1)
                        act.activation(t[:, :], t[:, :], ACT.Exp, scale=-1.0).then_inc(log_step, 1)
                        act.wait_ge(log_step, 2 * dt + 2)
                        act.activation(t[:, :], t[:, :], ACT.Ln, bias=1.0).then_inc(log_ready, 1)
                if kind == "r":
                    act.wait_ge(unit_read, reads(n))
                    act.activation(r_ab[:, k, :], r_ab[:, k, :], ACT.Silu).then_inc(r_silu, 1)

            act.wait_ge(pad_zeroed, 4)
            for d in range(2):
                for t in range(2):
                    dt = 2 * d + t
                    act.wait_ge(gate_summed, dt + 1)
                    if dt:
                        act.wait_ge(q_gated, dt)
                    act.activation(T[3][:, :], gcum[:, dt, :], ACT.Exp, scale=1.0 / GATE_NORM).then_inc(exp_pos, 1)
                    if dt:
                        act.wait_ge(k_gated, dt)
                    act.activation(T[4][:, :], gcum[:, dt, :], ACT.Exp, scale=-1.0 / GATE_NORM).then_inc(exp_neg, 1)
                    end = slice(CHUNK - 1, TOK, CHUNK) if d == 0 else slice(0, TOK, CHUNK)
                    act.activation(dec[:, dt, :], gcum[:, dt, end], ACT.Exp, scale=1.0 / GATE_NORM).then_inc(decay_ready, 1)
                for t in range(2):
                    act.wait_ge(kT_done, 2 * d + t + 1)
                    for b in range(2):
                        for e in range(2):
                            rows = slice(e * CHUNK, (e + 1) * CHUNK)
                            last = act.activation(kintok[rows, t, b * HT:(b + 1) * HT, e, :],
                                                  misc_ps[rows, b, 0:HALF].rearrange("p (m k) -> p m k", m=HT), ACT.Copy)
                    last.then_inc(kT_read, 1)

            def head_squares(h):
                act.wait_ge(o_read, 2 * TT)
                if h >= 2:
                    act.wait_ge(colsum_done, CHAIN["o"] + h - 1)
                act.activation(T[2 + h % 2][:, :], o_ab[:, h, :], ACT.Square).then_inc(osq_ready, 1)
                root_of(CHAIN["o"] + h, DV)

            head_squares(0)
            for h in range(HEADS):
                if h + 1 < HEADS:
                    head_squares(h + 1)
                act.wait_ge(o_gated, h + 1)
                act.activation(pairB[:, h, 0, :], T[4][:, :], ACT.Copy).then_inc(mixed_hi, 1)

            def group_hi(g):
                if g >= 2:
                    act.wait_ge(wave_done, HT * (g - 1))
                act.activation(fpair[:, g % 2, 0, :], f_ab[:, g, :], ACT.Copy).then_inc(f_hi, 1)

            group_hi(0)
            group_hi(1)
            for i in range(FG * HT):
                g, m = i // HT, 2 * (i % HT)
                wave_product(act, i)
                act.activation(wave[:, 0, g, m:m + 2, :], misc_ps[:, i % 4, :].rearrange("p (m n) -> p m n", m=2),
                               ACT.Copy).then_inc(wave_hi, 1)
                if i % HT == HT - 1 and g + 2 < FG:
                    group_hi(g + 2)
            for j in range(5):
                ahead(BASE["fnet"] + j)
            for part, (s0, ln) in enumerate(((0, SEQ), (SEQ, DEC))):
                if part:
                    ahead(BASE["fnet"] + 5)
                for g in range(FG):
                    token_product(act, part, g)
                    act.activation(pairB[:, HEADS + g, 0, s0:s0 + ln], misc_ps[:, g, 0:ln], ACT.Copy).then_inc(mixed_hi, 1)

            def out_projection(seg, r=None, gain=None, pair=None):
                n0 = BASE[seg]
                if seg == "down12":
                    for s in range(KT - 2):
                        ahead(n0 + s)
                    return
                with act.Fori(0, KT // 2) as i:
                    for s in range(2):
                        ahead_loop(n0, s, i)
                        if r is not None:
                            finish(KT * r + s + 2 * i, reads(n0 + s) + 2 * i, r, gain, pair, s + 2 * i)

            def ffn(layer, g, acts, nxt):
                root_of(g, D)
                done = FT * layer
                for c, tiles in enumerate(CHUNKS):
                    n0 = BASE[f"gate_up{layer}{c}"]
                    with act.Fori(0, tiles) as i:
                        ahead_loop(n0, 0, i)
                        act.wait_ge(unit_read, reads(n0) + 2 * i)
                        act.activation(T[0][:, :], T[0][:, :], ACT.Silu).then_inc(silu_done, 1)
                        ahead_loop(n0, 1, i)
                        act.wait_ge(prod_done, done + 1 + i)
                        act.activation(acts[:, i, 0, :], T[1][:, :], ACT.Copy).then_inc(act_hi, 1)
                    done += tiles
                    out_projection(f"down{layer}{c}", *(nxt if c == 2 and nxt else ()))

            out_projection("ab_out", 1, "ffn0", pairA)
            ffn(0, CHAIN["ffn0"], pairB, (2, "c", pairA))

            def head_evacuate(i, n, kind):
                act.wait_ge(unit_read, reads(n))
                if i:
                    act.wait_ge(colsum_done, CHAIN["qk"] + i)
                act.activation(T[1][:, :], T[0][:, :], ACT.Square).then_inc(qk_sq, 1)
                if i >= 2:
                    act.wait_ge(rot_done, i - 1)
                    act.wait_ge(qk_cos, i - 1)
                col = COL["qn" if kind == "q" else "kn"]
                act.activation(T[2 + i % 2][:, :], T[0][:, :], ACT.Copy, scale=cols[:, col:col + 1]).then_inc(qk_gain, 1)

            def head_pair(i):
                return kpair[:, QK[i][2]] if QK[i][1] == "k" else pairB[:, QK[i][2]]

            def head_hi(i):
                act.wait_ge(bc_read, CHAIN["qk"] + i + 1)
                act.activation(head_pair(i)[:, 0, :], T[4][:, :], ACT.Copy).then_inc(qk_hi, 1)

            qk_index = {n: i for i, (n, _, _) in enumerate(QK)}
            root_of(CHAIN["c"], D)
            for j, (kind, _, _) in enumerate(C_UNITS):
                n = BASE["c"] + j
                ahead(n)
                if j - 1 in qk_index:
                    root_of(CHAIN["qk"] + qk_index[j - 1], HD)
                if j in qk_index:
                    head_evacuate(qk_index[j], n, kind)
                if j - 2 in qk_index:
                    head_hi(qk_index[j - 2])
            root_of(CHAIN["qk"] + len(QK) - 1, HD)
            head_hi(len(QK) - 2)
            head_hi(len(QK) - 1)

            def transposed(j):
                a, _, _, ln, qt, _ = STEPS[j]
                act.wait_ge(pT_done, j + 1)
                if a >= 2:
                    act.wait_ge(pv_done, a - 1)
                act.activation(probsT[a % 2][:, 0:ln // P, qt * P:(qt + 1) * P],
                               misc_ps[:, 2 + j % 2, 0:ln].rearrange("p (m q) -> p m q", q=P), ACT.Copy).then_inc(pT_read, 1)

            def result_hi(a):
                h, s0, ln = ITEMS[a]
                act.wait_ge(pv_done, a + 1)
                act.activation(pairA[:, h, 0, s0:s0 + ln], unit_ps[:, 0, a % 2, 0:ln], ACT.Copy).then_inc(pv_hi, 1)

            for j in range(len(STEPS) + 1):
                if j < len(STEPS):
                    _, _, _, ln, _, _ = STEPS[j]
                    act.wait_ge(s_neg, j + 1)
                    if j >= 3:
                        act.wait_ge(pT_done, j - 2)
                    act.activation(probs[j % 3][:, 0:ln], misc_ps[:, j % 2, 0:ln], ACT.Exp, scale=HD ** -0.5,
                                   bias=negmax[:, j % 2, 1:2], accum_out=expsum[:, j % 2, 0:1]).then_inc(s_exp, 1)
                if j:
                    transposed(j - 1)
                    if STEPS[j - 1][4] == 0 and STEPS[j - 1][0]:
                        result_hi(STEPS[j - 1][0] - 1)
            result_hi(len(ITEMS) - 1)
            out_projection("c_out", 3, "ffn1", pairB)
            ffn(1, CHAIN["ffn1"], pairA, None)

        @block.vector
        def _(dve):
            def split_lo(w, slot=None):
                s = w % 2 if slot is None else slot
                dve.wait_ge(hi_split, w + 1)
                dve.tensor_tensor(wlo[:, s, :, :], raw[:, s, :, :], whi[:, s, :, :].bitcast(F32), ALU.subtract).then_inc(
                    lo_split, 1)

            def ahead(n):
                if n - KT + 2 < N_WEIGHTS:
                    split_lo(n - KT + 2)

            def ahead_loop(n0, s, i):
                w = n0 - KT + 2 + s
                split_lo(w + 2 * i, slot=w % 2)

            def gain_lo(f, gain, pair, tile):
                dve.wait_ge(h_hi, f + 1)
                col = (cols[:, COL[gain] + tile:COL[gain] + tile + 1] if isinstance(tile, int)
                       else cols[:, bass.ds(COL[gain] + tile, 1)])
                dve.scalar_tensor_tensor(pair[:, tile, 1, :], x[:, tile, :], col, pair[:, tile, 0, :].bitcast(F32),
                                         ALU.mult, ALU.subtract).then_inc(h_lo, 1)

            def inverse(g):
                dve.wait_ge(root_done, g + 1)
                if g >= 2:
                    dve.wait_ge(bc_done, g - 1)
                dve.reciprocal(inv[:, g % 2, :], root[:, g % 2, :]).then_inc(inv_done, 1)

            def trunk_norm(g):
                inverse(g)
                dve.wait_ge(inv_done, g + 1)
                dve.tensor_copy(inv_tok[:, :], inv[:, g % 2, :]).then_inc(inv_copied, 1)
                dve.wait_ge(bc_done, g + 1)
                dve.tensor_copy(rstd[:, :, :], misc_ps[:, 1:3, 0:HALF]).then_inc(bc_read, 1)
                dve.wait_ge(bc_read, g + 1)

            def token_major(n, out):
                for h in range(2):
                    last = dve.tensor_tensor(out[:, h * HT:(h + 1) * HT, :],
                                             unit_ps[:, n % 2, h, 0:HALF].rearrange("p (m e) -> p m e", m=HT),
                                             inv_tok[:, h * HT:(h + 1) * HT].unsqueeze(2).to_broadcast([P, HT, P]), ALU.mult)
                last.then_inc(unit_read, 1)

            dve.memset(ones[:, :], 1.0).then_inc(const_ready, 1)
            dve.memset(reset[:, :, :], 1.0).then_inc(reset_ready, 1)
            dve.wait_ge(reset_ready, 1)
            dve.memset(reset[:, 0, 0:TOK:CHUNK], 0.0).then_inc(reset_ready, 1)
            dve.memset(reset[:, 1, CHUNK - 1:TOK:CHUNK], 0.0).then_inc(reset_ready, 1)
            split_lo(0)
            split_lo(1)
            dve.wait_ge(tables_landed, 48)
            for f in range(KT):
                dve.wait_ge(unit_done, f + 1)
                dve.tensor_copy(two(x[:, f, :]), ups(f)).then_inc(unit_read, 1)
                gain_lo(f, "ab", pairA, f)

            trunk_norm(CHAIN["ab"])
            dve.wait_ge(reset_ready, 3)
            for j, (kind, k, _) in enumerate(AB_UNITS):
                n = BASE["ab"] + j
                dve.wait_ge(unit_done, n + 1)
                if kind == "l":
                    dve.tensor_tensor(two(ranks[0:2 * RANK, :]), ups(n)[0:2 * RANK], rstd[0:2 * RANK], ALU.mult).then_inc(unit_read, 1)
                elif kind == "q":
                    dve.scalar_tensor_tensor(two(q_ab[:, k, :]), ups(n), DK ** -0.5, rstd[:, :, :], ALU.mult,
                                             ALU.mult).then_inc(unit_read, 1)
                elif kind == "v":
                    token_major(n, v_ab[:, :, k * DV:(k + 1) * DV])
                else:
                    out = {"k": k_ab, "r": r_ab, "f": f_ab}[kind]
                    dve.tensor_tensor(two(out[:, k, :]), ups(n), rstd[:, :, :], ALU.mult).then_inc(unit_read, 1)
                ahead(n)
                if j in (2, 3):
                    d = j - 2
                    for dt in (2 * d, 2 * d + 1):
                        dve.wait_ge(z_done, dt + 1)
                        bank = 2 * (dt % 2)
                        dve.tensor_scalar(two(gcum[:, dt, :]), misc_ps[:, bank:bank + 2, 0:HALF],
                                          cols[:, COL["bias"] + dt:COL["bias"] + dt + 1], None, ALU.add).then_inc(z_read, 1)
                    for dt in (2 * d, 2 * d + 1):
                        dve.wait_ge(log_ready, dt + 1)
                        if dt:
                            dve.wait_ge(gate_summed, dt)
                        dve.scalar_tensor_tensor(T[5][:, :], gcum[:, dt, :], 0.0, T[3 + dt % 2][:, :], ALU.min,
                                                 ALU.subtract).then_inc(gate_ready, 1)
                        dve.wait_ge(gate_ready, dt + 1)
                        step = 1 if d == 0 else -1
                        dve.tensor_tensor_scan(gcum[:, dt, ::step], reset[:, d, ::step], T[5][:, ::step], 0.0, ALU.mult,
                                               ALU.add).then_inc(gate_summed, 1)

            added = 0
            dve.wait_ge(pad_zeroed, 4)
            for d in range(2):
                for t in range(2):
                    dt = 2 * d + t
                    dve.wait_ge(exp_pos, dt + 1)
                    if d:
                        dve.wait_ge(o_done, TT)
                    for e in range(2):
                        rows = slice(e * DK, (e + 1) * DK)
                        last = dve.tensor_tensor(qpad[rows, 2 * t + e, :], q_ab[rows, t, :], T[3][rows, :], ALU.mult)
                    last.then_inc(q_gated, 1)
                dve.wait_ge(decay_ready, 2 * d + 2)
                for i, (c, nxt, first) in enumerate(STATES[d]):
                    dve.wait_ge(kv_done, NS * d + i + 1)
                    kv = misc_ps[:, i % 2, 0:2 * P].rearrange("p (t e) -> p t e", t=2)
                    decay = dec[:, 2 * d:2 * d + 2, c].unsqueeze(2).to_broadcast([P, 2, P])
                    if not first:
                        dve.wait_ge(state_sum, NS * d + i)
                        dve.tensor_tensor(T[5][:, 0:2 * P].rearrange("p (t e) -> p t e", t=2), kv, state[:, c, :, :],
                                          ALU.add).then_inc(kv_added, 1)
                        added += 1
                        dve.wait_ge(kv_added, added)
                        kv = T[5][:, 0:2 * P].rearrange("p (t e) -> p t e", t=2)
                    dve.tensor_tensor(state[:, nxt, :, :], kv, decay, ALU.mult).then_inc(state_sum, 1)

                def masked(m):
                    dve.wait_ge(att_done, TT * d + m + 1)
                    if d or m >= 2:
                        dve.wait_ge(o_done, TT * d + m - 1 if m else TT * d)
                    dve.tensor_tensor(T[m % 2][:, 0:HEADS * P].rearrange("p (h i) -> p h i", h=HEADS),
                                      misc_ps[:, 2, :].rearrange("p (h i) -> p h i", h=HEADS),
                                      mask[:, d, :].unsqueeze(1).to_broadcast([P, HEADS, P]), ALU.mult).then_inc(att_masked, 1)

                masked(0)
                for m in range(TT):
                    if m + 1 < TT:
                        masked(m + 1)
                    dve.wait_ge(o_done, TT * d + m + 1)
                    o = o_ab[:, :, m * P:(m + 1) * P]
                    out = misc_ps[:, 3, :].rearrange("p (h i) -> p h i", h=HEADS)
                    if d == 0:
                        dve.tensor_copy(o, out).then_inc(o_read, 1)
                    else:
                        dve.wait_ge(o_read, TT)
                        dve.tensor_tensor(o, out, o, ALU.add).then_inc(o_read, 1)

            inverse(CHAIN["o"])
            dve.wait_ge(r_silu, 4)
            dve.wait_ge(o_read, 2 * TT)
            for h in range(HEADS):
                g = CHAIN["o"] + h
                if h + 1 < HEADS:
                    inverse(g + 1)
                dve.wait_ge(bc_done, g + 1)
                if h:
                    dve.wait_ge(o_gated, h)
                dve.tensor_tensor(two(T[5][:, :]), two(o_ab[:, h, :]), misc_ps[:, 1:3, 0:HALF], ALU.mult).then_inc(bc_read, 1)
                dve.wait_ge(bc_read, g + 1)
                if h:
                    dve.wait_ge(mixed_lo, h)
                dve.scalar_tensor_tensor(T[4][:, :], T[5][:, :], cols[:, COL["out"]:COL["out"] + 1], r_ab[:, h, :],
                                         ALU.mult, ALU.mult).then_inc(o_gated, 1)
                dve.wait_ge(mixed_hi, h + 1)
                dve.tensor_tensor(pairB[:, h, 1, :], T[4][:, :], pairB[:, h, 0, :].bitcast(F32), ALU.subtract).then_inc(mixed_lo, 1)

            def group_lo(g):
                dve.wait_ge(f_hi, g + 1)
                dve.tensor_tensor(fpair[:, g % 2, 1, :], f_ab[:, g, :], fpair[:, g % 2, 0, :].bitcast(F32),
                                  ALU.subtract).then_inc(f_lo, 1)

            group_lo(0)
            group_lo(1)
            for i in range(FG * HT):
                g, m = i // HT, 2 * (i % HT)
                dve.wait_ge(wave_hi, i + 1)
                dve.tensor_tensor(wave[:, 1, g, m:m + 2, :], misc_ps[:, i % 4, :].rearrange("p (m n) -> p m n", m=2),
                                  wave[:, 0, g, m:m + 2, :].bitcast(F32), ALU.subtract).then_inc(wave_lo, 1)
                if i % HT == HT - 1 and g + 2 < FG:
                    group_lo(g + 2)
            for j in range(5):
                ahead(BASE["fnet"] + j)
            for part, (s0, ln) in enumerate(((0, SEQ), (SEQ, DEC))):
                if part:
                    ahead(BASE["fnet"] + 5)
                for g in range(FG):
                    dve.wait_ge(mixed_hi, HEADS + FG * part + g + 1)
                    dve.tensor_tensor(pairB[:, HEADS + g, 1, s0:s0 + ln], misc_ps[:, g, 0:ln],
                                      pairB[:, HEADS + g, 0, s0:s0 + ln].bitcast(F32), ALU.subtract).then_inc(mixed_lo, 1)

            def out_projection(seg, r=None, gain=None, pair=None):
                n0 = BASE[seg]
                dve.wait_ge(unit_read, reads(n0 - 1))

                def add(n, slot, tile):
                    dve.wait_ge(unit_done, n + 1)
                    dve.tensor_tensor(two(x[:, tile, :]), unit_ps[:, slot, :, 0:HALF], two(x[:, tile, :]),
                                      ALU.add).then_inc(unit_read, 1)

                if seg == "down12":
                    for s in range(KT):
                        add(n0 + s, (n0 + s) % 2, s)
                        ahead(n0 + s)
                    return
                with dve.Fori(0, KT // 2) as i:
                    for s in range(2):
                        add(n0 + s + 2 * i, (n0 + s) % 2, s + 2 * i)
                        ahead_loop(n0, s, i)
                        if r is not None:
                            gain_lo(KT * r + s + 2 * i, gain, pair, s + 2 * i)

            def ffn(layer, g, nxt):
                trunk_norm(g)
                done = FT * layer
                for c, tiles in enumerate(CHUNKS):
                    n0 = BASE[f"gate_up{layer}{c}"]
                    with dve.Fori(0, tiles) as i:
                        dve.wait_ge(unit_done, n0 + 1 + 2 * i)
                        dve.wait_ge(prod_done, done + i)
                        dve.tensor_tensor(two(T[0][:, :]), ups(n0), rstd[:, :, :], ALU.mult).then_inc(unit_read, 1)
                        ahead_loop(n0, 0, i)
                        dve.wait_ge(unit_done, n0 + 2 + 2 * i)
                        dve.wait_ge(act_lo, done + i)
                        dve.tensor_tensor(two(T[1][:, :]), ups(n0 + 1), rstd[:, :, :], ALU.mult).then_inc(unit_read, 1)
                        ahead_loop(n0, 1, i)
                    done += tiles
                    out_projection(f"down{layer}{c}", *(nxt if c == 2 and nxt else ()))

            out_projection("ab_out", 1, "ffn0", pairA)
            ffn(0, CHAIN["ffn0"], (2, "c", pairA))

            qk_index = {n: i for i, (n, _, _) in enumerate(QK)}

            def head_scale(i):
                sin = ropes[:, 1, :]
                dve.wait_ge(rot_done, i + 1)
                if i:
                    dve.wait_ge(qk_sum, i)
                for h, b in enumerate((3, 0)):
                    last = dve.tensor_tensor(T[5][:, h * HALF:(h + 1) * HALF], misc_ps[:, b, 0:HALF],
                                             sin[:, h * HALF:(h + 1) * HALF], ALU.mult)
                last.then_inc(rot_read, 1)
                dve.wait_ge(qk_sum, i + 1)
                dve.wait_ge(bc_done, CHAIN["qk"] + i + 1)
                dve.tensor_tensor(two(T[4][:, :]), two(T[4][:, :]), misc_ps[:, 1:3, 0:HALF], ALU.mult).then_inc(bc_read, 1)

            trunk_norm(CHAIN["c"])
            dve.wait_ge(rope_landed, 16)
            for j, (kind, k, _) in enumerate(C_UNITS):
                n = BASE["c"] + j
                dve.wait_ge(unit_done, n + 1)
                if kind == "v":
                    token_major(n, v_c[:, :, k * HD:(k + 1) * HD])
                else:
                    if qk_index[j]:
                        dve.wait_ge(qk_gain, qk_index[j])
                    dve.tensor_tensor(two(T[0][:, :]), ups(n), rstd[:, :, :], ALU.mult).then_inc(unit_read, 1)
                ahead(n)
                if j - 1 in qk_index:
                    inverse(CHAIN["qk"] + qk_index[j - 1])
                if j - 2 in qk_index:
                    head_scale(qk_index[j - 2])
            inverse(CHAIN["qk"] + len(QK) - 1)
            head_scale(len(QK) - 2)
            head_scale(len(QK) - 1)

            def normalized(j):
                ln = STEPS[j][3]
                dve.wait_ge(s_exp, j + 1)
                dve.reciprocal(expsum[:, j % 2, 1:2], expsum[:, j % 2, 0:1]).then_inc(s_inv, 1)
                dve.wait_ge(s_inv, j + 1)
                dve.tensor_scalar(probs[j % 3][:, 0:ln], probs[j % 3][:, 0:ln], expsum[:, j % 2, 1:2], None,
                                  ALU.mult).then_inc(s_norm, 1)

            def result_lo(a):
                h, s0, ln = ITEMS[a]
                dve.wait_ge(pv_hi, a + 1)
                dve.tensor_tensor(pairA[:, h, 1, s0:s0 + ln], unit_ps[:, 0, a % 2, 0:ln],
                                  pairA[:, h, 0, s0:s0 + ln].bitcast(F32), ALU.subtract).then_inc(pv_lo, 1)

            for j in range(len(STEPS) + 1):
                if j < len(STEPS):
                    ln = STEPS[j][3]
                    dve.wait_ge(s_done, j + 1)
                    dve.reduce_max(negmax[:, j % 2, 0:1], misc_ps[:, j % 2, 0:ln], AX.X).then_inc(s_max, 1)
                    dve.wait_ge(s_max, j + 1)
                    dve.tensor_scalar(negmax[:, j % 2, 1:2], negmax[:, j % 2, 0:1], -HD ** -0.5, None,
                                      ALU.mult).then_inc(s_neg, 1)
                if j:
                    normalized(j - 1)
                    if STEPS[j - 1][4] == 0 and STEPS[j - 1][0]:
                        result_lo(STEPS[j - 1][0] - 1)
            result_lo(len(ITEMS) - 1)
            out_projection("c_out", 3, "ffn1", pairB)
            ffn(1, CHAIN["ffn1"], None)
            for f in range(KT):
                n = BASE["store"] + f
                dve.wait_ge(unit_done, n + 1)
                for h in range(2):
                    last = dve.tensor_copy(y_tok[:, h * HT:(h + 1) * HT, f * P:(f + 1) * P],
                                           unit_ps[:, n % 2, h, 0:HALF].rearrange("p (m e) -> p m e", m=HT))
                last.then_inc(unit_read, 1)

        @block.gpsimd
        def _(pool):
            def sum_squares(f):
                pool.wait_ge(sq_ready, f + 1)
                pool.tensor_tensor(sumsq[:, :], sumsq[:, :], T[2][:, :], ALU.add).then_inc(sq_summed, 1)

            def squares(r, g_last):
                if g_last is not None:
                    pool.wait_ge(colsum_done, g_last + 1)
                pool.memset(sumsq[:, :], 0.0).then_inc(sum_zeroed, 1)
                pool.wait_ge(sum_zeroed, r + 1)
                if r == 0:
                    for f in range(KT):
                        if f:
                            pool.wait_ge(sq_summed, f)
                        sum_squares(f)
                    return
                with pool.Fori(0, KT) as i:
                    pool.wait_ge(sq_summed, KT * r + i)
                    sum_squares(KT * r + i)

            squares(0, None)
            pool.wait_ge(unit_done, BASE["fnet"])
            for e in range(2):
                rows = slice(e * DK, (e + 1) * DK)
                pool.memset(qpad[rows, 1 - e:HEADS:2, :], 0.0).then_inc(pad_zeroed, 1)
                pool.memset(kintok[rows, :, :, 1 - e, :], 0.0).then_inc(pad_zeroed, 1)
            for dt in range(4):
                pool.wait_ge(exp_neg, dt + 1)
                if dt >= 2:
                    pool.wait_ge(att_done, TT)
                pool.tensor_tensor(kin[:, dt % 2, :], k_ab[:, dt % 2, :], T[4][:, :], ALU.mult).then_inc(k_gated, 1)

            def ffn(layer):
                done = FT * layer
                for c, tiles in enumerate(CHUNKS):
                    n0 = BASE[f"gate_up{layer}{c}"]
                    acts = pairA if layer else pairB
                    with pool.Fori(0, tiles) as i:
                        pool.wait_ge(silu_done, done + 1 + i)
                        pool.wait_ge(unit_read, reads(n0 + 1) + 2 * i)
                        pool.tensor_tensor(T[1][:, :], T[0][:, :], T[1][:, :], ALU.mult).then_inc(prod_done, 1)
                        pool.wait_ge(act_hi, done + 1 + i)
                        pool.tensor_tensor(acts[:, i, 1, :], T[1][:, :], acts[:, i, 0, :].bitcast(F32),
                                           ALU.subtract).then_inc(act_lo, 1)
                    done += tiles

            squares(1, CHAIN["ab"])
            ffn(0)
            squares(2, CHAIN["ffn0"])
            pool.wait_ge(h_lo, KT * 3)
            pool.dma_start(ropes[:, :, :], rope.rearrange("p (a t) -> p a t", a=2)).then_inc(rope_landed, 16)
            pool.wait_ge(rope_landed, 16)
            for i, (_, kind, k) in enumerate(QK):
                pair = kpair[:, k] if kind == "k" else pairB[:, k]
                pool.wait_ge(qk_gain, i + 1)
                if i:
                    pool.wait_ge(qk_lo, i)
                pool.tensor_tensor(T[4][:, :], T[2 + i % 2][:, :], ropes[:, 0, :], ALU.mult).then_inc(qk_cos, 1)
                pool.wait_ge(qk_cos, i + 1)
                pool.wait_ge(rot_read, i + 1)
                pool.tensor_tensor(T[4][:, :], T[4][:, :], T[5][:, :], ALU.add).then_inc(qk_sum, 1)
                pool.wait_ge(qk_hi, i + 1)
                pool.tensor_tensor(pair[:, 1, :], T[4][:, :], pair[:, 0, :].bitcast(F32), ALU.subtract).then_inc(qk_lo, 1)
            squares(3, CHAIN["c"])
            ffn(1)


def _tables():
    ident = np.eye(P)
    i = np.arange(P)
    same = (i[:, None] // CHUNK) == (i[None, :] // CHUNK)
    forward = same & (i[:, None] <= i[None, :])
    backward = same & (i[:, None] >= i[None, :])
    rot = np.zeros((P, P))
    q = HD // 4
    for half in (0, HD // 2):
        for k in range(q):
            rot[half + q + k, half + k] = -1.0
            rot[half + k, half + q + k] = 1.0
    return np.concatenate([ident, forward, backward, rot], axis=1).astype(np.float32)


def _rope():
    half = HD // 2
    inv = (np.float32(ROPE_THETA) ** (-np.arange(0, half, 2, dtype=np.float32) / np.float32(half))).astype(np.float32)
    t = np.concatenate([np.arange(SEQ), np.arange(DEC)])
    out = []
    for fn in (np.cos, np.sin):
        rows = []
        for d in range(HD):
            pos = (t // GRID_W if d < half else t % GRID_W).astype(np.float32)
            rows.append(fn(pos * inv[d % (half // 2)]))
        out.append(np.stack(rows))
    return np.concatenate(out, axis=1).astype(np.float32)


def _dft():
    def cs(n):
        k = np.outer(np.arange(n), np.arange(n)) % n
        return np.cos(2 * np.pi * k / n), np.sin(2 * np.pi * k / n)

    out = np.zeros((6, P, SLOT))
    out[0, :, 0:2 * FW] = np.concatenate(cs(FW), axis=1)
    c, s = cs(SEQ)
    both = (np.concatenate([c, -s]) / np.sqrt(SEQ * FW)).reshape(8, P, SEQ)
    for j in range(4):
        out[1 + j] = np.concatenate([both[2 * j], both[2 * j + 1]], axis=1)
    c, s = cs(DEC)
    both = (np.concatenate([c, -s]) / np.sqrt(DEC * FW)).reshape(4, P, DEC)
    out[5] = np.concatenate(list(both), axis=1)
    return out.astype(np.float32)


def kernel(x_prompt, x_sample, ab_norm, ab_w_in, gla_up_f, gla_bias_f, gla_up_b, gla_bias_b, gla_out_norm, ab_w_out,
           c_norm, c_w_in, c_q_norm, c_k_norm, c_w_out, ffn_norm, ffn_w_gate, ffn_w_up, ffn_w_down):
    import concourse.bacc as bacc
    from concourse.bass_utils import run_bass_kernel_spmd

    def tiles(v):
        return np.asarray(v).reshape(-1, P).T

    eps = np.full((P, 1), EPS, np.float32)
    columns = np.concatenate([tiles(ab_norm[0]), tiles(ffn_norm[0]), tiles(c_norm[0]), tiles(ffn_norm[1]),
                              tiles(gla_out_norm[0]), tiles(c_q_norm[0]), tiles(c_k_norm[0]), tiles(gla_bias_f[0]),
                              tiles(gla_bias_b[0]), eps], axis=1)
    up_pad = np.zeros((2 * RANK, 4 * P), np.float32)
    up_pad[0:RANK, 0:2 * P] = gla_up_f[0]
    up_pad[RANK:, 2 * P:] = gla_up_b[0]
    arrays = {
        "in_x_prompt": np.asarray(x_prompt)[0], "in_x_sample": np.asarray(x_sample)[0],
        "in_ab_w_in": np.asarray(ab_w_in)[0], "in_ab_w_out": np.asarray(ab_w_out)[0],
        "in_c_w_in": np.asarray(c_w_in)[0], "in_c_w_out": np.asarray(c_w_out)[0],
        "in_w_gate": ffn_w_gate, "in_w_up": ffn_w_up, "in_w_down": ffn_w_down,
        "in_columns": columns, "in_up_pad": up_pad,
        "const_tables": _tables(), "const_rope": _rope(), "const_dft": _dft(),
    }
    arrays = {k: np.ascontiguousarray(v) for k, v in arrays.items()}
    nc = bacc.Bacc("TRN2", target_bir_lowering=False, num_devices=1)
    args = [nc.dram_tensor(k, v.shape, mybir.dt.from_np(v.dtype), kind="ExternalInput").ap() for k, v in arrays.items()]
    for name, n in (("out_prompt", SEQ), ("out_sample", DEC)):
        args.append(nc.dram_tensor(name, (n, D), F32, kind="ExternalOutput").ap())
    trunk_kernel(nc, *args)
    r = run_bass_kernel_spmd(nc, [arrays], core_ids=[0]).results[0]
    return r["out_prompt"][None], r["out_sample"][None]
```

```python
from contextlib import ExitStack

import numpy as np

import concourse.bass as bass
import concourse.mybir as mybir
from concourse.alu_op_type import AluOpType as ALU

ACT = mybir.ActivationFunctionType
F32 = mybir.dt.float32
F32R = mybir.dt.float32r
AX = mybir.AxisListType

P = 128
D = 1024
KT = D // P
SEQ, DEC = 512, 256
TOK = SEQ + DEC
TT = TOK // P
HALF = TOK // 2
HT = TT // 2
EPS = 1e-6
HEADS, DK, DV, RANK, CHUNK = 4, 64, 128, 16, 64
NCH = TOK // CHUNK
GATE_NORM = 16.0
FG, FW = 4, 128
AH, KVH, HD = 8, 2, 128
FFN = 2816
FT = FFN // P
CHUNKS = (8, 8, 6)
assert sum(CHUNKS) == FT
ROPE_THETA, GRID_W = 10000.0, 64
SLOT = KT * P

C_Q, C_K, C_V = 0, HEADS * DK, 2 * HEADS * DK
C_R = C_V + HEADS * DV
C_L = C_R + HEADS * DV
C_F = C_L + 2 * RANK
AB_UNITS = ([("l", 0, C_L)] + [("q", j, C_Q + P * j) for j in range(2)] + [("k", j, C_K + P * j) for j in range(2)]
            + [("v", j, C_V + P * j) for j in range(4)] + [("r", j, C_R + P * j) for j in range(4)]
            + [("f", j, C_F + P * j) for j in range(4)])
EARLY_UNITS, EARLY_KT = 3, AH - 3
C_UNITS = ([("k", j, (AH + j) * HD) for j in range(KVH)] + [("v", j, (AH + KVH + j) * HD) for j in range(KVH)]
           + [("q", j, j * HD) for j in range(AH)] + [("o", j, j * P) for j in range(EARLY_UNITS)])
QK = [(n, kind, j) for n, (kind, j, _) in enumerate(C_UNITS) if kind in "qk"]

SEGMENTS = [("load", KT), ("ab", len(AB_UNITS)), ("fnet", 6), ("ab_out", KT)]
for _l in range(2):
    if _l:
        SEGMENTS += [("c", len(C_UNITS)), ("c_out", KT)]
    for _c, _t in enumerate(CHUNKS):
        SEGMENTS += [(f"gate_up{_l}{_c}", 2 * _t), (f"down{_l}{_c}", KT)]
SEGMENTS += [("store", KT)]
BASE, _n = {}, 0
for _name, _k in SEGMENTS:
    BASE[_name] = _n
    _n += _k
N_WEIGHTS = BASE["store"] - KT
FNET_END = BASE["ab_out"]

CHAIN = {"ab": 0, "o": 1, "ffn0": 1 + HEADS, "c": 2 + HEADS, "qk": 3 + HEADS, "ffn1": 3 + HEADS + len(QK)}

COL = {"ab": 0, "ffn0": KT, "c": 2 * KT, "ffn1": 3 * KT, "out": 4 * KT, "qn": 4 * KT + 1, "kn": 4 * KT + 2,
       "bias": 4 * KT + 3, "eps": 4 * KT + 7}
N_COL = 4 * KT + 8

SEQS = ((0, SEQ // CHUNK), (SEQ // CHUNK, NCH))
STATES = ([(c, c + 1, c == a) for a, b in SEQS for c in range(a, b - 1)],
          [(c, c - 1, c == b - 1) for a, b in SEQS for c in range(b - 1, a, -1)])
NS = len(STATES[0])
FIRSTS = ({a for a, _ in SEQS}, {b - 1 for _, b in SEQS})

STEPS, ITEMS, LAST_STEP = [], [], []
for _h in range(AH):
    for _s, _len in ((0, SEQ), (SEQ, DEC)):
        for _q in range(_len // P):
            STEPS.append((len(ITEMS), _h, _s, _len, _q))
        ITEMS.append((_h, _s, _len))
        LAST_STEP.append(len(STEPS) - 1)
HEAD_STEPS = len(STEPS) // AH

PLAN = {}


def _put(slot, *event):
    PLAN.setdefault(slot, []).append(event)


UNIT_OF = [n for n, _, _ in QK]
LAG = 3
for _n, (_kind, _j, _) in enumerate(C_UNITS):
    if _kind == "v":
        _put(8 * (_n + 1) + 2, "values_turn", _j)
for _i, (_n, _kind, _j) in enumerate(QK):
    _at = 8 * (_n + 1)
    if _kind == "q":
        for _r in range(HEAD_STEPS):
            _t = _j * HEAD_STEPS + _r
            _put(_at + 11 + _r + LAG, "flip", _t)
            if _t in LAST_STEP:
                _put(_at + 13 + _r + LAG, "values", LAST_STEP.index(_t))
                _put(_at + 14 + _r + LAG, "result", LAST_STEP.index(_t))
for _i, (_n, _kind, _j) in enumerate(QK):
    _at = 8 * (_n + 1)
    if _kind == "q":
        for _r in range(HEAD_STEPS):
            _put(_at + 11 + _r, "scores", _j * HEAD_STEPS + _r)
            _put(_at + 12 + _r, "softmax", _j * HEAD_STEPS + _r)
    _put(_at + 2, "sums", _i)
    _put(_at + (4 if _kind == "q" else 5), "turn", _i, 0)
    _put(_at + (6 if _kind == "q" else 5), "turn", _i, 1)
    _put(_at + 8, "split", _i)
SLOTS = max(max(PLAN), 8 * len(C_UNITS)) + 1


def broadcasts(g):
    return g + 1 if g < CHAIN["qk"] + KVH else CHAIN["qk"] + KVH + (g == CHAIN["ffn1"])


def reads(n):
    return n + 1 - max(0, min(n + 1, FNET_END) - BASE["fnet"])


def trunk_kernel(nc, x_prompt, x_sample, ab_w_in, ab_w_out, c_w_in, c_w_out, w_gate, w_up, w_down,
                 columns, up_pad, tables, rope, dft, y_prompt, y_sample):
    ctx = ExitStack()
    with ctx:
        place = [-(-nc.sbuf_base // 32) * 32]

        def at(name, shape, offset, dt=F32):
            return nc.alloc_sbuf_tensor_at(name, [P, *shape], dt, offset=offset)

        def fresh(nbytes):
            place[0] += -(-nbytes // 32) * 32
            return place[0] - -(-nbytes // 32) * 32

        KB3 = TOK * 4
        x = at("x", [KT, TOK], fresh(KT * KB3))
        A = fresh(2 * KT * KB3)
        B = fresh(2 * KT * KB3)
        Dreg = fresh(32768)
        Treg = fresh(6 * KB3)
        raw = at("w_raw", [2, KT, P], fresh(2 * SLOT * 4))
        whi = at("w_hi", [2, KT, P], fresh(2 * SLOT * 4), F32R)
        wlo = at("w_lo", [2, KT, P], fresh(2 * SLOT * 4), F32R)
        rstd = at("rstd", [2, HALF], fresh(KB3))
        sumsq = at("sumsq", [TOK], fresh(KB3))
        tab = at("tab", [4, P], fresh(4 * P * 4))
        cols = at("cols", [N_COL], fresh(N_COL * 4))
        upw = at("upw", [4, P], fresh(4 * P * 4))
        ones = at("ones", [2], fresh(32))
        root = at("root", [2, TT], fresh(64))
        inv = at("inv", [2, TT], fresh(64))
        q_scale = at("q_scale", [AH, TT], fresh(AH * TT * 4))
        dec = at("dec", [4, NCH], fresh(4 * NCH * 4))
        negmax = at("negmax", [2, 2], fresh(32))
        expsum = at("expsum", [2, 2], fresh(32))
        assert place[0] <= nc.sbuf_usable_end, (place[0], nc.sbuf_usable_end)
        ident, mask, rot = tab[:, 0, :], tab[:, 1:3, :], tab[:, 3, :]

        pairA = at("pair_a", [KT, 2, TOK], A, F32R)
        pairB = at("pair_b", [KT, 2, TOK], B, F32R)
        T = [at(f"t{j}", [TOK], Treg + j * KB3) for j in range(6)]
        x_tok = at("x_tok", [TT, D], B)
        y_tok = at("y_tok", [TT, D], A)
        gcum = at("gcum", [4, TOK], B)
        q_ab = at("q_ab", [2, TOK], B + 4 * KB3)
        k_ab = at("k_ab", [2, TOK], B + 6 * KB3)
        v_ab = at("v_ab", [TT, HEADS * DV], B + 8 * KB3)
        r_ab = at("r_ab", [4, TOK], B + 12 * KB3)
        f_ab = at("f_ab", [FG, TOK], Dreg)
        o_ab = at("o_ab", [HEADS, TOK], Dreg + 4 * KB3)
        reset = at("reset", [2, TOK], Dreg + 8 * KB3)
        ranks = T[0]
        qpad = at("qpad", [HEADS, TOK], A)
        kin = at("kin", [2, TOK], A + 4 * KB3)
        kintok = at("kintok", [2, TT, 2, P], A + 6 * KB3)
        state = at("state", [NCH, 2, P], A + 10 * KB3)
        fpair = at("fpair", [2, 2, TOK], Dreg + 4 * KB3, F32R)
        wave = at("wave", [2, FG, TT, 2 * FW], A, F32R)
        kpair = at("kpair", [KVH, 2, TOK], Dreg, F32R)
        v_c = at("v_c", [TT, KVH * HD], Dreg + 4 * KB3)
        v_flat = [T[5], sumsq]
        ropes = at("ropes", [2, TOK], Dreg + 6 * KB3)
        probs = [T[5], sumsq, upw]
        probs = [probs[0][:, 0:SEQ], probs[1][:, 0:SEQ], probs[2][:, :, :].rearrange("p a b -> p (a b)")]
        probsT = [at("probs_t", [4, SEQ], Dreg + 8 * KB3),
                  at("sample_t", [11, TOK], Treg + 5 * KB3)[:, 0:11:10, SEQ:TOK]]

        unit_ps = ctx.enter_context(nc.psum_tensor("unit_ps", [P, 2, 2, 512], F32))
        misc_ps = ctx.enter_context(nc.psum_tensor("misc_ps", [P, 4, 512], F32))

        def ups(n):
            return unit_ps[:, n % 2, :, 0:HALF]

        def two(ap):
            return ap.rearrange("p (a b) -> p a b", a=2)

        def sem(name):
            return ctx.enter_context(nc.semaphore(name))

        x_landed = [sem(f"x_landed{j}") for j in range(2)]
        tables_landed = sem("tables_landed")
        rope_landed = sem("rope_landed")
        weights_landed = [sem(f"weights_landed{j}") for j in range(2)]
        hi_split, lo_split = sem("hi_split"), sem("lo_split")
        unit_done, unit_read = sem("unit_done"), sem("unit_read")
        h_hi, h_lo = sem("h_hi"), sem("h_lo")
        sq_ready, sq_summed, sum_zeroed = sem("sq_ready"), sem("sq_summed"), sem("sum_zeroed")
        colsum_done, root_done, inv_done = sem("colsum_done"), sem("root_done"), sem("inv_done")
        bc_done, bc_read = sem("bc_done"), sem("bc_read")
        const_ready = sem("const_ready")
        half_done, half_read, q_scaled = sem("half_done"), sem("half_read"), sem("q_scaled")
        reset_ready = sem("reset_ready")
        vT_done, vT_read = sem("vT_done"), sem("vT_read")
        z_done, z_read, log_ready, log_step = sem("z_done"), sem("z_read"), sem("log_ready"), sem("log_step")
        gate_ready, gate_summed = sem("gate_ready"), sem("gate_summed")
        r_silu = sem("r_silu")
        pad_zeroed = sem("pad_zeroed")
        exp_pos, exp_neg, decay_ready = sem("exp_pos"), sem("exp_neg"), sem("decay_ready")
        q_gated, k_gated = sem("q_gated"), sem("k_gated")
        kT_done, kT_read = sem("kT_done"), sem("kT_read")
        kv_done, kv_added, state_sum = sem("kv_done"), sem("kv_added"), sem("state_sum")
        att_done, att_masked = sem("att_done"), sem("att_masked")
        o_done, o_read = sem("o_done"), sem("o_read")
        osq_ready, o_gated = sem("osq_ready"), sem("o_gated")
        mixed_hi, mixed_lo = sem("mixed_hi"), sem("mixed_lo")
        f_hi, f_lo = sem("f_hi"), sem("f_lo")
        wave_done, wave_hi, wave_lo = sem("wave_done"), sem("wave_hi"), sem("wave_lo")
        y_done = sem("y_done")
        silu_done, prod_done, act_hi, act_lo = sem("silu_done"), sem("prod_done"), sem("act_hi"), sem("act_lo")
        qk_sq, qk_gain, rot_done, rot_read = sem("qk_sq"), sem("qk_gain"), sem("rot_done"), sem("rot_read")
        qk_cos, qk_sum, qk_hi, qk_lo = sem("qk_cos"), sem("qk_sum"), sem("qk_hi"), sem("qk_lo")
        s_done, s_max, s_neg, s_exp, s_inv, s_norm = (sem("s_done"), sem("s_max"), sem("s_neg"), sem("s_exp"),
                                                      sem("s_inv"), sem("s_norm"))
        pT_done, pT_read, pv_done, pv_hi, pv_lo = (sem("pT_done"), sem("pT_read"), sem("pv_done"), sem("pv_hi"),
                                                   sem("pv_lo"))
        y_stored = sem("y_stored")

        def flip_bank(j):
            return misc_ps[:, 2, :] if j % 2 == 0 else unit_ps[:, 1, 0, :]

        values_bank = unit_ps[:, 1, 1, :]

        def wave_product(eng, i):
            if i < FG * HT - 1:
                eng.wait_ge(wave_done, i + 1)
            else:
                eng.wait_ge(unit_done, BASE["fnet"] + 1)

        def token_product(eng, part, g):
            if g < FG - 1:
                eng.wait_ge(y_done, (FG - 1) * part + g + 1)
            else:
                eng.wait_ge(unit_done, BASE["fnet"] + 5 + part)

        block = ctx.enter_context(nc.Block())

        @block.sync
        def _(sp):
            sp.dma_start(x_tok[:, 0:SEQ // P, :], x_prompt.rearrange("(m p) d -> p m d", p=P)).then_inc(x_landed[0], 16)
            sp.dma_start(x_tok[:, SEQ // P:, :], x_sample.rearrange("(m p) d -> p m d", p=P)).then_inc(x_landed[1], 16)

            def weights(w, src, kt, slot=None):
                s = w % 2 if slot is None else slot
                if slot is not None or w >= 2:
                    sp.wait_ge(lo_split, w - 1)
                sp.dma_start(raw[:, s, 0:kt, :], src.rearrange("(k p) n -> p k n", p=P)).then_inc(weights_landed[s], 16)

            def columns_of(w0, mat, count, kt):
                with sp.Fori(0, count // 2) as i:
                    for s in range(2):
                        weights(w0 + s + 2 * i, mat[:, bass.ds((2 * i + s) * P, P)], kt, slot=(w0 + s) % 2)

            for n, (_, _, c) in enumerate(AB_UNITS):
                weights(n, ab_w_in[:, c:c + P], KT)
            for j in range(6):
                w = BASE["fnet"] - KT + j
                sp.wait_ge(lo_split, w - 1)
                sp.dma_start(raw[:, w % 2, :, :], dft[j].rearrange("p (k n) -> p k n", k=KT)).then_inc(
                    weights_landed[w % 2], 16)
            columns_of(BASE["ab_out"] - KT, ab_w_out, KT, KT)
            for layer in range(2):
                if layer:
                    for n, (kind, _, c) in enumerate(C_UNITS):
                        if kind == "o":
                            weights(BASE["c"] - KT + n, c_w_out[0:EARLY_KT * P, c:c + P], EARLY_KT)
                        else:
                            weights(BASE["c"] - KT + n, c_w_in[:, c:c + P], KT)
                    for n in range(KT):
                        first = EARLY_KT if n < EARLY_UNITS else 0
                        weights(BASE["c_out"] - KT + n, c_w_out[first * P:, n * P:(n + 1) * P], KT - first)
                first = 0
                for c, tiles in enumerate(CHUNKS):
                    w0 = BASE[f"gate_up{layer}{c}"] - KT
                    with sp.Fori(0, tiles) as i:
                        for s, mat in enumerate((w_gate, w_up)):
                            weights(w0 + s + 2 * i, mat[layer][:, bass.ds((first + i) * P, P)], KT, slot=(w0 + s) % 2)
                    columns_of(BASE[f"down{layer}{c}"] - KT, w_down[layer][first * P:(first + tiles) * P, :], KT, tiles)
                    first += tiles
            for n in range(KT):
                sp.wait_ge(unit_read, reads(BASE["store"] + n))
                sl = slice(n * P, (n + 1) * P)
                sp.dma_start(y_prompt[:, sl].rearrange("(m p) d -> p m d", p=P),
                             y_tok[:, 0:SEQ // P, sl]).then_inc(y_stored, 16)
                sp.dma_start(y_sample[:, sl].rearrange("(m p) d -> p m d", p=P),
                             y_tok[:, SEQ // P:, sl]).then_inc(y_stored, 16)
            sp.wait_ge(y_stored, 32 * KT)

        @block.tensor
        def _(pe):
            def product3(out, w_hi, w_lo, m_hi, m_lo, start, stop):
                pe.matmul(out, w_hi, m_hi, start=start, stop=False)
                pe.matmul(out, w_hi, m_lo, start=False, stop=False)
                return pe.matmul(out, w_lo, m_hi, start=False, stop=stop)

            def linear(n, slot, pair, kt, waits, middle=None):
                pe.wait_ge(lo_split, n - KT + 1)
                pe.wait_ge(unit_read, waits[2])
                pe.wait_ge(waits[0], waits[1] - 1)
                for k in range(kt):
                    if k == kt - 1:
                        pe.wait_ge(waits[0], waits[1])
                    for h in range(2):
                        last = product3(unit_ps[:, slot, h, 0:HALF], whi[:, slot, k, :], wlo[:, slot, k, :],
                                        pair[:, k, 0, h * HALF:(h + 1) * HALF], pair[:, k, 1, h * HALF:(h + 1) * HALF],
                                        k == 0, k == kt - 1)
                last.then_inc(unit_done, 1)

            def column_sums(g, squares):
                for m in range(TT):
                    last = pe.matmul(misc_ps[:, 0, 2 * m:2 * m + 2], squares[:, m * P:(m + 1) * P], ones[:, :],
                                     start=True, stop=True)
                last.then_inc(colsum_done, 1)

            def broadcast(g):
                pe.wait_ge(inv_done, g + 1)
                if g:
                    pe.wait_ge(bc_read, broadcasts(g) - 1)
                for m in range(TT):
                    last = pe.matmul(misc_ps[:, 1 + m // HT, (m % HT) * P:(m % HT + 1) * P],
                                     inv[:, g % 2, m:m + 1].to_broadcast([P, P]), ident, start=True, stop=True)
                last.then_inc(bc_done, 1)

            def trunk_norm(g, r):
                pe.wait_ge(sq_summed, KT * (r + 1))
                column_sums(g, sumsq)
                broadcast(g)

            pe.wait_ge(tables_landed, 48)
            pe.wait_ge(const_ready, 1)
            pe.wait_ge(x_landed[0], 16)
            pe.wait_ge(x_landed[1], 16)
            for n in range(KT):
                if n >= 2:
                    pe.wait_ge(unit_read, reads(n - 2))
                for m in range(TT):
                    last = pe.transpose(unit_ps[:, n % 2, m // HT, (m % HT) * P:(m % HT + 1) * P],
                                        x_tok[:, m, n * P:(n + 1) * P], ident)
                last.then_inc(unit_done, 1)

            for j, (kind, _, _) in enumerate(AB_UNITS):
                n = BASE["ab"] + j
                linear(n, n % 2, pairA, KT, (h_lo, KT, reads(n - 2)))
                if AB_UNITS[j - 1][0] == "v":
                    k = AB_UNITS[j - 1][1]
                    pe.wait_ge(unit_read, reads(n - 1))
                    if k == 0:
                        pe.wait_ge(z_read, 4)
                    elif k >= 2:
                        pe.wait_ge(vT_read, k - 1)
                    for m in range(TT):
                        last = pe.transpose(misc_ps[:, 2 * (k % 2) + m // HT, (m % HT) * P:(m % HT + 1) * P],
                                            T[1 + k % 2][:, m * P:(m + 1) * P], ident)
                    last.then_inc(vT_done, 1)
                if j == 0:
                    trunk_norm(CHAIN["ab"], 0)
                if j in (2, 3):
                    pe.wait_ge(unit_read, reads(BASE["ab"]))
                    pe.wait_ge(bc_read, 1)
                    for t in range(2):
                        dt = 2 * (j - 2) + t
                        if dt >= 2:
                            pe.wait_ge(z_read, dt - 1)
                        for h in range(2):
                            last = pe.matmul(misc_ps[:, 2 * t + h, 0:HALF], upw[0:2 * RANK, dt, :],
                                             ranks[0:2 * RANK, h * HALF:(h + 1) * HALF], start=True, stop=True)
                        last.then_inc(z_done, 1)

            for d in range(2):
                for t in range(2):
                    dt = 2 * d + t
                    pe.wait_ge(k_gated, dt + 1)
                    if dt == 0:
                        pe.wait_ge(vT_read, HEADS)
                    elif t == 1:
                        pe.wait_ge(kT_read, dt)
                    else:
                        pe.wait_ge(state_sum, NS)
                    for m in range(TT):
                        last = pe.transpose(misc_ps[:, m // HT, (m % HT) * P:(m % HT + 1) * P],
                                            kin[:, t, m * P:(m + 1) * P], ident)
                    last.then_inc(kT_done, 1)
                pe.wait_ge(kT_read, 2 * d + 2)
                for i, (c, _, _) in enumerate(STATES[d]):
                    if i >= 2:
                        pe.wait_ge(state_sum, NS * d + i - 1)
                    for t in range(2):
                        for e in range(2):
                            last = pe.matmul(misc_ps[e * DK:(e + 1) * DK, i % 2, t * P:(t + 1) * P],
                                             kintok[:, t, c // 2, c % 2, e * DK:(e + 1) * DK],
                                             v_ab[:, c // 2, (2 * t + e) * DV:(2 * t + e + 1) * DV],
                                             start=True, stop=True)
                    last.then_inc(kv_done, 1)

                def scores(m):
                    if d or m:
                        pe.wait_ge(att_masked, TT * d + m)
                    for h in range(HEADS):
                        last = pe.matmul(misc_ps[:, 2, h * P:(h + 1) * P], kin[:, h // 2, m * P:(m + 1) * P],
                                         qpad[:, h, m * P:(m + 1) * P], start=True, stop=True)
                    last.then_inc(att_done, 1)

                pe.wait_ge(q_gated, 2 * d + 2)
                pe.wait_ge(state_sum, NS * (d + 1))
                scores(0)
                for m in range(TT):
                    if m + 1 < TT:
                        scores(m + 1)
                    pe.wait_ge(att_masked, TT * d + m + 1)
                    if d or m:
                        pe.wait_ge(o_read, TT * d + m)
                    for h in range(HEADS):
                        inter = [c for c in (2 * m, 2 * m + 1) if c not in FIRSTS[d]]
                        last = pe.matmul(misc_ps[:, 3, h * P:(h + 1) * P], v_ab[:, m, h * DV:(h + 1) * DV],
                                         T[m % 2][:, h * P:(h + 1) * P], start=True, stop=not inter)
                        for c in inter:
                            o = (c % 2) * CHUNK
                            last = pe.matmul(misc_ps[:, 3, h * P + o:h * P + o + CHUNK], state[:, c, h // 2, :],
                                             qpad[:, h, c * CHUNK:(c + 1) * CHUNK], start=False, stop=c == inter[-1])
                    last.then_inc(o_done, 1)

            for h in range(HEADS):
                g = CHAIN["o"] + h
                pe.wait_ge(osq_ready, h + 1)
                if h:
                    pe.wait_ge(root_done, g)
                column_sums(g, T[2 + h % 2])
                if h:
                    broadcast(g - 1)
            broadcast(CHAIN["o"] + HEADS - 1)

            n = BASE["fnet"]
            pe.wait_ge(lo_split, n - KT + 1)
            pe.wait_ge(bc_read, CHAIN["o"] + HEADS)
            for i in range(FG * HT):
                g, b = i // HT, i % 4
                pe.wait_ge(f_lo, g + 1)
                if i >= 4:
                    pe.wait_ge(wave_lo, i - 3)
                for m in (2 * (i % HT), 2 * (i % HT) + 1):
                    last = product3(misc_ps[:, b, (m % 2) * 2 * FW:(m % 2 + 1) * 2 * FW],
                                    fpair[:, g % 2, 0, m * P:(m + 1) * P], fpair[:, g % 2, 1, m * P:(m + 1) * P],
                                    whi[:, n % 2, 0:2, :], wlo[:, n % 2, 0:2, :], True, True)
                last.then_inc(unit_done if i == FG * HT - 1 else wave_done, 1)
            pe.wait_ge(wave_lo, FG * HT)
            for j in range(4):
                n = BASE["fnet"] + 1 + j
                pe.wait_ge(lo_split, n - KT + 1)
                for g in range(FG):
                    for kk in range(2):
                        k = 2 * j + kk
                        part, m = k // 4, k % 4
                        last = product3(misc_ps[:, g, :], wave[:, 0, g, m, part * FW:(part + 1) * FW],
                                        wave[:, 1, g, m, part * FW:(part + 1) * FW],
                                        whi[:, n % 2, 4 * kk:4 * kk + 4, :], wlo[:, n % 2, 4 * kk:4 * kk + 4, :],
                                        k == 0, k == 7)
                    if j == 3 and g < FG - 1:
                        last.then_inc(y_done, 1)
                last.then_inc(unit_done, 1)
            n = BASE["fnet"] + 5
            pe.wait_ge(lo_split, n - KT + 1)
            for g in range(FG):
                pe.wait_ge(mixed_lo, HEADS + g + 1)
                for k in range(4):
                    part, m = k // 2, SEQ // P + k % 2
                    last = product3(misc_ps[:, g, 0:DEC], wave[:, 0, g, m, part * FW:(part + 1) * FW],
                                    wave[:, 1, g, m, part * FW:(part + 1) * FW],
                                    whi[:, n % 2, 2 * k:2 * k + 2, :], wlo[:, n % 2, 2 * k:2 * k + 2, :],
                                    k == 0, k == 3)
                if g < FG - 1:
                    last.then_inc(y_done, 1)
            last.then_inc(unit_done, 1)

            def out_projection(seg, pair, ready, count, kt):
                n0 = BASE[seg]
                with pe.Fori(0, KT // 2) as i:
                    for s in range(2):
                        linear(n0 + s + 2 * i, (n0 + s) % 2, pair, kt, (ready, count, reads(n0 + s - 2) + 2 * i))

            def ffn(layer, g, r, pair, acts):
                done = FT * layer
                for c, tiles in enumerate(CHUNKS):
                    n0 = BASE[f"gate_up{layer}{c}"]

                    def gate_up(i, between=None):
                        for s in range(2):
                            linear(n0 + s + 2 * i, (n0 + s) % 2, pair, KT,
                                   (h_lo, KT * (r + 1), reads(n0 + s - 2) + 2 * i))
                            if s == 0 and between:
                                between()

                    gate_up(0, (lambda: trunk_norm(g, r)) if c == 0 else None)
                    with pe.Fori(1, tiles) as i:
                        gate_up(i)
                    done += tiles
                    out_projection(f"down{layer}{c}", acts, act_lo, done, tiles)

            out_projection("ab_out", pairB, mixed_lo, HEADS + 2 * FG, KT)
            ffn(0, CHAIN["ffn0"], 1, pairA, pairB)

            def head_sums(i):
                pe.wait_ge(qk_sq, i + 1)
                bank = 3 if QK[i][1] == "q" else 0
                if i:
                    pe.wait_ge(rot_read, 2 * i)
                for m in range(TT):
                    last = pe.matmul(misc_ps[:, bank, 2 * m:2 * m + 2], T[1][:, m * P:(m + 1) * P], ones[:, :],
                                     start=True, stop=True)
                last.then_inc(colsum_done, 1)

            def turn(i, half):
                pe.wait_ge(qk_gain, i + 1)
                pe.wait_ge(root_done, CHAIN["qk"] + i + 1)
                if QK[i][1] == "q" and half:
                    pe.wait_ge(rot_read, 2 * i + 1)
                bank = 0 if QK[i][1] == "k" and half else 3
                pe.matmul(misc_ps[:, bank, 0:HALF], rot, T[2 + i % 2][:, half * HALF:(half + 1) * HALF],
                          start=True, stop=True).then_inc(rot_done, 1)

            def attention_scores(j):
                _, h, s0, ln, qt = STEPS[j]
                pe.wait_ge(qk_lo, KVH + h + 1)
                if j >= 2:
                    pe.wait_ge(s_exp, j - 1)
                q = slice(s0 + qt * P, s0 + (qt + 1) * P)
                kv = h // (AH // KVH)
                last = product3(misc_ps[:, j % 2, 0:ln], pairB[:, h, 0, q], pairB[:, h, 1, q],
                                kpair[:, kv, 0, s0:s0 + ln], kpair[:, kv, 1, s0:s0 + ln], True, True)
                last.then_inc(s_done, 1)

            def flip(j):
                ln = STEPS[j][3]
                pe.wait_ge(s_norm, j + 1)
                if j >= 2:
                    pe.wait_ge(pT_read, j - 1)
                elif j == 1:
                    pe.wait_ge(vT_read, HEADS + KVH)
                for m in range(ln // P):
                    last = pe.transpose(flip_bank(j)[:, m * P:(m + 1) * P], probs[j % 3][:, m * P:(m + 1) * P], ident)
                last.then_inc(pT_done, 1)

            def values(a):
                h, s0, ln = ITEMS[a]
                kv = h // (AH // KVH)
                pe.wait_ge(pT_read, LAST_STEP[a] + 1)
                if a:
                    pe.wait_ge(pv_lo, a)
                for m in range(ln // P):
                    last = pe.matmul(values_bank[:, 0:ln], v_c[:, s0 // P + m, kv * HD:(kv + 1) * HD],
                                     probsT[a % 2][:, m, 0:ln], start=m == 0, stop=m == ln // P - 1)
                last.then_inc(pv_done, 1)

            def between(slot):
                for what, i, *half in PLAN.get(slot, ()):
                    if what == "sums":
                        head_sums(i)
                    elif what == "turn":
                        if QK[i][1] == "k" and not half[0]:
                            broadcast(CHAIN["qk"] + i)
                        turn(i, *half)
                    elif what == "scores":
                        attention_scores(i)
                    elif what == "flip":
                        flip(i)
                    elif what == "values":
                        values(i)
                    elif what == "values_turn":
                        pe.wait_ge(unit_read, reads(BASE["c"] + slot // 8 - 1))
                        if i:
                            pe.wait_ge(vT_read, HEADS + i)
                        for m in range(TT):
                            last = pe.transpose(unit_ps[:, 1, m // HT, (m % HT) * P:(m % HT + 1) * P],
                                                v_flat[i][:, m * P:(m + 1) * P], ident)
                        last.then_inc(vT_done, 1)

            pe.wait_ge(unit_read, reads(BASE["c"] - 1))
            for j, (kind, _, _) in enumerate(C_UNITS):
                n = BASE["c"] + j
                pe.wait_ge(lo_split, n - KT + 1)
                for slot in range(8):
                    half = slot // 4
                    if j and slot == 0:
                        pe.wait_ge(half_read, j)
                    if j and slot == 4:
                        pe.wait_ge(unit_read, reads(n - 1))
                    kt = EARLY_KT if kind == "o" else KT
                    moving = pairB if kind == "o" else pairA
                    for k in range(kt * (slot % 4) // 4, kt * (slot % 4 + 1) // 4):
                        if kind == "o":
                            pe.wait_ge(pv_lo, 2 * (k + 1))
                        if j == 0:
                            pe.wait_ge(h_lo, 2 * KT + k + 1)
                        tokens = slice(half * HALF, (half + 1) * HALF)
                        last = product3(unit_ps[:, 0, half, 0:HALF], whi[:, n % 2, k, :], wlo[:, n % 2, k, :],
                                        moving[:, k, 0, tokens], moving[:, k, 1, tokens], k == 0, k == kt - 1)
                    if slot % 4 == 3:
                        last.then_inc(unit_done if half else half_done, 1)
                    if j == 0 and slot == 4:
                        trunk_norm(CHAIN["c"], 2)
                    between(8 * j + slot)
            for slot in range(8 * len(C_UNITS), SLOTS):
                between(slot)
            pe.wait_ge(pv_lo, len(ITEMS))
            for j in range(KT):
                n = BASE["c_out"] + j
                first = EARLY_KT if j < EARLY_UNITS else 0
                linear(n, n % 2, pairB[:, first:, :, :], KT - first, (pv_lo, len(ITEMS), reads(n - 2 + (j == 0))))
            ffn(1, CHAIN["ffn1"], 3, pairA, pairB)

            for f in range(KT):
                n = BASE["store"] + f
                pe.wait_ge(unit_read, max(reads(n - 2), reads(BASE["store"] - KT + f)))
                for m in range(TT):
                    last = pe.transpose(unit_ps[:, n % 2, m // HT, (m % HT) * P:(m % HT + 1) * P],
                                        x[:, f, m * P:(m + 1) * P], ident)
                last.then_inc(unit_done, 1)

        @block.scalar
        def _(act):
            act.dma_start(tab[:, :, :], tables.rearrange("p (a b) -> p a b", a=4)).then_inc(tables_landed, 16)
            act.dma_start(cols[:, :], columns).then_inc(tables_landed, 16)
            act.dma_start(upw[0:2 * RANK, :, :], up_pad.rearrange("p (a b) -> p a b", a=4)).then_inc(tables_landed, 16)

            def split_hi(w, slot=None, turn=None):
                s = w % 2 if slot is None else slot
                act.wait_ge(weights_landed[s], 16 * ((w // 2 if turn is None else turn) + 1))
                if slot is not None or w >= 2:
                    act.wait_ge(unit_done, w - 2 + KT + 1)
                act.activation(whi[:, s, :, :], raw[:, s, :, :], ACT.Copy).then_inc(hi_split, 1)

            def ahead(n):
                if n - KT + 2 < N_WEIGHTS:
                    split_hi(n - KT + 2)

            def ahead_loop(n0, s, i):
                w = n0 - KT + 2 + s
                split_hi(w + 2 * i, slot=w % 2, turn=w // 2 + i)

            def finish(f, n_read, r, gain, pair, tile):
                if not isinstance(f, int) or f:
                    act.wait_ge(sq_summed, f)
                act.wait_ge(unit_read, n_read)
                act.activation(pair[:, tile, 0, :], x[:, tile, :], ACT.Copy,
                               scale=cols[:, bass.ds(COL[gain] + tile, 1)] if not isinstance(tile, int)
                               else cols[:, COL[gain] + tile:COL[gain] + tile + 1]).then_inc(h_hi, 1)
                act.activation(T[2][:, :], x[:, tile, :], ACT.Square).then_inc(sq_ready, 1)

            def root_of(g, width):
                act.wait_ge(colsum_done, g + 1)
                act.activation(root[:, g % 2, :], misc_ps[:, 0, 0:2 * TT:2], ACT.Sqrt, scale=1.0 / width,
                               bias=cols[:, COL["eps"]:COL["eps"] + 1]).then_inc(root_done, 1)

            def values_turned(turned, ps, out):
                act.wait_ge(vT_done, turned)
                act.activation(out.rearrange("p (a m) e -> p a m e", a=2), ps.rearrange("p a (m e) -> p a m e", m=HT),
                               ACT.Copy).then_inc(vT_read, 1)

            act.wait_ge(tables_landed, 48)
            split_hi(0)
            split_hi(1)
            for f in range(KT):
                finish(f, reads(f), 0, "ab", pairA, f)
            root_of(CHAIN["ab"], D)
            for j, (kind, k, _) in enumerate(AB_UNITS):
                n = BASE["ab"] + j
                ahead(n)
                if AB_UNITS[j - 1][0] == "v":
                    k_last = AB_UNITS[j - 1][1]
                    values_turned(k_last + 1, misc_ps[:, 2 * (k_last % 2):2 * (k_last % 2) + 2, 0:HALF],
                                  v_ab[:, :, k_last * DV:(k_last + 1) * DV])
                if j in (2, 3):
                    for dt in (2 * (j - 2), 2 * (j - 2) + 1):
                        t = T[3 + dt % 2]
                        act.wait_ge(z_read, dt + 1)
                        if dt >= 2:
                            act.wait_ge(gate_ready, dt - 1)
                        act.activation(t[:, :], gcum[:, dt, :], ACT.Abs).then_inc(log_step, 1)
                        act.wait_ge(log_step, 2 * dt + 1)
                        act.activation(t[:, :], t[:, :], ACT.Exp, scale=-1.0).then_inc(log_step, 1)
                        act.wait_ge(log_step, 2 * dt + 2)
                        act.activation(t[:, :], t[:, :], ACT.Ln, bias=1.0).then_inc(log_ready, 1)
                if kind == "r":
                    act.wait_ge(unit_read, reads(n))
                    act.activation(r_ab[:, k, :], r_ab[:, k, :], ACT.Silu).then_inc(r_silu, 1)

            act.wait_ge(pad_zeroed, 4)
            for d in range(2):
                for t in range(2):
                    dt = 2 * d + t
                    act.wait_ge(gate_summed, dt + 1)
                    if dt:
                        act.wait_ge(q_gated, dt)
                    act.activation(T[3][:, :], gcum[:, dt, :], ACT.Exp, scale=1.0 / GATE_NORM).then_inc(exp_pos, 1)
                    if dt:
                        act.wait_ge(k_gated, dt)
                    act.activation(T[4][:, :], gcum[:, dt, :], ACT.Exp, scale=-1.0 / GATE_NORM).then_inc(exp_neg, 1)
                    end = slice(CHUNK - 1, TOK, CHUNK) if d == 0 else slice(0, TOK, CHUNK)
                    act.activation(dec[:, dt, :], gcum[:, dt, end], ACT.Exp, scale=1.0 / GATE_NORM).then_inc(decay_ready, 1)
                for t in range(2):
                    act.wait_ge(kT_done, 2 * d + t + 1)
                    for b in range(2):
                        for e in range(2):
                            rows = slice(e * CHUNK, (e + 1) * CHUNK)
                            last = act.activation(kintok[rows, t, b * HT:(b + 1) * HT, e, :],
                                                  misc_ps[rows, b, 0:HALF].rearrange("p (m k) -> p m k", m=HT), ACT.Copy)
                    last.then_inc(kT_read, 1)

            def head_squares(h):
                act.wait_ge(o_read, 2 * TT)
                if h >= 2:
                    act.wait_ge(colsum_done, CHAIN["o"] + h - 1)
                act.activation(T[2 + h % 2][:, :], o_ab[:, h, :], ACT.Square).then_inc(osq_ready, 1)
                root_of(CHAIN["o"] + h, DV)

            head_squares(0)
            for h in range(HEADS):
                if h + 1 < HEADS:
                    head_squares(h + 1)
                act.wait_ge(o_gated, h + 1)
                act.activation(pairB[:, h, 0, :], T[4][:, :], ACT.Copy).then_inc(mixed_hi, 1)

            def group_hi(g):
                if g >= 2:
                    act.wait_ge(wave_done, HT * (g - 1))
                act.activation(fpair[:, g % 2, 0, :], f_ab[:, g, :], ACT.Copy).then_inc(f_hi, 1)

            group_hi(0)
            group_hi(1)
            for i in range(FG * HT):
                g, m = i // HT, 2 * (i % HT)
                wave_product(act, i)
                act.activation(wave[:, 0, g, m:m + 2, :], misc_ps[:, i % 4, :].rearrange("p (m n) -> p m n", m=2),
                               ACT.Copy).then_inc(wave_hi, 1)
                if i % HT == HT - 1 and g + 2 < FG:
                    group_hi(g + 2)
            for j in range(5):
                ahead(BASE["fnet"] + j)
            for part, (s0, ln) in enumerate(((0, SEQ), (SEQ, DEC))):
                if part:
                    ahead(BASE["fnet"] + 5)
                for g in range(FG):
                    token_product(act, part, g)
                    act.activation(pairB[:, HEADS + g, 0, s0:s0 + ln], misc_ps[:, g, 0:ln], ACT.Copy).then_inc(mixed_hi, 1)

            def out_projection(seg, r=None, gain=None, pair=None):
                n0 = BASE[seg]
                if seg == "down12":
                    for s in range(KT - 2):
                        ahead(n0 + s)
                    return
                with act.Fori(0, KT // 2) as i:
                    for s in range(2):
                        ahead_loop(n0, s, i)
                        if r is not None:
                            finish(KT * r + s + 2 * i, reads(n0 + s) + 2 * i, r, gain, pair, s + 2 * i)

            def ffn(layer, g, acts, nxt):
                root_of(g, D)
                done = FT * layer
                for c, tiles in enumerate(CHUNKS):
                    n0 = BASE[f"gate_up{layer}{c}"]
                    with act.Fori(0, tiles) as i:
                        ahead_loop(n0, 0, i)
                        act.wait_ge(unit_read, reads(n0) + 2 * i)
                        act.activation(T[0][:, :], T[0][:, :], ACT.Silu).then_inc(silu_done, 1)
                        ahead_loop(n0, 1, i)
                        act.wait_ge(prod_done, done + 1 + i)
                        act.activation(acts[:, i, 0, :], T[1][:, :], ACT.Copy).then_inc(act_hi, 1)
                    done += tiles
                    out_projection(f"down{layer}{c}", *(nxt if c == 2 and nxt else ()))

            out_projection("ab_out", 1, "ffn0", pairA)
            ffn(0, CHAIN["ffn0"], pairB, (2, "c", pairA))

            def head_evacuate(i, n):
                if i:
                    act.wait_ge(qk_sum, i)
                act.activation(T[1][:, :], T[0][:, :], ACT.Square).then_inc(qk_sq, 1)
                if i >= 2:
                    act.wait_ge(rot_done, 2 * (i - 1))
                    act.wait_ge(qk_cos, i - 1)
                col = COL["qn" if QK[i][1] == "q" else "kn"]
                act.activation(T[2 + i % 2][:, :], T[0][:, :], ACT.Copy, scale=cols[:, col:col + 1]).then_inc(qk_gain, 1)

            def head_root(i):
                g = CHAIN["qk"] + i
                bank = 3 if QK[i][1] == "q" else 0
                act.wait_ge(colsum_done, g + 1)
                act.wait_ge(inv_done, g - 1)
                act.activation(root[:, g % 2, :], misc_ps[:, bank, 0:2 * TT:2], ACT.Sqrt, scale=1.0 / HD,
                               bias=cols[:, COL["eps"]:COL["eps"] + 1]).then_inc(root_done, 1)

            def head_hi(i):
                if QK[i][1] == "k":
                    act.wait_ge(bc_read, broadcasts(CHAIN["qk"] + i))
                else:
                    act.wait_ge(qk_sum, i + 1)
                pair = kpair[:, QK[i][2]] if QK[i][1] == "k" else pairB[:, QK[i][2]]
                act.activation(pair[:, 0, :], T[4][:, :], ACT.Copy).then_inc(qk_hi, 1)

            def exponentials(j):
                _, h, s0, ln, qt = STEPS[j]
                act.wait_ge(s_neg, j + 1)
                if j >= 3:
                    act.wait_ge(pT_done, j - 2)
                act.activation(probs[j % 3][:, 0:ln], misc_ps[:, j % 2, 0:ln], ACT.Exp,
                               scale=q_scale[:, h, s0 // P + qt:s0 // P + qt + 1], bias=negmax[:, j % 2, 1:2],
                               accum_out=expsum[:, j % 2, 0:1]).then_inc(s_exp, 1)

            def flipped(j):
                a, _, _, ln, qt = STEPS[j]
                act.wait_ge(pT_done, j + 1)
                if a >= 2:
                    act.wait_ge(pv_done, a - 1)
                act.activation(probsT[a % 2][:, 0:ln // P, qt * P:(qt + 1) * P],
                               flip_bank(j)[:, 0:ln].rearrange("p (m q) -> p m q", q=P), ACT.Copy).then_inc(pT_read, 1)

            def result_hi(a):
                h, s0, ln = ITEMS[a]
                act.wait_ge(pv_done, a + 1)
                act.activation(pairB[:, h, 0, s0:s0 + ln], values_bank[:, 0:ln], ACT.Copy).then_inc(pv_hi, 1)

            root_of(CHAIN["c"], D)
            for slot in range(SLOTS):
                j = slot // 8 - 1
                if slot % 8 == 0 and 0 <= j < len(C_UNITS):
                    ahead(BASE["c"] + j)
                    if j in UNIT_OF:
                        act.wait_ge(unit_read, reads(BASE["c"] + j))
                        head_evacuate(UNIT_OF.index(j), BASE["c"] + j)
                for what, i, *half in PLAN.get(slot, ()):
                    if what == "sums":
                        head_root(i)
                    elif what == "split":
                        head_hi(i)
                    elif what == "scores":
                        exponentials(i)
                    elif what == "flip":
                        flipped(i)
                    elif what == "values":
                        result_hi(i)
                    elif what == "values_turn":
                        values_turned(HEADS + i + 1, unit_ps[:, 1, :, 0:HALF], v_c[:, :, i * HD:(i + 1) * HD])
            out_projection("c_out", 3, "ffn1", pairA)
            ffn(1, CHAIN["ffn1"], pairB, None)

        @block.vector
        def _(dve):
            def split_lo(w, slot=None):
                s = w % 2 if slot is None else slot
                dve.wait_ge(hi_split, w + 1)
                dve.tensor_tensor(wlo[:, s, :, :], raw[:, s, :, :], whi[:, s, :, :].bitcast(F32), ALU.subtract).then_inc(
                    lo_split, 1)

            def ahead(n):
                if n - KT + 2 < N_WEIGHTS:
                    split_lo(n - KT + 2)

            def ahead_loop(n0, s, i):
                w = n0 - KT + 2 + s
                split_lo(w + 2 * i, slot=w % 2)

            def gain_lo(f, gain, pair, tile):
                dve.wait_ge(h_hi, f + 1)
                col = (cols[:, COL[gain] + tile:COL[gain] + tile + 1] if isinstance(tile, int)
                       else cols[:, bass.ds(COL[gain] + tile, 1)])
                dve.scalar_tensor_tensor(pair[:, tile, 1, :], x[:, tile, :], col, pair[:, tile, 0, :].bitcast(F32),
                                         ALU.mult, ALU.subtract).then_inc(h_lo, 1)

            def inverse(g):
                dve.wait_ge(root_done, g + 1)
                if g >= 2:
                    dve.wait_ge(bc_done, broadcasts(g - 2))
                dve.reciprocal(inv[:, g % 2, :], root[:, g % 2, :]).then_inc(inv_done, 1)

            def trunk_norm(g):
                inverse(g)
                dve.wait_ge(bc_done, broadcasts(g))
                dve.tensor_copy(rstd[:, :, :], misc_ps[:, 1:3, 0:HALF]).then_inc(bc_read, 1)
                dve.wait_ge(bc_read, broadcasts(g))

            dve.memset(ones[:, :], 1.0).then_inc(const_ready, 1)
            dve.memset(reset[:, :, :], 1.0).then_inc(reset_ready, 1)
            dve.wait_ge(reset_ready, 1)
            dve.memset(reset[:, 0, 0:TOK:CHUNK], 0.0).then_inc(reset_ready, 1)
            dve.memset(reset[:, 1, CHUNK - 1:TOK:CHUNK], 0.0).then_inc(reset_ready, 1)
            split_lo(0)
            split_lo(1)
            dve.wait_ge(tables_landed, 48)
            for f in range(KT):
                dve.wait_ge(unit_done, f + 1)
                dve.tensor_copy(two(x[:, f, :]), ups(f)).then_inc(unit_read, 1)
                if f:
                    gain_lo(f - 1, "ab", pairA, f - 1)
            gain_lo(KT - 1, "ab", pairA, KT - 1)

            trunk_norm(CHAIN["ab"])
            dve.wait_ge(reset_ready, 3)
            for j, (kind, k, _) in enumerate(AB_UNITS):
                n = BASE["ab"] + j
                dve.wait_ge(unit_done, n + 1)
                if kind == "l":
                    dve.tensor_tensor(two(ranks[0:2 * RANK, :]), ups(n)[0:2 * RANK], rstd[0:2 * RANK], ALU.mult).then_inc(unit_read, 1)
                elif kind == "q":
                    dve.scalar_tensor_tensor(two(q_ab[:, k, :]), ups(n), DK ** -0.5, rstd[:, :, :], ALU.mult,
                                             ALU.mult).then_inc(unit_read, 1)
                elif kind == "v":
                    if k >= 2:
                        dve.wait_ge(vT_done, k - 1)
                    dve.tensor_tensor(two(T[1 + k % 2][:, :]), ups(n), rstd[:, :, :], ALU.mult).then_inc(unit_read, 1)
                else:
                    out = {"k": k_ab, "r": r_ab, "f": f_ab}[kind]
                    dve.tensor_tensor(two(out[:, k, :]), ups(n), rstd[:, :, :], ALU.mult).then_inc(unit_read, 1)
                ahead(n)
                if j in (2, 3):
                    d = j - 2
                    for dt in (2 * d, 2 * d + 1):
                        dve.wait_ge(z_done, dt + 1)
                        bank = 2 * (dt % 2)
                        dve.tensor_scalar(two(gcum[:, dt, :]), misc_ps[:, bank:bank + 2, 0:HALF],
                                          cols[:, COL["bias"] + dt:COL["bias"] + dt + 1], None, ALU.add).then_inc(z_read, 1)
                    for dt in (2 * d, 2 * d + 1):
                        dve.wait_ge(log_ready, dt + 1)
                        if dt:
                            dve.wait_ge(gate_summed, dt)
                        dve.scalar_tensor_tensor(T[5][:, :], gcum[:, dt, :], 0.0, T[3 + dt % 2][:, :], ALU.min,
                                                 ALU.subtract).then_inc(gate_ready, 1)
                        dve.wait_ge(gate_ready, dt + 1)
                        step = 1 if d == 0 else -1
                        dve.tensor_tensor_scan(gcum[:, dt, ::step], reset[:, d, ::step], T[5][:, ::step], 0.0, ALU.mult,
                                               ALU.add).then_inc(gate_summed, 1)

            added = 0
            dve.wait_ge(pad_zeroed, 4)
            for d in range(2):
                for t in range(2):
                    dt = 2 * d + t
                    dve.wait_ge(exp_pos, dt + 1)
                    if d:
                        dve.wait_ge(o_done, TT)
                    for e in range(2):
                        rows = slice(e * DK, (e + 1) * DK)
                        last = dve.tensor_tensor(qpad[rows, 2 * t + e, :], q_ab[rows, t, :], T[3][rows, :], ALU.mult)
                    last.then_inc(q_gated, 1)
                dve.wait_ge(decay_ready, 2 * d + 2)
                for i, (c, nxt, first) in enumerate(STATES[d]):
                    dve.wait_ge(kv_done, NS * d + i + 1)
                    kv = misc_ps[:, i % 2, 0:2 * P].rearrange("p (t e) -> p t e", t=2)
                    decay = dec[:, 2 * d:2 * d + 2, c].unsqueeze(2).to_broadcast([P, 2, P])
                    if not first:
                        dve.wait_ge(state_sum, NS * d + i)
                        dve.tensor_tensor(T[5][:, 0:2 * P].rearrange("p (t e) -> p t e", t=2), kv, state[:, c, :, :],
                                          ALU.add).then_inc(kv_added, 1)
                        added += 1
                        dve.wait_ge(kv_added, added)
                        kv = T[5][:, 0:2 * P].rearrange("p (t e) -> p t e", t=2)
                    dve.tensor_tensor(state[:, nxt, :, :], kv, decay, ALU.mult).then_inc(state_sum, 1)

                def masked(m):
                    dve.wait_ge(att_done, TT * d + m + 1)
                    if d or m >= 2:
                        dve.wait_ge(o_done, TT * d + m - 1 if m else TT * d)
                    dve.tensor_tensor(T[m % 2][:, 0:HEADS * P].rearrange("p (h i) -> p h i", h=HEADS),
                                      misc_ps[:, 2, :].rearrange("p (h i) -> p h i", h=HEADS),
                                      mask[:, d, :].unsqueeze(1).to_broadcast([P, HEADS, P]), ALU.mult).then_inc(att_masked, 1)

                masked(0)
                for m in range(TT):
                    if m + 1 < TT:
                        masked(m + 1)
                    dve.wait_ge(o_done, TT * d + m + 1)
                    o = o_ab[:, :, m * P:(m + 1) * P]
                    out = misc_ps[:, 3, :].rearrange("p (h i) -> p h i", h=HEADS)
                    if d == 0:
                        dve.tensor_copy(o, out).then_inc(o_read, 1)
                    else:
                        dve.wait_ge(o_read, TT)
                        dve.tensor_tensor(o, out, o, ALU.add).then_inc(o_read, 1)

            inverse(CHAIN["o"])
            dve.wait_ge(r_silu, 4)
            dve.wait_ge(o_read, 2 * TT)
            for h in range(HEADS):
                g = CHAIN["o"] + h
                if h + 1 < HEADS:
                    inverse(g + 1)
                dve.wait_ge(bc_done, g + 1)
                if h:
                    dve.wait_ge(o_gated, h)
                dve.tensor_tensor(two(T[5][:, :]), two(o_ab[:, h, :]), misc_ps[:, 1:3, 0:HALF], ALU.mult).then_inc(bc_read, 1)
                dve.wait_ge(bc_read, g + 1)
                if h:
                    dve.wait_ge(mixed_lo, h)
                dve.scalar_tensor_tensor(T[4][:, :], T[5][:, :], cols[:, COL["out"]:COL["out"] + 1], r_ab[:, h, :],
                                         ALU.mult, ALU.mult).then_inc(o_gated, 1)
                dve.wait_ge(mixed_hi, h + 1)
                dve.tensor_tensor(pairB[:, h, 1, :], T[4][:, :], pairB[:, h, 0, :].bitcast(F32), ALU.subtract).then_inc(mixed_lo, 1)

            def group_lo(g):
                dve.wait_ge(f_hi, g + 1)
                dve.tensor_tensor(fpair[:, g % 2, 1, :], f_ab[:, g, :], fpair[:, g % 2, 0, :].bitcast(F32),
                                  ALU.subtract).then_inc(f_lo, 1)

            group_lo(0)
            group_lo(1)
            for i in range(FG * HT):
                g, m = i // HT, 2 * (i % HT)
                dve.wait_ge(wave_hi, i + 1)
                dve.tensor_tensor(wave[:, 1, g, m:m + 2, :], misc_ps[:, i % 4, :].rearrange("p (m n) -> p m n", m=2),
                                  wave[:, 0, g, m:m + 2, :].bitcast(F32), ALU.subtract).then_inc(wave_lo, 1)
                if i % HT == HT - 1 and g + 2 < FG:
                    group_lo(g + 2)
            for j in range(5):
                ahead(BASE["fnet"] + j)
            for part, (s0, ln) in enumerate(((0, SEQ), (SEQ, DEC))):
                if part:
                    ahead(BASE["fnet"] + 5)
                for g in range(FG):
                    dve.wait_ge(mixed_hi, HEADS + FG * part + g + 1)
                    dve.tensor_tensor(pairB[:, HEADS + g, 1, s0:s0 + ln], misc_ps[:, g, 0:ln],
                                      pairB[:, HEADS + g, 0, s0:s0 + ln].bitcast(F32), ALU.subtract).then_inc(mixed_lo, 1)

            def out_projection(seg, r=None, gain=None, pair=None):
                n0 = BASE[seg]
                dve.wait_ge(unit_read, reads(n0 - 1))

                def add(n, slot, tile):
                    dve.wait_ge(unit_done, n + 1)
                    dve.tensor_tensor(two(x[:, tile, :]), unit_ps[:, slot, :, 0:HALF], two(x[:, tile, :]),
                                      ALU.add).then_inc(unit_read, 1)

                if seg == "down12":
                    for s in range(KT):
                        add(n0 + s, (n0 + s) % 2, s)
                        ahead(n0 + s)
                    return
                with dve.Fori(0, KT // 2) as i:
                    for s in range(2):
                        add(n0 + s + 2 * i, (n0 + s) % 2, s + 2 * i)
                        ahead_loop(n0, s, i)
                        if r is not None:
                            gain_lo(KT * r + s + 2 * i, gain, pair, s + 2 * i)

            def ffn(layer, g, nxt):
                trunk_norm(g)
                done = FT * layer
                for c, tiles in enumerate(CHUNKS):
                    n0 = BASE[f"gate_up{layer}{c}"]

                    def gate_up(i, earlier=True):
                        dve.wait_ge(unit_done, n0 + 1 + 2 * i)
                        if earlier:
                            dve.wait_ge(prod_done, done + i)
                        dve.tensor_tensor(two(T[0][:, :]), ups(n0), rstd[:, :, :], ALU.mult).then_inc(unit_read, 1)
                        ahead_loop(n0, 0, i)
                        dve.wait_ge(unit_done, n0 + 2 + 2 * i)
                        if earlier:
                            dve.wait_ge(act_lo, done + i)
                        dve.tensor_tensor(two(T[1][:, :]), ups(n0 + 1), rstd[:, :, :], ALU.mult).then_inc(unit_read, 1)
                        ahead_loop(n0, 1, i)

                    gate_up(0, done > 0)
                    with dve.Fori(1, tiles) as i:
                        gate_up(i)
                    done += tiles
                    out_projection(f"down{layer}{c}", *(nxt if c == 2 and nxt else ()))

            out_projection("ab_out", 1, "ffn0", pairA)
            ffn(0, CHAIN["ffn0"], (2, "c", pairA))

            def evacuate_half(j, half):
                n, (kind, k, _) = BASE["c"] + j, C_UNITS[j]
                ps = unit_ps[:, 0, half, 0:HALF]
                dve.wait_ge(unit_done if half else half_done, n + 1 if half else j + 1)
                if kind == "v":
                    done = dve.tensor_tensor(v_flat[k][:, half * HALF:(half + 1) * HALF], ps, rstd[:, half, :], ALU.mult)
                elif kind == "o":
                    done = dve.tensor_tensor(x[:, k, half * HALF:(half + 1) * HALF], ps,
                                             x[:, k, half * HALF:(half + 1) * HALF], ALU.add)
                else:
                    if not half and UNIT_OF.index(j):
                        dve.wait_ge(qk_gain, UNIT_OF.index(j))
                    done = dve.tensor_tensor(T[0][:, half * HALF:(half + 1) * HALF], ps, rstd[:, half, :], ALU.mult)
                done.then_inc(unit_read if half else half_read, 1)

            def head_inverse(i):
                g = CHAIN["qk"] + i
                if QK[i][1] == "k":
                    inverse(g)
                    return
                dve.wait_ge(root_done, g + 1)
                dve.reciprocal(q_scale[:, QK[i][2], :], root[:, g % 2, :]).then_inc(inv_done, 1)
                dve.wait_ge(inv_done, g + 1)
                dve.tensor_scalar(q_scale[:, QK[i][2], :], q_scale[:, QK[i][2], :], HD ** -0.5, None,
                                  ALU.mult).then_inc(q_scaled, 1)

            def turned(i, half):
                tokens = slice(half * HALF, (half + 1) * HALF)
                bank = 0 if QK[i][1] == "k" and half else 3
                dve.wait_ge(rot_done, 2 * i + half + 1)
                dve.tensor_tensor(T[1][:, tokens], misc_ps[:, bank, 0:HALF], ropes[:, 1, tokens], ALU.mult).then_inc(rot_read, 1)
                if QK[i][1] == "k" and half:
                    dve.wait_ge(qk_sum, i + 1)
                    dve.wait_ge(bc_done, broadcasts(CHAIN["qk"] + i))
                    dve.tensor_tensor(two(T[4][:, :]), two(T[4][:, :]), misc_ps[:, 1:3, 0:HALF], ALU.mult).then_inc(bc_read, 1)

            def largest(j):
                _, h, s0, ln, qt = STEPS[j]
                dve.wait_ge(s_done, j + 1)
                if j >= 2:
                    dve.wait_ge(s_exp, j - 1)
                dve.reduce_max(negmax[:, j % 2, 0:1], misc_ps[:, j % 2, 0:ln], AX.X).then_inc(s_max, 1)
                dve.wait_ge(s_max, j + 1)
                dve.tensor_scalar(negmax[:, j % 2, 1:2], negmax[:, j % 2, 0:1],
                                  q_scale[:, h, s0 // P + qt:s0 // P + qt + 1], -1.0, ALU.mult, ALU.mult).then_inc(s_neg, 1)

            def normalized(j):
                ln = STEPS[j][3]
                dve.wait_ge(s_exp, j + 1)
                dve.reciprocal(expsum[:, j % 2, 1:2], expsum[:, j % 2, 0:1]).then_inc(s_inv, 1)
                dve.wait_ge(s_inv, j + 1)
                dve.tensor_scalar(probs[j % 3][:, 0:ln], probs[j % 3][:, 0:ln], expsum[:, j % 2, 1:2], None,
                                  ALU.mult).then_inc(s_norm, 1)

            def result_lo(a):
                h, s0, ln = ITEMS[a]
                dve.wait_ge(pv_hi, a + 1)
                dve.tensor_tensor(pairB[:, h, 1, s0:s0 + ln], values_bank[:, 0:ln],
                                  pairB[:, h, 0, s0:s0 + ln].bitcast(F32), ALU.subtract).then_inc(pv_lo, 1)

            trunk_norm(CHAIN["c"])
            dve.wait_ge(rope_landed, 16)
            for slot in range(SLOTS):
                j = slot // 8
                if slot % 8 == 0 and 0 < j <= len(C_UNITS):
                    evacuate_half(j - 1, 1)
                    ahead(BASE["c"] + j - 1)
                elif slot % 8 == 4 and j < len(C_UNITS):
                    evacuate_half(j, 0)
                for what, i, *half in PLAN.get(slot, ()):
                    if what == "sums":
                        head_inverse(i)
                    elif what == "turn":
                        turned(i, *half)
                    elif what == "scores":
                        largest(i)
                    elif what == "softmax":
                        normalized(i)
                    elif what == "result":
                        result_lo(i)
            out_projection("c_out", 3, "ffn1", pairA)
            ffn(1, CHAIN["ffn1"], None)
            for f in range(KT):
                n = BASE["store"] + f
                dve.wait_ge(unit_done, n + 1)
                for h in range(2):
                    last = dve.tensor_copy(y_tok[:, h * HT:(h + 1) * HT, f * P:(f + 1) * P],
                                           unit_ps[:, n % 2, h, 0:HALF].rearrange("p (m e) -> p m e", m=HT))
                last.then_inc(unit_read, 1)

        @block.gpsimd
        def _(pool):
            def sum_squares(f):
                pool.wait_ge(sq_ready, f + 1)
                pool.tensor_tensor(sumsq[:, :], sumsq[:, :], T[2][:, :], ALU.add).then_inc(sq_summed, 1)

            def squares(r, g_last):
                if g_last is not None:
                    pool.wait_ge(colsum_done, g_last + 1)
                pool.memset(sumsq[:, :], 0.0).then_inc(sum_zeroed, 1)
                pool.wait_ge(sum_zeroed, r + 1)
                if r == 0:
                    for f in range(KT):
                        if f:
                            pool.wait_ge(sq_summed, f)
                        sum_squares(f)
                    return
                with pool.Fori(0, KT) as i:
                    pool.wait_ge(sq_summed, KT * r + i)
                    sum_squares(KT * r + i)

            squares(0, None)
            pool.wait_ge(unit_done, BASE["fnet"])
            for e in range(2):
                rows = slice(e * DK, (e + 1) * DK)
                pool.memset(qpad[rows, 1 - e:HEADS:2, :], 0.0).then_inc(pad_zeroed, 1)
                pool.memset(kintok[rows, :, :, 1 - e, :], 0.0).then_inc(pad_zeroed, 1)
            for dt in range(4):
                pool.wait_ge(exp_neg, dt + 1)
                if dt >= 2:
                    pool.wait_ge(att_done, TT)
                pool.tensor_tensor(kin[:, dt % 2, :], k_ab[:, dt % 2, :], T[4][:, :], ALU.mult).then_inc(k_gated, 1)

            def ffn(layer):
                done = FT * layer
                for c, tiles in enumerate(CHUNKS):
                    n0 = BASE[f"gate_up{layer}{c}"]
                    with pool.Fori(0, tiles) as i:
                        pool.wait_ge(silu_done, done + 1 + i)
                        pool.wait_ge(unit_read, reads(n0 + 1) + 2 * i)
                        pool.tensor_tensor(T[1][:, :], T[0][:, :], T[1][:, :], ALU.mult).then_inc(prod_done, 1)
                        pool.wait_ge(act_hi, done + 1 + i)
                        pool.tensor_tensor(pairB[:, i, 1, :], T[1][:, :], pairB[:, i, 0, :].bitcast(F32),
                                           ALU.subtract).then_inc(act_lo, 1)
                    done += tiles

            squares(1, CHAIN["ab"])
            ffn(0)
            squares(2, CHAIN["ffn0"])
            pool.wait_ge(h_lo, KT * 3)
            pool.dma_start(ropes[:, :, :], rope.rearrange("p (a t) -> p a t", a=2)).then_inc(rope_landed, 16)
            pool.wait_ge(rope_landed, 16)
            for i, (_, kind, k) in enumerate(QK):
                pair = kpair[:, k] if kind == "k" else pairB[:, k]
                pool.wait_ge(qk_gain, i + 1)
                if i:
                    pool.wait_ge(qk_lo, i)
                pool.tensor_tensor(T[4][:, :], T[2 + i % 2][:, :], ropes[:, 0, :], ALU.mult).then_inc(qk_cos, 1)
                pool.wait_ge(qk_cos, i + 1)
                pool.wait_ge(rot_read, 2 * i + 2)
                pool.tensor_tensor(T[4][:, :], T[4][:, :], T[1][:, :], ALU.add).then_inc(qk_sum, 1)
                pool.wait_ge(qk_hi, i + 1)
                pool.tensor_tensor(pair[:, 1, :], T[4][:, :], pair[:, 0, :].bitcast(F32), ALU.subtract).then_inc(qk_lo, 1)
            pool.wait_ge(pv_done, len(ITEMS))
            squares(3, CHAIN["c"])
            ffn(1)


def _tables():
    ident = np.eye(P)
    i = np.arange(P)
    same = (i[:, None] // CHUNK) == (i[None, :] // CHUNK)
    forward = same & (i[:, None] <= i[None, :])
    backward = same & (i[:, None] >= i[None, :])
    rot = np.zeros((P, P))
    q = HD // 4
    for half in (0, HD // 2):
        for k in range(q):
            rot[half + q + k, half + k] = -1.0
            rot[half + k, half + q + k] = 1.0
    return np.concatenate([ident, forward, backward, rot], axis=1).astype(np.float32)


def _rope():
    half = HD // 2
    inv = (np.float32(ROPE_THETA) ** (-np.arange(0, half, 2, dtype=np.float32) / np.float32(half))).astype(np.float32)
    t = np.concatenate([np.arange(SEQ), np.arange(DEC)])
    out = []
    for fn in (np.cos, np.sin):
        rows = []
        for d in range(HD):
            pos = (t // GRID_W if d < half else t % GRID_W).astype(np.float32)
            rows.append(fn(pos * inv[d % (half // 2)]))
        out.append(np.stack(rows))
    return np.concatenate(out, axis=1).astype(np.float32)


def _dft():
    def cs(n):
        k = np.outer(np.arange(n), np.arange(n)) % n
        return np.cos(2 * np.pi * k / n), np.sin(2 * np.pi * k / n)

    out = np.zeros((6, P, SLOT))
    out[0, :, 0:2 * FW] = np.concatenate(cs(FW), axis=1)
    c, s = cs(SEQ)
    both = (np.concatenate([c, -s]) / np.sqrt(SEQ * FW)).reshape(8, P, SEQ)
    for j in range(4):
        out[1 + j] = np.concatenate([both[2 * j], both[2 * j + 1]], axis=1)
    c, s = cs(DEC)
    both = (np.concatenate([c, -s]) / np.sqrt(DEC * FW)).reshape(4, P, DEC)
    out[5] = np.concatenate(list(both), axis=1)
    return out.astype(np.float32)


def kernel(x_prompt, x_sample, ab_norm, ab_w_in, gla_up_f, gla_bias_f, gla_up_b, gla_bias_b, gla_out_norm, ab_w_out,
           c_norm, c_w_in, c_q_norm, c_k_norm, c_w_out, ffn_norm, ffn_w_gate, ffn_w_up, ffn_w_down):
    import concourse.bacc as bacc
    from concourse.bass_utils import run_bass_kernel_spmd

    def tiles(v):
        return np.asarray(v).reshape(-1, P).T

    eps = np.full((P, 1), EPS, np.float32)
    columns = np.concatenate([tiles(ab_norm[0]), tiles(ffn_norm[0]), tiles(c_norm[0]), tiles(ffn_norm[1]),
                              tiles(gla_out_norm[0]), tiles(c_q_norm[0]), tiles(c_k_norm[0]), tiles(gla_bias_f[0]),
                              tiles(gla_bias_b[0]), eps], axis=1)
    up_pad = np.zeros((2 * RANK, 4 * P), np.float32)
    up_pad[0:RANK, 0:2 * P] = gla_up_f[0]
    up_pad[RANK:, 2 * P:] = gla_up_b[0]
    arrays = {
        "in_x_prompt": np.asarray(x_prompt)[0], "in_x_sample": np.asarray(x_sample)[0],
        "in_ab_w_in": np.asarray(ab_w_in)[0], "in_ab_w_out": np.asarray(ab_w_out)[0],
        "in_c_w_in": np.asarray(c_w_in)[0], "in_c_w_out": np.asarray(c_w_out)[0],
        "in_w_gate": ffn_w_gate, "in_w_up": ffn_w_up, "in_w_down": ffn_w_down,
        "in_columns": columns, "in_up_pad": up_pad,
        "const_tables": _tables(), "const_rope": _rope(), "const_dft": _dft(),
    }
    arrays = {k: np.ascontiguousarray(v) for k, v in arrays.items()}
    nc = bacc.Bacc("TRN2", target_bir_lowering=False, num_devices=1)
    args = [nc.dram_tensor(k, v.shape, mybir.dt.from_np(v.dtype), kind="ExternalInput").ap() for k, v in arrays.items()]
    for name, n in (("out_prompt", SEQ), ("out_sample", DEC)):
        args.append(nc.dram_tensor(name, (n, D), F32, kind="ExternalOutput").ap())
    trunk_kernel(nc, *args)
    r = run_bass_kernel_spmd(nc, [arrays], core_ids=[0]).results[0]
    return r["out_prompt"][None], r["out_sample"][None]
```

```python
from contextlib import ExitStack

import numpy as np

import concourse.bass as bass
import concourse.mybir as mybir
from concourse.alu_op_type import AluOpType as ALU

ACT = mybir.ActivationFunctionType
F32 = mybir.dt.float32
F32R = mybir.dt.float32r
AX = mybir.AxisListType

P = 128
D = 1024
KT = D // P
SEQ, DEC = 512, 256
TOK = SEQ + DEC
TT = TOK // P
HALF = TOK // 2
HT = TT // 2
EPS = 1e-6
HEADS, DK, DV, RANK, CHUNK = 4, 64, 128, 16, 64
NCH = TOK // CHUNK
GATE_NORM = 16.0
FG, FW = 4, 128
AH, KVH, HD = 8, 2, 128
FFN = 2816
FT = FFN // P
CHUNKS = (8, 8, 6)
assert sum(CHUNKS) == FT
ROPE_THETA, GRID_W = 10000.0, 64
SLOT = KT * P

C_Q, C_K, C_V = 0, HEADS * DK, 2 * HEADS * DK
C_R = C_V + HEADS * DV
C_L = C_R + HEADS * DV
C_F = C_L + 2 * RANK
AB_UNITS = ([("l", 0, C_L)] + [("q", j, C_Q + P * j) for j in range(2)] + [("k", j, C_K + P * j) for j in range(2)]
            + [("v", j, C_V + P * j) for j in range(4)] + [("r", j, C_R + P * j) for j in range(4)]
            + [("f", j, C_F + P * j) for j in range(4)])
EARLY_KT = (AH - 3, AH - 2, AH - 2)
EARLY_UNITS = len(EARLY_KT)
C_UNITS = ([("k", j, (AH + j) * HD) for j in range(KVH)] + [("v", j, (AH + KVH + j) * HD) for j in range(KVH)]
           + [("q", j, j * HD) for j in range(AH)] + [("o", j, j * P) for j in range(EARLY_UNITS)])
QK = [(n, kind, j) for n, (kind, j, _) in enumerate(C_UNITS) if kind in "qk"]

SEGMENTS = [("load", KT), ("ab", len(AB_UNITS)), ("fnet", 6), ("ab_out", KT)]
for _l in range(2):
    if _l:
        SEGMENTS += [("c", len(C_UNITS)), ("c_out", KT)]
    for _c, _t in enumerate(CHUNKS):
        SEGMENTS += [(f"gate_up{_l}{_c}", 2 * _t), (f"down{_l}{_c}", KT)]
SEGMENTS += [("store", KT)]
BASE, _n = {}, 0
for _name, _k in SEGMENTS:
    BASE[_name] = _n
    _n += _k
N_WEIGHTS = BASE["store"] - KT
FNET_END = BASE["ab_out"]

CHAIN = {"ab": 0, "o": 1, "ffn0": 1 + HEADS, "c": 2 + HEADS, "qk": 3 + HEADS, "ffn1": 3 + HEADS + len(QK)}

COL = {"ab": 0, "ffn0": KT, "c": 2 * KT, "ffn1": 3 * KT, "out": 4 * KT, "qn": 4 * KT + 1, "kn": 4 * KT + 2,
       "bias": 4 * KT + 3, "eps": 4 * KT + 7}
N_COL = 4 * KT + 8

SEQS = ((0, SEQ // CHUNK), (SEQ // CHUNK, NCH))
STATES = ([(c, c + 1, c == a) for a, b in SEQS for c in range(a, b - 1)],
          [(c, c - 1, c == b - 1) for a, b in SEQS for c in range(b - 1, a, -1)])
NS = len(STATES[0])
ORDER = [[(m, 1 + max(i for i, (_, nxt, _) in enumerate(STATES[d]) if nxt // 2 == m)) for m in tiles]
         for d, tiles in enumerate(((0, 1, 2, 3, 4, 5), (3, 2, 1, 0, 5, 4)))]
assert TT == 6 and SEQ == 4 * P
FIRSTS = ({a for a, _ in SEQS}, {b - 1 for _, b in SEQS})

STEPS, ITEMS, LAST_STEP = [], [], []
for _h in range(AH):
    for _s, _len in ((0, SEQ), (SEQ, DEC)):
        for _q in range(_len // P):
            STEPS.append((len(ITEMS), _h, _s, _len, _q))
        ITEMS.append((_h, _s, _len))
        LAST_STEP.append(len(STEPS) - 1)
HEAD_STEPS = len(STEPS) // AH

PLAN = {}


def _put(slot, *event):
    PLAN.setdefault(slot, []).append(event)


UNIT_OF = [n for n, _, _ in QK]
LAG = 3
for _n, (_kind, _j, _) in enumerate(C_UNITS):
    if _kind == "v":
        _put(8 * (_n + 1) + 2, "values_turn", _j)
for _i, (_n, _kind, _j) in enumerate(QK):
    _at = 8 * (_n + 1)
    if _kind == "q":
        for _r in range(HEAD_STEPS):
            _t = _j * HEAD_STEPS + _r
            _put(_at + 11 + _r + LAG, "flip", _t)
            if _t in LAST_STEP:
                _put(_at + 13 + _r + LAG, "values", LAST_STEP.index(_t))
                _put(_at + 14 + _r + LAG, "result", LAST_STEP.index(_t))
for _i, (_n, _kind, _j) in enumerate(QK):
    _at = 8 * (_n + 1)
    if _kind == "q":
        for _r in range(HEAD_STEPS):
            _put(_at + 11 + _r, "scores", _j * HEAD_STEPS + _r)
            _put(_at + 12 + _r, "softmax", _j * HEAD_STEPS + _r)
    _put(_at + 2, "sums", _i)
    _put(_at + (4 if _kind == "q" else 5), "turn", _i, 0)
    _put(_at + (6 if _kind == "q" else 5), "turn", _i, 1)
    _put(_at + 8, "split", _i)
SLOTS = max(max(PLAN), 8 * len(C_UNITS)) + 1


def broadcasts(g):
    return g + 1 if g < CHAIN["qk"] + KVH else CHAIN["qk"] + KVH + (g == CHAIN["ffn1"])


def reads(n):
    return n + 1 - max(0, min(n + 1, FNET_END) - BASE["fnet"])


def trunk_kernel(nc, x_prompt, x_sample, ab_w_in, ab_w_out, c_w_in, c_w_out, w_gate, w_up, w_down,
                 columns, up_pad, tables, rope, dft, y_prompt, y_sample):
    ctx = ExitStack()
    with ctx:
        place = [-(-nc.sbuf_base // 32) * 32]

        def at(name, shape, offset, dt=F32):
            return nc.alloc_sbuf_tensor_at(name, [P, *shape], dt, offset=offset)

        def fresh(nbytes):
            place[0] += -(-nbytes // 32) * 32
            return place[0] - -(-nbytes // 32) * 32

        KB3 = TOK * 4
        x = at("x", [KT, TOK], fresh(KT * KB3))
        A = fresh(2 * KT * KB3)
        B = fresh(2 * KT * KB3)
        Dreg = fresh(32768)
        Treg = fresh(6 * KB3)
        raw = at("w_raw", [2, KT, P], fresh(2 * SLOT * 4))
        whi = at("w_hi", [2, KT, P], fresh(2 * SLOT * 4), F32R)
        wlo = at("w_lo", [2, KT, P], fresh(2 * SLOT * 4), F32R)
        rstd = at("rstd", [2, HALF], fresh(KB3))
        sumsq = at("sumsq", [TOK], fresh(KB3))
        tab = at("tab", [4, P], fresh(4 * P * 4))
        cols = at("cols", [N_COL], fresh(N_COL * 4))
        upw_at = fresh(4 * P * 4)
        upw = at("upw", [4, P], upw_at)
        ones = at("ones", [2], fresh(32))
        root = at("root", [2, TT], fresh(64))
        inv = at("inv", [2, TT], fresh(64))
        q_scale = at("q_scale", [AH, TT], fresh(AH * TT * 4))
        root_o = at("root_o", [HEADS * TT], fresh(HEADS * TT * 4))
        inv_o = at("inv_o", [HEADS * TT], fresh(HEADS * TT * 4))
        dec = at("dec", [4, NCH], fresh(4 * NCH * 4))
        negmax = at("negmax", [2, 2], fresh(32))
        expsum = at("expsum", [2, 2], fresh(32))
        assert place[0] <= nc.sbuf_usable_end, (place[0], nc.sbuf_usable_end)
        ident, mask, rot = tab[:, 0, :], tab[:, 1:3, :], tab[:, 3, :]

        pairA = at("pair_a", [KT, 2, TOK], A, F32R)
        pairB = at("pair_b", [KT, 2, TOK], B, F32R)
        T = [at(f"t{j}", [TOK], Treg + j * KB3) for j in range(6)]
        x_tok = at("x_tok", [TT, D], B)
        y_tok = at("y_tok", [TT, D], A)
        gcum = at("gcum", [4, TOK], B)
        q_ab = at("q_ab", [2, TOK], B + 4 * KB3)
        k_ab = at("k_ab", [2, TOK], B + 6 * KB3)
        v_ab = at("v_ab", [TT, HEADS * DV], B + 8 * KB3)
        r_ab = at("r_ab", [4, TOK], B + 12 * KB3)
        f_ab = at("f_ab", [FG, TOK], Dreg)
        o_ab = at("o_ab", [HEADS, TOK], Dreg + 4 * KB3)
        reset = at("reset", [2, TOK], Dreg + 8 * KB3)
        ranks = T[0]
        qpad = at("qpad", [HEADS, TOK], A)
        kintok = at("kintok", [2, TT, 2, P], A + 4 * KB3)
        state = at("state", [NCH, 2, P], A + 8 * KB3)
        kin = at("kin", [2, TOK], Dreg + 8 * KB3)
        probs_ab = T[0:3] + [at(f"masked{j}", [HEADS * P], A + 12 * KB3 + j * HEADS * P * 4) for j in range(3)]
        o_sq = at("o_sq", [3, HEADS, P], A + 14 * KB3)
        kv_sum = at("kv_sum", [2, P], upw_at)
        decayed = [T[3], T[5]]
        fpair = [at("fpair0", [2, TOK], Dreg + 8 * KB3, F32R), at("fpair1", [2, TOK], Treg, F32R)]
        wave = at("wave", [2, FG, TT, 2 * FW], A, F32R)
        kpair = at("kpair", [KVH, 2, TOK], Dreg, F32R)
        v_c = at("v_c", [TT, KVH * HD], Dreg + 4 * KB3)
        v_flat = [T[5], sumsq]
        ropes = at("ropes", [2, TOK], Dreg + 6 * KB3)
        probs = [T[5], sumsq, upw]
        probs = [probs[0][:, 0:SEQ], probs[1][:, 0:SEQ], probs[2][:, :, :].rearrange("p a b -> p (a b)")]
        probsT = [at("probs_t", [4, SEQ], Dreg + 8 * KB3),
                  at("sample_t", [11, TOK], Treg + 5 * KB3)[:, 0:11:10, SEQ:TOK]]

        unit_ps = ctx.enter_context(nc.psum_tensor("unit_ps", [P, 2, 2, 512], F32))
        misc_ps = ctx.enter_context(nc.psum_tensor("misc_ps", [P, 4, 512], F32))

        def ups(n):
            return unit_ps[:, n % 2, :, 0:HALF]

        def two(ap):
            return ap.rearrange("p (a b) -> p a b", a=2)

        def sem(name):
            return ctx.enter_context(nc.semaphore(name))

        x_landed = [sem(f"x_landed{j}") for j in range(2)]
        ident_landed, columns_landed, up_landed = sem("ident_landed"), sem("columns_landed"), sem("up_landed")
        rope_landed = sem("rope_landed")
        weights_landed = [sem(f"weights_landed{j}") for j in range(2)]
        hi_split, lo_split = sem("hi_split"), sem("lo_split")
        unit_done, unit_read = sem("unit_done"), sem("unit_read")
        h_hi, h_lo = sem("h_hi"), sem("h_lo")
        sq_ready, sq_summed, sum_zeroed = sem("sq_ready"), sem("sq_summed"), sem("sum_zeroed")
        colsum_done, root_done, inv_done = sem("colsum_done"), sem("root_done"), sem("inv_done")
        bc_done, bc_read = sem("bc_done"), sem("bc_read")
        const_ready = sem("const_ready")
        half_done, half_read, q_scaled = sem("half_done"), sem("half_read"), sem("q_scaled")
        reset_ready = sem("reset_ready")
        vT_done, vT_read = sem("vT_done"), sem("vT_read")
        z_done, z_read, log_ready, log_step = sem("z_done"), sem("z_read"), sem("log_ready"), sem("log_step")
        gate_ready, gate_summed = sem("gate_ready"), sem("gate_summed")
        r_silu = sem("r_silu")
        kintok_zeroed, qpad_zeroed = sem("kintok_zeroed"), sem("qpad_zeroed")
        exp_pos, exp_neg, decay_ready = sem("exp_pos"), sem("exp_neg"), sem("decay_ready")
        q_gated, k_gated = sem("q_gated"), sem("k_gated")
        kT_done, kT_read = sem("kT_done"), sem("kT_read")
        kv_done, kv_added, state_sum = sem("kv_done"), sem("kv_added"), sem("state_sum")
        att_done, att_masked = sem("att_done"), sem("att_masked")
        o_done, o_read = sem("o_done"), sem("o_read")
        osq_ready, o_gated = sem("osq_ready"), sem("o_gated")
        mixed_hi, mixed_lo = sem("mixed_hi"), sem("mixed_lo")
        f_hi, f_lo = sem("f_hi"), sem("f_lo")
        wave_done, wave_hi, wave_lo = sem("wave_done"), sem("wave_hi"), sem("wave_lo")
        y_done = sem("y_done")
        silu_done, prod_done, act_hi, act_lo = sem("silu_done"), sem("prod_done"), sem("act_hi"), sem("act_lo")
        qk_sq, qk_gain, rot_done, rot_read = sem("qk_sq"), sem("qk_gain"), sem("rot_done"), sem("rot_read")
        qk_cos, qk_sum, qk_hi, qk_lo = sem("qk_cos"), sem("qk_sum"), sem("qk_hi"), sem("qk_lo")
        s_done, s_max, s_neg, s_exp, s_inv, s_norm = (sem("s_done"), sem("s_max"), sem("s_neg"), sem("s_exp"),
                                                      sem("s_inv"), sem("s_norm"))
        pT_done, pT_read, pv_done, pv_hi, pv_lo = (sem("pT_done"), sem("pT_read"), sem("pv_done"), sem("pv_hi"),
                                                   sem("pv_lo"))
        y_stored = sem("y_stored")

        def flip_bank(j):
            return misc_ps[:, 2, :] if j % 2 == 0 else unit_ps[:, 1, 0, :]

        values_bank = unit_ps[:, 1, 1, :]

        def keys_banks(t):
            return misc_ps[:, 2 * t:2 * t + 2, :]

        def wave_product(eng, i):
            if i < FG * HT - 1:
                eng.wait_ge(wave_done, i + 1)
            else:
                eng.wait_ge(unit_done, BASE["fnet"] + 1)

        def sample_bank(g):
            return unit_ps[:, 0, g // 2, (g % 2) * DEC:(g % 2 + 1) * DEC]

        def token_product(eng, part, g):
            if part and g < 2:
                eng.wait_ge(y_done, FG - 1 + 2)
            elif not part and g < FG - 1:
                eng.wait_ge(y_done, g + 1)
            else:
                eng.wait_ge(unit_done, BASE["fnet"] + 5 + part)

        block = ctx.enter_context(nc.Block())

        @block.sync
        def _(sp):
            for half in range(2):
                features = slice(half * D // 2, (half + 1) * D // 2)
                for tiles, source in ((slice(0, SEQ // P), x_prompt), (slice(SEQ // P, TT), x_sample)):
                    sp.dma_start(x_tok[:, tiles, features],
                                 source[:, features].rearrange("(m p) d -> p m d", p=P)).then_inc(x_landed[half], 16)

            def weights(w, src, kt, slot=None):
                s = w % 2 if slot is None else slot
                if slot is not None or w >= 2:
                    sp.wait_ge(lo_split, w - 1)
                sp.dma_start(raw[:, s, 0:kt, :], src.rearrange("(k p) n -> p k n", p=P)).then_inc(weights_landed[s], 16)

            def columns_of(w0, mat, count, kt):
                with sp.Fori(0, count // 2) as i:
                    for s in range(2):
                        weights(w0 + s + 2 * i, mat[:, bass.ds((2 * i + s) * P, P)], kt, slot=(w0 + s) % 2)

            for n, (_, _, c) in enumerate(AB_UNITS):
                weights(n, ab_w_in[:, c:c + P], KT)
            for j in range(6):
                w = BASE["fnet"] - KT + j
                sp.wait_ge(lo_split, w - 1)
                sp.dma_start(raw[:, w % 2, :, :], dft[j].rearrange("p (k n) -> p k n", k=KT)).then_inc(
                    weights_landed[w % 2], 16)
            columns_of(BASE["ab_out"] - KT, ab_w_out, KT, KT)
            for layer in range(2):
                if layer:
                    for n, (kind, _, c) in enumerate(C_UNITS):
                        if kind == "o":
                            weights(BASE["c"] - KT + n, c_w_out[0:EARLY_KT[c // P] * P, c:c + P], EARLY_KT[c // P])
                        else:
                            weights(BASE["c"] - KT + n, c_w_in[:, c:c + P], KT)
                    for n in range(KT):
                        first = EARLY_KT[n] if n < EARLY_UNITS else 0
                        weights(BASE["c_out"] - KT + n, c_w_out[first * P:, n * P:(n + 1) * P], KT - first)
                first = 0
                for c, tiles in enumerate(CHUNKS):
                    w0 = BASE[f"gate_up{layer}{c}"] - KT
                    with sp.Fori(0, tiles) as i:
                        for s, mat in enumerate((w_gate, w_up)):
                            weights(w0 + s + 2 * i, mat[layer][:, bass.ds((first + i) * P, P)], KT, slot=(w0 + s) % 2)
                    columns_of(BASE[f"down{layer}{c}"] - KT, w_down[layer][first * P:(first + tiles) * P, :], KT, tiles)
                    first += tiles
            for n in range(KT):
                sp.wait_ge(unit_read, reads(BASE["store"] + n))
                sl = slice(n * P, (n + 1) * P)
                sp.dma_start(y_prompt[:, sl].rearrange("(m p) d -> p m d", p=P),
                             y_tok[:, 0:SEQ // P, sl]).then_inc(y_stored, 16)
                sp.dma_start(y_sample[:, sl].rearrange("(m p) d -> p m d", p=P),
                             y_tok[:, SEQ // P:, sl]).then_inc(y_stored, 16)
            sp.wait_ge(y_stored, 32 * KT)

        @block.tensor
        def _(pe):
            def product3(out, w_hi, w_lo, m_hi, m_lo, start, stop):
                pe.matmul(out, w_hi, m_hi, start=start, stop=False)
                pe.matmul(out, w_hi, m_lo, start=False, stop=False)
                return pe.matmul(out, w_lo, m_hi, start=False, stop=stop)

            def linear(n, slot, pair, kt, waits, middle=None, ready=None):
                pe.wait_ge(lo_split, n - KT + 1)
                pe.wait_ge(unit_read, waits[2])
                if not ready:
                    pe.wait_ge(waits[0], waits[1] - 1)
                for k in range(kt):
                    if k == kt - 1 and middle:
                        middle()
                    if ready or k == kt - 1:
                        pe.wait_ge(waits[0], ready[k] if ready else waits[1])
                    for h in range(2):
                        last = product3(unit_ps[:, slot, h, 0:HALF], whi[:, slot, k, :], wlo[:, slot, k, :],
                                        pair[:, k, 0, h * HALF:(h + 1) * HALF], pair[:, k, 1, h * HALF:(h + 1) * HALF],
                                        k == 0, k == kt - 1)
                last.then_inc(unit_done, 1)

            def column_sums(g, squares):
                for m in range(TT):
                    last = pe.matmul(misc_ps[:, 0, 2 * m:2 * m + 2], squares[:, m * P:(m + 1) * P], ones[:, :],
                                     start=True, stop=True)
                last.then_inc(colsum_done, 1)

            def broadcast(g):
                pe.wait_ge(inv_done, g + 1)
                if g:
                    pe.wait_ge(bc_read, broadcasts(g) - 1)
                for m in range(TT):
                    last = pe.matmul(misc_ps[:, 1 + m // HT, (m % HT) * P:(m % HT + 1) * P],
                                     inv[:, g % 2, m:m + 1].to_broadcast([P, P]), ident, start=True, stop=True)
                last.then_inc(bc_done, 1)

            def trunk_sums(g, r):
                pe.wait_ge(sq_summed, KT * (r + 1))
                column_sums(g, sumsq)

            pe.wait_ge(ident_landed, 16)
            pe.wait_ge(const_ready, 1)
            for n in range(KT):
                if n % (KT // 2) == 0:
                    pe.wait_ge(x_landed[n // (KT // 2)], 32)
                if n >= 2:
                    pe.wait_ge(unit_read, reads(n - 2))
                for m in range(TT):
                    last = pe.transpose(unit_ps[:, n % 2, m // HT, (m % HT) * P:(m % HT + 1) * P],
                                        x_tok[:, m, n * P:(n + 1) * P], ident)
                last.then_inc(unit_done, 1)

            def turn_keys(d, t):
                pe.wait_ge(k_gated, 2 * d + t + 1)
                if d == 0 and t == 0:
                    pe.wait_ge(vT_read, HEADS)
                elif d and t == 0:
                    pe.wait_ge(state_sum, NS)
                elif d:
                    pe.wait_ge(att_masked, TT)
                for m in range(TT):
                    last = pe.transpose(keys_banks(t)[:, m // HT, (m % HT) * P:(m % HT + 1) * P],
                                        kin[:, t, m * P:(m + 1) * P], ident)
                last.then_inc(kT_done, 1)

            for j, (kind, _, _) in enumerate(AB_UNITS):
                n = BASE["ab"] + j
                if j == 0:
                    linear(n, n % 2, pairA, KT, (h_lo, KT, reads(n - 2)),
                           lambda: trunk_sums(CHAIN["ab"], 0), range(1, KT + 1))
                else:
                    linear(n, n % 2, pairA, KT, (h_lo, KT, reads(n - 2)))
                if AB_UNITS[j - 1][0] == "v":
                    k = AB_UNITS[j - 1][1]
                    pe.wait_ge(unit_read, reads(n - 1))
                    if k == 0:
                        pe.wait_ge(z_read, 4)
                    elif k >= 2:
                        pe.wait_ge(vT_read, k - 1)
                    for m in range(TT):
                        last = pe.transpose(misc_ps[:, 2 * (k % 2) + m // HT, (m % HT) * P:(m % HT + 1) * P],
                                            T[1 + k % 2][:, m * P:(m + 1) * P], ident)
                    last.then_inc(vT_done, 1)
                if j == 0:
                    broadcast(CHAIN["ab"])
                if j in (2, 3):
                    pe.wait_ge(unit_read, reads(BASE["ab"]))
                    pe.wait_ge(up_landed, 16)
                    pe.wait_ge(bc_read, 1)
                    for t in range(2):
                        dt = 2 * (j - 2) + t
                        if dt >= 2:
                            pe.wait_ge(z_read, dt - 1)
                        for h in range(2):
                            last = pe.matmul(misc_ps[:, 2 * t + h, 0:HALF], upw[0:2 * RANK, dt, :],
                                             ranks[0:2 * RANK, h * HALF:(h + 1) * HALF], start=True, stop=True)
                        last.then_inc(z_done, 1)
                if j >= len(AB_UNITS) - 2:
                    turn_keys(0, j - len(AB_UNITS) + 2)

            def keys_values(d, i):
                c = STATES[d][i][0]
                if i >= 2:
                    pe.wait_ge(state_sum, NS * d + i - 1)
                for t in range(2):
                    for e in range(2):
                        last = pe.matmul(misc_ps[e * DK:(e + 1) * DK, i % 2, t * P:(t + 1) * P],
                                         kintok[:, t, c // 2, c % 2, e * DK:(e + 1) * DK],
                                         v_ab[:, c // 2, (2 * t + e) * DV:(2 * t + e + 1) * DV],
                                         start=True, stop=True)
                last.then_inc(kv_done, 1)

            def chunk_scores(d, r):
                m = ORDER[d][r][0]
                pe.wait_ge(q_gated, 2 * d + 2)
                pe.wait_ge(qpad_zeroed, 2)
                if r >= 2:
                    pe.wait_ge(att_masked, TT * d + r - 1)
                for h in range(HEADS):
                    last = pe.matmul(misc_ps[:, 2 + r % 2, h * P:(h + 1) * P], kin[:, h // 2, m * P:(m + 1) * P],
                                     qpad[:, h, m * P:(m + 1) * P], start=True, stop=True)
                last.then_inc(att_done, 1)

            def head_column_sums(r):
                m = ORDER[1][r][0]
                pe.wait_ge(osq_ready, r + 1)
                for h in range(HEADS):
                    at_column = 2 * (h * TT + m)
                    last = pe.matmul(unit_ps[:, 1, 0, at_column:at_column + 2], o_sq[:, r % 3, h, :], ones[:, :],
                                     start=True, stop=True)
                if r == TT - 1:
                    last.then_inc(colsum_done, HEADS)

            def tile_output(d, r):
                m, states = ORDER[d][r]
                pe.wait_ge(att_masked, TT * d + r + 1)
                pe.wait_ge(state_sum, NS * d + states)
                if d or r >= 2:
                    pe.wait_ge(o_read, TT * d + r - 1)
                else:
                    pe.wait_ge(unit_read, reads(BASE["fnet"] - 1))
                inter = [c for c in (2 * m, 2 * m + 1) if c not in FIRSTS[d]]
                for t in range(2):
                    for h in (2 * t, 2 * t + 1):
                        last = pe.matmul(unit_ps[:, 0, r % 2, h * P:(h + 1) * P], v_ab[:, m, h * DV:(h + 1) * DV],
                                         probs_ab[r][:, h * P:(h + 1) * P], start=h == 0, stop=h == HEADS - 1 and not inter)
                    for c in inter:
                        o = (c % 2) * CHUNK
                        out = unit_ps[:, 0, r % 2, :].rearrange("p (h i) -> p h i", h=HEADS)
                        last = pe.matmul(out[:, 2 * t:2 * t + 2, o:o + CHUNK], state[:, c, t, :],
                                         qpad[:, 2 * t:2 * t + 2, c * CHUNK:(c + 1) * CHUNK],
                                         start=False, stop=t == 1 and c == inter[-1])
                last.then_inc(o_done, 1)
                if d == 0 and r in (3, 5):
                    turn_keys(1, (r - 3) // 2)
                if d and r >= 2:
                    head_column_sums(r - 2)

            for d in range(2):
                pe.wait_ge(kT_read, 2 * d + 2)
                if d == 0:
                    pe.wait_ge(kintok_zeroed, 2)
                for i in range(NS):
                    keys_values(d, i)
                    if 0 <= i - 2 < TT:
                        chunk_scores(d, i - 2)
                    if i >= 3 and i % 2:
                        tile_output(d, (i - 3) // 2)
                for r in (TT - 2, TT - 1):
                    tile_output(d, r)
            for r in (TT - 2, TT - 1):
                head_column_sums(r)

            def broadcast_head(h):
                pe.wait_ge(inv_done, CHAIN["o"] + HEADS)
                if h >= 2:
                    pe.wait_ge(bc_read, CHAIN["o"] + h - 1)
                else:
                    pe.wait_ge(o_read, 2 * TT)
                for m in range(TT):
                    last = pe.matmul(unit_ps[:, h % 2, m // HT, (m % HT) * P:(m % HT + 1) * P],
                                     inv_o[:, h * TT + m:h * TT + m + 1].to_broadcast([P, P]), ident,
                                     start=True, stop=True)
                last.then_inc(bc_done, 1)

            n = BASE["fnet"]
            for i in range(FG * HT):
                g, b = i // HT, i % 4
                if i == 0:
                    pe.wait_ge(lo_split, n - KT + 1)
                pe.wait_ge(f_lo, g + 1)
                if i >= 4:
                    pe.wait_ge(wave_lo, i - 3)
                for m in (2 * (i % HT), 2 * (i % HT) + 1):
                    last = product3(misc_ps[:, b, (m % 2) * 2 * FW:(m % 2 + 1) * 2 * FW],
                                    fpair[g % 2][:, 0, m * P:(m + 1) * P], fpair[g % 2][:, 1, m * P:(m + 1) * P],
                                    whi[:, n % 2, 0:2, :], wlo[:, n % 2, 0:2, :], True, True)
                last.then_inc(unit_done if i == FG * HT - 1 else wave_done, 1)
            pe.wait_ge(wave_lo, FG * HT)
            for j in range(4):
                n = BASE["fnet"] + 1 + j
                pe.wait_ge(lo_split, n - KT + 1)
                for g in range(FG):
                    for kk in range(2):
                        k = 2 * j + kk
                        part, m = k // 4, k % 4
                        last = product3(misc_ps[:, g, :], wave[:, 0, g, m, part * FW:(part + 1) * FW],
                                        wave[:, 1, g, m, part * FW:(part + 1) * FW],
                                        whi[:, n % 2, 4 * kk:4 * kk + 4, :], wlo[:, n % 2, 4 * kk:4 * kk + 4, :],
                                        k == 0, k == 7)
                    if j == 3 and g < FG - 1:
                        last.then_inc(y_done, 1)
                last.then_inc(unit_done, 1)
                for h in ((0, 1), (2,), (3,), ())[j]:
                    broadcast_head(h)
            n = BASE["fnet"] + 5
            pe.wait_ge(lo_split, n - KT + 1)
            pe.wait_ge(bc_read, CHAIN["o"] + HEADS - 1)
            for g in range(FG):
                for k in range(4):
                    part, m = k // 2, SEQ // P + k % 2
                    last = product3(sample_bank(g), wave[:, 0, g, m, part * FW:(part + 1) * FW],
                                    wave[:, 1, g, m, part * FW:(part + 1) * FW],
                                    whi[:, n % 2, 2 * k:2 * k + 2, :], wlo[:, n % 2, 2 * k:2 * k + 2, :],
                                    k == 0, k == 3)
                if g < FG - 1:
                    last.then_inc(y_done, 1)
            last.then_inc(unit_done, 1)

            def out_projection(seg, pair, ready, count, kt, first=0):
                n0 = BASE[seg]
                with pe.Fori(first, KT // 2) as i:
                    for s in range(2):
                        linear(n0 + s + 2 * i, (n0 + s) % 2, pair, kt, (ready, count, reads(n0 + s - 2) + 2 * i))

            def ffn(layer, g, r, pair, acts):
                done = FT * layer
                for c, tiles in enumerate(CHUNKS):
                    n0 = BASE[f"gate_up{layer}{c}"]

                    def gate_up(i, first=False):
                        for s in range(2):
                            linear(n0 + s + 2 * i, (n0 + s) % 2, pair, KT,
                                   (h_lo, KT * (r + 1), reads(n0 + s - 2) + 2 * i),
                                   (lambda: trunk_sums(g, r)) if first and s == 0 else None)
                            if s == 0 and first:
                                broadcast(g)

                    gate_up(0, c == 0)
                    with pe.Fori(1, tiles) as i:
                        gate_up(i)
                    done += tiles
                    out_projection(f"down{layer}{c}", acts, act_lo, done, tiles)

            n = BASE["ab_out"]
            whole = HEADS + 2 * FG
            linear(n, n % 2, pairB, KT, (mixed_lo, whole, reads(n - 2)), None,
                   [*range(1, HEADS + 1), *range(HEADS + FG + 1, whole + 1)])
            linear(n + 1, (n + 1) % 2, pairB, KT, (mixed_lo, whole, reads(n - 1)))
            out_projection("ab_out", pairB, mixed_lo, whole, KT, 1)
            ffn(0, CHAIN["ffn0"], 1, pairA, pairB)

            def head_sums(i):
                pe.wait_ge(qk_sq, i + 1)
                bank = 3 if QK[i][1] == "q" else 0
                if i:
                    pe.wait_ge(rot_read, 2 * i)
                for m in range(TT):
                    last = pe.matmul(misc_ps[:, bank, 2 * m:2 * m + 2], T[1][:, m * P:(m + 1) * P], ones[:, :],
                                     start=True, stop=True)
                last.then_inc(colsum_done, 1)

            def turn(i, half):
                pe.wait_ge(qk_gain, i + 1)
                pe.wait_ge(root_done, CHAIN["qk"] + i + 1)
                if QK[i][1] == "q" and half:
                    pe.wait_ge(rot_read, 2 * i + 1)
                bank = 0 if QK[i][1] == "k" and half else 3
                pe.matmul(misc_ps[:, bank, 0:HALF], rot, T[2 + i % 2][:, half * HALF:(half + 1) * HALF],
                          start=True, stop=True).then_inc(rot_done, 1)

            def attention_scores(j):
                _, h, s0, ln, qt = STEPS[j]
                pe.wait_ge(qk_lo, KVH + h + 1)
                if j >= 2:
                    pe.wait_ge(s_exp, j - 1)
                q = slice(s0 + qt * P, s0 + (qt + 1) * P)
                kv = h // (AH // KVH)
                last = product3(misc_ps[:, j % 2, 0:ln], pairB[:, h, 0, q], pairB[:, h, 1, q],
                                kpair[:, kv, 0, s0:s0 + ln], kpair[:, kv, 1, s0:s0 + ln], True, True)
                last.then_inc(s_done, 1)

            def flip(j):
                ln = STEPS[j][3]
                pe.wait_ge(s_norm, j + 1)
                if j >= 2:
                    pe.wait_ge(pT_read, j - 1)
                elif j == 1:
                    pe.wait_ge(vT_read, HEADS + KVH)
                for m in range(ln // P):
                    last = pe.transpose(flip_bank(j)[:, m * P:(m + 1) * P], probs[j % 3][:, m * P:(m + 1) * P], ident)
                last.then_inc(pT_done, 1)

            def values(a):
                h, s0, ln = ITEMS[a]
                kv = h // (AH // KVH)
                pe.wait_ge(pT_read, LAST_STEP[a] + 1)
                if a:
                    pe.wait_ge(pv_lo, a)
                for m in range(ln // P):
                    last = pe.matmul(values_bank[:, 0:ln], v_c[:, s0 // P + m, kv * HD:(kv + 1) * HD],
                                     probsT[a % 2][:, m, 0:ln], start=m == 0, stop=m == ln // P - 1)
                last.then_inc(pv_done, 1)

            def between(slot):
                for what, i, *half in PLAN.get(slot, ()):
                    if what == "sums":
                        head_sums(i)
                    elif what == "turn":
                        if QK[i][1] == "k" and not half[0]:
                            broadcast(CHAIN["qk"] + i)
                        turn(i, *half)
                    elif what == "scores":
                        attention_scores(i)
                    elif what == "flip":
                        flip(i)
                    elif what == "values":
                        values(i)
                    elif what == "values_turn":
                        pe.wait_ge(unit_read, reads(BASE["c"] + slot // 8 - 1))
                        if i:
                            pe.wait_ge(vT_read, HEADS + i)
                        for m in range(TT):
                            last = pe.transpose(unit_ps[:, 1, m // HT, (m % HT) * P:(m % HT + 1) * P],
                                                v_flat[i][:, m * P:(m + 1) * P], ident)
                        last.then_inc(vT_done, 1)

            pe.wait_ge(unit_read, reads(BASE["c"] - 1))
            for j, (kind, _, _) in enumerate(C_UNITS):
                n = BASE["c"] + j
                pe.wait_ge(lo_split, n - KT + 1)
                for slot in range(8):
                    half = slot // 4
                    if j and slot == 0:
                        pe.wait_ge(half_read, j)
                    if j and slot == 4:
                        pe.wait_ge(unit_read, reads(n - 1))
                    kt = EARLY_KT[C_UNITS[j][1]] if kind == "o" else KT
                    moving = pairB if kind == "o" else pairA
                    for k in range(kt * (slot % 4) // 4, kt * (slot % 4 + 1) // 4):
                        if kind == "o":
                            pe.wait_ge(pv_lo, 2 * (k + 1))
                        if j == 0:
                            pe.wait_ge(h_lo, 2 * KT + k + 1)
                        tokens = slice(half * HALF, (half + 1) * HALF)
                        last = product3(unit_ps[:, 0, half, 0:HALF], whi[:, n % 2, k, :], wlo[:, n % 2, k, :],
                                        moving[:, k, 0, tokens], moving[:, k, 1, tokens], k == 0, k == kt - 1)
                    if slot % 4 == 3:
                        last.then_inc(unit_done if half else half_done, 1)
                    if j == 0 and slot == 4:
                        trunk_sums(CHAIN["c"], 2)
                    if j == 0 and slot == 5:
                        broadcast(CHAIN["c"])
                    between(8 * j + slot)
            for slot in range(8 * len(C_UNITS), SLOTS):
                between(slot)
            pe.wait_ge(pv_lo, len(ITEMS))
            for j in range(KT):
                n = BASE["c_out"] + j
                first = EARLY_KT[j] if j < EARLY_UNITS else 0
                linear(n, n % 2, pairB[:, first:, :, :], KT - first, (pv_lo, len(ITEMS), reads(n - 2 + (j == 0))))
            ffn(1, CHAIN["ffn1"], 3, pairA, pairB)

            for f in range(KT):
                n = BASE["store"] + f
                pe.wait_ge(unit_read, max(reads(n - 2), reads(BASE["store"] - KT + f)))
                for m in range(TT):
                    last = pe.transpose(unit_ps[:, n % 2, m // HT, (m % HT) * P:(m % HT + 1) * P],
                                        x[:, f, m * P:(m + 1) * P], ident)
                last.then_inc(unit_done, 1)

        @block.scalar
        def _(act):
            act.dma_start(tab[:, :, :], tables.rearrange("p (a b) -> p a b", a=4)).then_inc(ident_landed, 16)
            act.dma_start(cols[:, :], columns).then_inc(columns_landed, 16)
            act.dma_start(upw[0:2 * RANK, :, :], up_pad.rearrange("p (a b) -> p a b", a=4)).then_inc(up_landed, 16)

            def split_hi(w, slot=None, turn=None):
                s = w % 2 if slot is None else slot
                act.wait_ge(weights_landed[s], 16 * ((w // 2 if turn is None else turn) + 1))
                if slot is not None or w >= 2:
                    act.wait_ge(unit_done, w - 2 + KT + 1)
                act.activation(whi[:, s, :, :], raw[:, s, :, :], ACT.Copy).then_inc(hi_split, 1)

            def ahead(n):
                if n - KT + 2 < N_WEIGHTS:
                    split_hi(n - KT + 2)

            def ahead_loop(n0, s, i):
                w = n0 - KT + 2 + s
                split_hi(w + 2 * i, slot=w % 2, turn=w // 2 + i)

            def finish(f, n_read, r, gain, pair, tile, odd):
                if not isinstance(f, int) or f >= 2:
                    act.wait_ge(sq_summed, f - 1)
                act.wait_ge(unit_read, n_read)
                act.activation(pair[:, tile, 0, :], x[:, tile, :], ACT.Copy,
                               scale=cols[:, bass.ds(COL[gain] + tile, 1)] if not isinstance(tile, int)
                               else cols[:, COL[gain] + tile:COL[gain] + tile + 1]).then_inc(h_hi, 1)
                act.activation(T[2 + odd][:, :], x[:, tile, :], ACT.Square).then_inc(sq_ready, 1)

            def root_of(g, width):
                act.wait_ge(colsum_done, g + 1)
                act.activation(root[:, g % 2, :], misc_ps[:, 0, 0:2 * TT:2], ACT.Sqrt, scale=1.0 / width,
                               bias=cols[:, COL["eps"]:COL["eps"] + 1]).then_inc(root_done, 1)

            def values_turned(turned, ps, out):
                act.wait_ge(vT_done, turned)
                act.activation(out.rearrange("p (a m) e -> p a m e", a=2), ps.rearrange("p a (m e) -> p a m e", m=HT),
                               ACT.Copy).then_inc(vT_read, 1)

            def decays(dt):
                d, t = divmod(dt, 2)
                act.wait_ge(gate_summed, 4)
                if d:
                    act.wait_ge(q_gated, 2)
                act.activation(decayed[t][:, :], gcum[:, dt, :], ACT.Exp, scale=1.0 / GATE_NORM).then_inc(exp_pos, 1)
                if dt:
                    act.wait_ge(k_gated, dt)
                act.activation(T[4][:, :], gcum[:, dt, :], ACT.Exp, scale=-1.0 / GATE_NORM).then_inc(exp_neg, 1)
                end = slice(CHUNK - 1, TOK, CHUNK) if d == 0 else slice(0, TOK, CHUNK)
                act.activation(dec[:, dt, :], gcum[:, dt, end], ACT.Exp, scale=1.0 / GATE_NORM).then_inc(decay_ready, 1)

            def keys_turned(d, t):
                act.wait_ge(kT_done, 2 * d + t + 1)
                for b in range(2):
                    for e in range(2):
                        rows = slice(e * CHUNK, (e + 1) * CHUNK)
                        last = act.activation(kintok[rows, t, b * HT:(b + 1) * HT, e, :],
                                              keys_banks(t)[rows, b, 0:HALF].rearrange("p (m k) -> p m k", m=HT), ACT.Copy)
                last.then_inc(kT_read, 1)

            act.wait_ge(columns_landed, 16)
            for f in range(KT):
                finish(f, reads(f), 0, "ab", pairA, f, f % 2)
                if f in (2, 5):
                    split_hi(f // 3)
            root_of(CHAIN["ab"], D)
            for j, (kind, k, _) in enumerate(AB_UNITS):
                n = BASE["ab"] + j
                if j < len(AB_UNITS) - 1:
                    ahead(n)
                if AB_UNITS[j - 1][0] == "v":
                    k_last = AB_UNITS[j - 1][1]
                    values_turned(k_last + 1, misc_ps[:, 2 * (k_last % 2):2 * (k_last % 2) + 2, 0:HALF],
                                  v_ab[:, :, k_last * DV:(k_last + 1) * DV])
                if j in (2, 4):
                    for dt in (j - 2, j - 1):
                        t = T[3 + dt % 2]
                        act.wait_ge(z_read, dt + 1)
                        if dt >= 2:
                            act.wait_ge(gate_ready, dt - 1)
                        act.activation(t[:, :], gcum[:, dt, :], ACT.Abs).then_inc(log_step, 1)
                        act.wait_ge(log_step, 2 * dt + 1)
                        act.activation(t[:, :], t[:, :], ACT.Exp, scale=-1.0).then_inc(log_step, 1)
                        act.wait_ge(log_step, 2 * dt + 2)
                        act.activation(t[:, :], t[:, :], ACT.Ln, bias=1.0).then_inc(log_ready, 1)
                if j in (len(AB_UNITS) - 4, len(AB_UNITS) - 3):
                    decays(j - len(AB_UNITS) + 4)
                if kind == "r":
                    act.wait_ge(unit_read, reads(n))
                    act.activation(r_ab[:, k, :], r_ab[:, k, :], ACT.Silu).then_inc(r_silu, 1)

            def group_hi(g):
                if g >= 2:
                    act.wait_ge(wave_done, HT * (g - 1))
                act.activation(fpair[g % 2][:, 0, :], f_ab[:, g, :], ACT.Copy).then_inc(f_hi, 1)

            act.wait_ge(unit_done, BASE["fnet"])
            for t in range(2):
                keys_turned(0, t)
            ahead(BASE["fnet"] - 1)
            decays(2)
            for m in range(TT):
                act.wait_ge(o_done, m + 1)
                act.activation(o_ab[:, :, m * P:(m + 1) * P], unit_ps[:, 0, m % 2, :].rearrange("p (h i) -> p h i", h=HEADS),
                               ACT.Copy).then_inc(o_read, 1)
                if m == 1:
                    decays(3)
                elif m >= 4:
                    keys_turned(1, m - 4)
            for r, (m, _) in enumerate(ORDER[1]):
                if r == 2:
                    act.wait_ge(att_done, 2 * TT)
                    group_hi(0)
                elif r == 3:
                    act.wait_ge(o_done, TT + 2)
                    group_hi(1)
                act.wait_ge(o_read, TT + r + 1)
                act.activation(o_sq[:, r % 3, :, :], o_ab[:, :, m * P:(m + 1) * P], ACT.Square).then_inc(osq_ready, 1)
            act.wait_ge(colsum_done, CHAIN["o"] + HEADS)
            act.activation(root_o[:, :], unit_ps[:, 1, 0, 0:2 * HEADS * TT:2], ACT.Sqrt, scale=1.0 / DV,
                           bias=cols[:, COL["eps"]:COL["eps"] + 1]).then_inc(root_done, HEADS)

            for i in range(FG * HT):
                g, m = i // HT, 2 * (i % HT)
                wave_product(act, i)
                act.activation(wave[:, 0, g, m:m + 2, :], misc_ps[:, i % 4, :].rearrange("p (m n) -> p m n", m=2),
                               ACT.Copy).then_inc(wave_hi, 1)
                if i % HT == HT - 1 and g + 2 < FG:
                    group_hi(g + 2)
            for j in range(5):
                ahead(BASE["fnet"] + j)
                for h in ((), (0, 1), (2,), (3,), ())[j]:
                    act.wait_ge(bc_read, CHAIN["o"] + h + 1)
                    act.activation(pairB[:, h, 0, :], T[3 + h % 2][:, :], ACT.Copy).then_inc(mixed_hi, 1)
            for part, (s0, ln) in enumerate(((0, SEQ), (SEQ, DEC))):
                if part:
                    ahead(BASE["fnet"] + 5)
                for g in range(FG):
                    token_product(act, part, g)
                    act.activation(pairB[:, HEADS + g, 0, s0:s0 + ln], sample_bank(g) if part else misc_ps[:, g, :],
                                   ACT.Copy).then_inc(mixed_hi, 1)

            def out_projection(seg, r=None, gain=None, pair=None):
                n0 = BASE[seg]
                if seg == "down12":
                    for s in range(KT - 2):
                        ahead(n0 + s)
                    return
                with act.Fori(0, KT // 2) as i:
                    for s in range(2):
                        ahead_loop(n0, s, i)
                        if r is not None:
                            finish(KT * r + s + 2 * i, reads(n0 + s) + 2 * i, r, gain, pair, s + 2 * i, s)

            def ffn(layer, g, acts, nxt):
                root_of(g, D)
                done = FT * layer
                for c, tiles in enumerate(CHUNKS):
                    n0 = BASE[f"gate_up{layer}{c}"]
                    with act.Fori(0, tiles) as i:
                        ahead_loop(n0, 0, i)
                        act.wait_ge(unit_read, reads(n0) + 2 * i)
                        act.activation(T[0][:, :], T[0][:, :], ACT.Silu).then_inc(silu_done, 1)
                        ahead_loop(n0, 1, i)
                        act.wait_ge(prod_done, done + 1 + i)
                        act.activation(acts[:, i, 0, :], T[1][:, :], ACT.Copy).then_inc(act_hi, 1)
                    done += tiles
                    out_projection(f"down{layer}{c}", *(nxt if c == 2 and nxt else ()))

            out_projection("ab_out", 1, "ffn0", pairA)
            ffn(0, CHAIN["ffn0"], pairB, (2, "c", pairA))

            def head_evacuate(i, n):
                if i:
                    act.wait_ge(qk_sum, i)
                act.activation(T[1][:, :], T[0][:, :], ACT.Square).then_inc(qk_sq, 1)
                if i >= 2:
                    act.wait_ge(rot_done, 2 * (i - 1))
                    act.wait_ge(qk_cos, i - 1)
                col = COL["qn" if QK[i][1] == "q" else "kn"]
                act.activation(T[2 + i % 2][:, :], T[0][:, :], ACT.Copy, scale=cols[:, col:col + 1]).then_inc(qk_gain, 1)

            def head_root(i):
                g = CHAIN["qk"] + i
                bank = 3 if QK[i][1] == "q" else 0
                act.wait_ge(colsum_done, g + 1)
                act.wait_ge(inv_done, g - 1)
                act.activation(root[:, g % 2, :], misc_ps[:, bank, 0:2 * TT:2], ACT.Sqrt, scale=1.0 / HD,
                               bias=cols[:, COL["eps"]:COL["eps"] + 1]).then_inc(root_done, 1)

            def head_hi(i):
                if QK[i][1] == "k":
                    act.wait_ge(bc_read, broadcasts(CHAIN["qk"] + i))
                else:
                    act.wait_ge(qk_sum, i + 1)
                pair = kpair[:, QK[i][2]] if QK[i][1] == "k" else pairB[:, QK[i][2]]
                act.activation(pair[:, 0, :], T[4][:, :], ACT.Copy).then_inc(qk_hi, 1)

            def exponentials(j):
                _, h, s0, ln, qt = STEPS[j]
                act.wait_ge(s_neg, j + 1)
                if j >= 3:
                    act.wait_ge(pT_done, j - 2)
                act.activation(probs[j % 3][:, 0:ln], misc_ps[:, j % 2, 0:ln], ACT.Exp,
                               scale=q_scale[:, h, s0 // P + qt:s0 // P + qt + 1], bias=negmax[:, j % 2, 1:2],
                               accum_out=expsum[:, j % 2, 0:1]).then_inc(s_exp, 1)

            def flipped(j):
                a, _, _, ln, qt = STEPS[j]
                act.wait_ge(pT_done, j + 1)
                if a >= 2:
                    act.wait_ge(pv_done, a - 1)
                act.activation(probsT[a % 2][:, 0:ln // P, qt * P:(qt + 1) * P],
                               flip_bank(j)[:, 0:ln].rearrange("p (m q) -> p m q", q=P), ACT.Copy).then_inc(pT_read, 1)

            def result_hi(a):
                h, s0, ln = ITEMS[a]
                act.wait_ge(pv_done, a + 1)
                act.activation(pairB[:, h, 0, s0:s0 + ln], values_bank[:, 0:ln], ACT.Copy).then_inc(pv_hi, 1)

            root_of(CHAIN["c"], D)
            for slot in range(SLOTS):
                j = slot // 8 - 1
                for what, i, *half in PLAN.get(slot, ()):
                    if what == "flip":
                        flipped(i)
                if slot % 8 == 0 and j in UNIT_OF:
                    act.wait_ge(unit_read, reads(BASE["c"] + j))
                    head_evacuate(UNIT_OF.index(j), BASE["c"] + j)
                for what, i, *half in PLAN.get(slot, ()):
                    if what == "sums":
                        head_root(i)
                    elif what == "split":
                        head_hi(i)
                    elif what == "scores":
                        exponentials(i)
                    elif what == "values":
                        result_hi(i)
                    elif what == "values_turn":
                        values_turned(HEADS + i + 1, unit_ps[:, 1, :, 0:HALF], v_c[:, :, i * HD:(i + 1) * HD])
                if slot % 8 == 0 and 0 <= j < len(C_UNITS):
                    ahead(BASE["c"] + j)
            out_projection("c_out", 3, "ffn1", pairA)
            ffn(1, CHAIN["ffn1"], pairB, None)

        @block.vector
        def _(dve):
            def split_lo(w, slot=None):
                s = w % 2 if slot is None else slot
                dve.wait_ge(hi_split, w + 1)
                dve.tensor_tensor(wlo[:, s, :, :], raw[:, s, :, :], whi[:, s, :, :].bitcast(F32), ALU.subtract).then_inc(
                    lo_split, 1)

            def ahead(n):
                if n - KT + 2 < N_WEIGHTS:
                    split_lo(n - KT + 2)

            def ahead_loop(n0, s, i):
                w = n0 - KT + 2 + s
                split_lo(w + 2 * i, slot=w % 2)

            def gain_lo(f, gain, pair, tile):
                dve.wait_ge(h_hi, f + 1)
                col = (cols[:, COL[gain] + tile:COL[gain] + tile + 1] if isinstance(tile, int)
                       else cols[:, bass.ds(COL[gain] + tile, 1)])
                dve.scalar_tensor_tensor(pair[:, tile, 1, :], x[:, tile, :], col, pair[:, tile, 0, :].bitcast(F32),
                                         ALU.mult, ALU.subtract).then_inc(h_lo, 1)

            def inverse(g):
                dve.wait_ge(root_done, g + 1)
                if g >= 2:
                    dve.wait_ge(bc_done, broadcasts(g - 2))
                dve.reciprocal(inv[:, g % 2, :], root[:, g % 2, :]).then_inc(inv_done, 1)

            def trunk_norm(g):
                inverse(g)
                dve.wait_ge(bc_done, broadcasts(g))
                dve.tensor_copy(rstd[:, :, :], misc_ps[:, 1:3, 0:HALF]).then_inc(bc_read, 1)
                dve.wait_ge(bc_read, broadcasts(g))

            dve.memset(ones[:, :], 1.0).then_inc(const_ready, 1)
            dve.memset(reset[:, :, :], 1.0).then_inc(reset_ready, 1)
            dve.wait_ge(reset_ready, 1)
            dve.memset(reset[:, 0, 0:TOK:CHUNK], 0.0).then_inc(reset_ready, 1)
            dve.memset(reset[:, 1, CHUNK - 1:TOK:CHUNK], 0.0).then_inc(reset_ready, 1)
            dve.wait_ge(columns_landed, 16)
            dve.wait_ge(ident_landed, 16)
            for f in range(KT):
                dve.wait_ge(unit_done, f + 1)
                dve.tensor_copy(two(x[:, f, :]), ups(f)).then_inc(unit_read, 1)
                if f:
                    gain_lo(f - 1, "ab", pairA, f - 1)
                if f in (3, 6):
                    split_lo(f // 3 - 1)
            gain_lo(KT - 1, "ab", pairA, KT - 1)

            trunk_norm(CHAIN["ab"])
            dve.wait_ge(reset_ready, 3)
            for j, (kind, k, _) in enumerate(AB_UNITS):
                n = BASE["ab"] + j
                dve.wait_ge(unit_done, n + 1)
                if kind == "l":
                    dve.tensor_tensor(two(ranks[0:2 * RANK, :]), ups(n)[0:2 * RANK], rstd[0:2 * RANK], ALU.mult).then_inc(unit_read, 1)
                elif kind == "q":
                    dve.scalar_tensor_tensor(two(q_ab[:, k, :]), ups(n), DK ** -0.5, rstd[:, :, :], ALU.mult,
                                             ALU.mult).then_inc(unit_read, 1)
                elif kind == "v":
                    if k >= 2:
                        dve.wait_ge(vT_done, k - 1)
                    dve.tensor_tensor(two(T[1 + k % 2][:, :]), ups(n), rstd[:, :, :], ALU.mult).then_inc(unit_read, 1)
                else:
                    out = {"k": k_ab, "r": r_ab, "f": f_ab}[kind]
                    dve.tensor_tensor(two(out[:, k, :]), ups(n), rstd[:, :, :], ALU.mult).then_inc(unit_read, 1)
                if j < len(AB_UNITS) - 1:
                    ahead(n)
                if j in (2, 3):
                    d = j - 2
                    for dt in (2 * d, 2 * d + 1):
                        dve.wait_ge(z_done, dt + 1)
                        bank = 2 * (dt % 2)
                        dve.tensor_scalar(two(gcum[:, dt, :]), misc_ps[:, bank:bank + 2, 0:HALF],
                                          cols[:, COL["bias"] + dt:COL["bias"] + dt + 1], None, ALU.add).then_inc(z_read, 1)
                if j in (3, 5):
                    d = (j - 3) // 2
                    for dt in (2 * d, 2 * d + 1):
                        dve.wait_ge(log_ready, dt + 1)
                        if dt:
                            dve.wait_ge(gate_summed, dt)
                        dve.scalar_tensor_tensor(T[5][:, :], gcum[:, dt, :], 0.0, T[3 + dt % 2][:, :], ALU.min,
                                                 ALU.subtract).then_inc(gate_ready, 1)
                        dve.wait_ge(gate_ready, dt + 1)
                        step = 1 if d == 0 else -1
                        dve.tensor_tensor_scan(gcum[:, dt, ::step], reset[:, d, ::step], T[5][:, ::step], 0.0, ALU.mult,
                                               ALU.add).then_inc(gate_summed, 1)

            def queries(d, t, tokens, last_part):
                dve.wait_ge(exp_pos, 2 * d + t + 1)
                for e in range(2):
                    rows = slice(e * DK, (e + 1) * DK)
                    last = dve.tensor_tensor(qpad[rows, 2 * t + e, tokens], q_ab[rows, t, tokens],
                                             decayed[t][rows, tokens], ALU.mult)
                if last_part:
                    last.then_inc(q_gated, 1)

            def next_state(d, i):
                c, nxt, first = STATES[d][i]
                dve.wait_ge(kv_done, NS * d + i + 1)
                kv = misc_ps[:, i % 2, 0:2 * P].rearrange("p (t e) -> p t e", t=2)
                decay = dec[:, 2 * d:2 * d + 2, c].unsqueeze(2).to_broadcast([P, 2, P])
                if not first:
                    dve.wait_ge(state_sum, NS * d + i)
                    dve.tensor_tensor(kv_sum[:, :, :], kv, state[:, c, :, :], ALU.add).then_inc(kv_added, 1)
                    dve.wait_ge(kv_added, sum(not f for _, _, f in (STATES[0] + STATES[1])[0:NS * d + i + 1]))
                    kv = kv_sum[:, :, :]
                dve.tensor_tensor(state[:, nxt, :, :], kv, decay, ALU.mult).then_inc(state_sum, 1)

            def masked(d, r):
                dve.wait_ge(att_done, TT * d + r + 1)
                dve.tensor_tensor(probs_ab[r][:, 0:HEADS * P].rearrange("p (h i) -> p h i", h=HEADS),
                                  misc_ps[:, 2 + r % 2, :].rearrange("p (h i) -> p h i", h=HEADS),
                                  mask[:, d, :].unsqueeze(1).to_broadcast([P, HEADS, P]), ALU.mult).then_inc(att_masked, 1)

            def both_directions(r):
                m = ORDER[1][r][0]
                o = o_ab[:, :, m * P:(m + 1) * P]
                dve.wait_ge(o_done, TT + r + 1)
                dve.wait_ge(o_read, TT)
                dve.tensor_tensor(o, unit_ps[:, 0, r % 2, :].rearrange("p (h i) -> p h i", h=HEADS), o,
                                  ALU.add).then_inc(o_read, 1)
                if r:
                    gate_output(r - 1)

            def gate_output(r):
                m = ORDER[1][r][0]
                o = o_ab[:, :, m * P:(m + 1) * P]
                dve.wait_ge(osq_ready, r + 1)
                dve.scalar_tensor_tensor(o, o, cols[:, COL["out"]:COL["out"] + 1], r_ab[:, :, m * P:(m + 1) * P],
                                         ALU.mult, ALU.mult).then_inc(o_gated, 1)

            def group_lo(g):
                dve.wait_ge(f_hi, g + 1)
                dve.tensor_tensor(fpair[g % 2][:, 1, :], f_ab[:, g, :], fpair[g % 2][:, 0, :].bitcast(F32),
                                  ALU.subtract).then_inc(f_lo, 1)

            for d in range(2):
                if d:
                    dve.wait_ge(o_done, SEQ // P)
                    for t in range(2):
                        queries(1, t, slice(0, SEQ), False)
                    dve.wait_ge(o_done, TT)
                    for t in range(2):
                        queries(1, t, slice(SEQ, TOK), True)
                    dve.wait_ge(r_silu, 4)
                dve.wait_ge(decay_ready, 2 * d + 2)
                for i in range(NS):
                    if d == 0 and i == 0:
                        for t in range(2):
                            queries(0, t, slice(0, TOK), True)
                    next_state(d, i)
                    if d == 0 and i == NS - 1:
                        ahead(BASE["fnet"] - 1)
                    if 0 <= i - 2 < TT:
                        masked(d, i - 2)
                    if d and i >= 5 and i % 2:
                        both_directions((i - 5) // 2)
            for r in (3, 4, 5):
                both_directions(r)
                if r >= 4:
                    group_lo(r - 4)
            gate_output(TT - 1)
            dve.wait_ge(root_done, CHAIN["o"] + HEADS)
            dve.reciprocal(inv_o[:, :], root_o[:, :]).then_inc(inv_done, HEADS)

            def head_out(h):
                t = T[3 + h % 2]
                dve.wait_ge(bc_done, CHAIN["o"] + h + 1)
                dve.tensor_tensor(two(t[:, :]), two(o_ab[:, h, :]), unit_ps[:, h % 2, :, 0:HALF],
                                  ALU.mult).then_inc(bc_read, 1)
                dve.wait_ge(mixed_hi, h + 1)
                dve.tensor_tensor(pairB[:, h, 1, :], t[:, :], pairB[:, h, 0, :].bitcast(F32),
                                  ALU.subtract).then_inc(mixed_lo, 1)

            dve.wait_ge(o_gated, TT)
            for i in range(FG * HT):
                g, m = i // HT, 2 * (i % HT)
                dve.wait_ge(wave_hi, i + 1)
                dve.tensor_tensor(wave[:, 1, g, m:m + 2, :], misc_ps[:, i % 4, :].rearrange("p (m n) -> p m n", m=2),
                                  wave[:, 0, g, m:m + 2, :].bitcast(F32), ALU.subtract).then_inc(wave_lo, 1)
                if i % HT == HT - 1 and g + 2 < FG:
                    group_lo(g + 2)
            for j in range(5):
                ahead(BASE["fnet"] + j)
                for h in ((), (0, 1), (2,), (3,), ())[j]:
                    head_out(h)
            for part, (s0, ln) in enumerate(((0, SEQ), (SEQ, DEC))):
                if part:
                    ahead(BASE["fnet"] + 5)
                for g in range(FG):
                    dve.wait_ge(mixed_hi, HEADS + FG * part + (g | part) + 1)
                    dve.tensor_tensor(pairB[:, HEADS + g, 1, s0:s0 + ln], sample_bank(g) if part else misc_ps[:, g, :],
                                      pairB[:, HEADS + g, 0, s0:s0 + ln].bitcast(F32), ALU.subtract).then_inc(mixed_lo, 1)

            def out_projection(seg, r=None, gain=None, pair=None):
                n0 = BASE[seg]
                dve.wait_ge(unit_read, reads(n0 - 1))

                def add(n, slot, tile):
                    dve.wait_ge(unit_done, n + 1)
                    dve.tensor_tensor(two(x[:, tile, :]), unit_ps[:, slot, :, 0:HALF], two(x[:, tile, :]),
                                      ALU.add).then_inc(unit_read, 1)

                if seg == "down12":
                    for s in range(KT):
                        add(n0 + s, (n0 + s) % 2, s)
                        ahead(n0 + s)
                    return
                with dve.Fori(0, KT // 2) as i:
                    for s in range(2):
                        add(n0 + s + 2 * i, (n0 + s) % 2, s + 2 * i)
                        ahead_loop(n0, s, i)
                        if r is not None:
                            gain_lo(KT * r + s + 2 * i, gain, pair, s + 2 * i)

            def ffn(layer, g, nxt):
                trunk_norm(g)
                done = FT * layer
                for c, tiles in enumerate(CHUNKS):
                    n0 = BASE[f"gate_up{layer}{c}"]

                    def gate_up(i, earlier=True):
                        dve.wait_ge(unit_done, n0 + 1 + 2 * i)
                        if earlier:
                            dve.wait_ge(prod_done, done + i)
                        dve.tensor_tensor(two(T[0][:, :]), ups(n0), rstd[:, :, :], ALU.mult).then_inc(unit_read, 1)
                        ahead_loop(n0, 0, i)
                        dve.wait_ge(unit_done, n0 + 2 + 2 * i)
                        if earlier:
                            dve.wait_ge(act_lo, done + i)
                        dve.tensor_tensor(two(T[1][:, :]), ups(n0 + 1), rstd[:, :, :], ALU.mult).then_inc(unit_read, 1)
                        ahead_loop(n0, 1, i)

                    gate_up(0, done > 0)
                    with dve.Fori(1, tiles) as i:
                        gate_up(i)
                    done += tiles
                    out_projection(f"down{layer}{c}", *(nxt if c == 2 and nxt else ()))

            out_projection("ab_out", 1, "ffn0", pairA)
            ffn(0, CHAIN["ffn0"], (2, "c", pairA))

            def evacuate_half(j, half):
                n, (kind, k, _) = BASE["c"] + j, C_UNITS[j]
                ps = unit_ps[:, 0, half, 0:HALF]
                dve.wait_ge(unit_done if half else half_done, n + 1 if half else j + 1)
                if kind == "v":
                    done = dve.tensor_tensor(v_flat[k][:, half * HALF:(half + 1) * HALF], ps, rstd[:, half, :], ALU.mult)
                elif kind == "o":
                    done = dve.tensor_tensor(x[:, k, half * HALF:(half + 1) * HALF], ps,
                                             x[:, k, half * HALF:(half + 1) * HALF], ALU.add)
                else:
                    if not half and UNIT_OF.index(j):
                        dve.wait_ge(qk_gain, UNIT_OF.index(j))
                    done = dve.tensor_tensor(T[0][:, half * HALF:(half + 1) * HALF], ps, rstd[:, half, :], ALU.mult)
                done.then_inc(unit_read if half else half_read, 1)

            def head_inverse(i):
                g = CHAIN["qk"] + i
                if QK[i][1] == "k":
                    inverse(g)
                    return
                dve.wait_ge(root_done, g + 1)
                dve.reciprocal(q_scale[:, QK[i][2], :], root[:, g % 2, :]).then_inc(inv_done, 1)
                dve.wait_ge(inv_done, g + 1)
                dve.tensor_scalar(q_scale[:, QK[i][2], :], q_scale[:, QK[i][2], :], HD ** -0.5, None,
                                  ALU.mult).then_inc(q_scaled, 1)

            def turned(i, half):
                tokens = slice(half * HALF, (half + 1) * HALF)
                bank = 0 if QK[i][1] == "k" and half else 3
                dve.wait_ge(rot_done, 2 * i + half + 1)
                dve.tensor_tensor(T[1][:, tokens], misc_ps[:, bank, 0:HALF], ropes[:, 1, tokens], ALU.mult).then_inc(rot_read, 1)
                if QK[i][1] == "k" and half:
                    dve.wait_ge(qk_sum, i + 1)
                    dve.wait_ge(bc_done, broadcasts(CHAIN["qk"] + i))
                    dve.tensor_tensor(two(T[4][:, :]), two(T[4][:, :]), misc_ps[:, 1:3, 0:HALF], ALU.mult).then_inc(bc_read, 1)

            def largest(j):
                _, h, s0, ln, qt = STEPS[j]
                dve.wait_ge(s_done, j + 1)
                if j >= 2:
                    dve.wait_ge(s_exp, j - 1)
                dve.reduce_max(negmax[:, j % 2, 0:1], misc_ps[:, j % 2, 0:ln], AX.X).then_inc(s_max, 1)
                dve.wait_ge(s_max, j + 1)
                dve.tensor_scalar(negmax[:, j % 2, 1:2], negmax[:, j % 2, 0:1],
                                  q_scale[:, h, s0 // P + qt:s0 // P + qt + 1], -1.0, ALU.mult, ALU.mult).then_inc(s_neg, 1)

            def normalized(j):
                ln = STEPS[j][3]
                dve.wait_ge(s_exp, j + 1)
                dve.reciprocal(expsum[:, j % 2, 1:2], expsum[:, j % 2, 0:1]).then_inc(s_inv, 1)
                dve.wait_ge(s_inv, j + 1)
                dve.tensor_scalar(probs[j % 3][:, 0:ln], probs[j % 3][:, 0:ln], expsum[:, j % 2, 1:2], None,
                                  ALU.mult).then_inc(s_norm, 1)

            def result_lo(a):
                h, s0, ln = ITEMS[a]
                dve.wait_ge(pv_hi, a + 1)
                dve.tensor_tensor(pairB[:, h, 1, s0:s0 + ln], values_bank[:, 0:ln],
                                  pairB[:, h, 0, s0:s0 + ln].bitcast(F32), ALU.subtract).then_inc(pv_lo, 1)

            trunk_norm(CHAIN["c"])
            dve.wait_ge(rope_landed, 16)
            for slot in range(SLOTS):
                j = slot // 8
                if slot % 8 == 0 and 0 < j <= len(C_UNITS):
                    evacuate_half(j - 1, 1)
                elif slot % 8 == 4 and j < len(C_UNITS):
                    evacuate_half(j, 0)
                for what, i, *half in PLAN.get(slot, ()):
                    if what == "sums":
                        head_inverse(i)
                    elif what == "turn":
                        turned(i, *half)
                    elif what == "scores":
                        largest(i)
                    elif what == "softmax":
                        normalized(i)
                    elif what == "result":
                        result_lo(i)
                if slot % 8 == 0 and 0 < j <= len(C_UNITS):
                    ahead(BASE["c"] + j - 1)
            out_projection("c_out", 3, "ffn1", pairA)
            ffn(1, CHAIN["ffn1"], None)
            for f in range(KT):
                n = BASE["store"] + f
                dve.wait_ge(unit_done, n + 1)
                for h in range(2):
                    last = dve.tensor_copy(y_tok[:, h * HT:(h + 1) * HT, f * P:(f + 1) * P],
                                           unit_ps[:, n % 2, h, 0:HALF].rearrange("p (m e) -> p m e", m=HT))
                last.then_inc(unit_read, 1)

        @block.gpsimd
        def _(pool):
            def sum_squares(f, odd):
                pool.wait_ge(sq_ready, f + 1)
                pool.tensor_tensor(sumsq[:, :], sumsq[:, :], T[2 + odd][:, :], ALU.add).then_inc(sq_summed, 1)

            def squares(r, g_last):
                if g_last is not None:
                    pool.wait_ge(colsum_done, g_last + 1)
                pool.memset(sumsq[:, :], 0.0).then_inc(sum_zeroed, 1)
                pool.wait_ge(sum_zeroed, r + 1)
                if r == 0:
                    for f in range(KT):
                        if f:
                            pool.wait_ge(sq_summed, f)
                        sum_squares(f, f % 2)
                    return
                with pool.Fori(0, KT // 2) as i:
                    for odd in range(2):
                        pool.wait_ge(sq_summed, KT * r + odd + 2 * i)
                        sum_squares(KT * r + odd + 2 * i, odd)

            squares(0, None)
            def keys(dt):
                pool.wait_ge(exp_neg, dt + 1)
                pool.tensor_tensor(kin[:, dt % 2, :], k_ab[:, dt % 2, :], T[4][:, :], ALU.mult).then_inc(k_gated, 1)

            pool.wait_ge(gate_summed, 4)
            keys(0)
            keys(1)
            pool.wait_ge(unit_done, BASE["fnet"])
            pool.wait_ge(k_gated, 2)
            for e in range(2):
                if e:
                    pool.wait_ge(kintok_zeroed, 1)
                pool.memset(kintok[e * CHUNK:(e + 1) * CHUNK, :, :, 1 - e, :], 0.0).then_inc(kintok_zeroed, 1)
            pool.wait_ge(kintok_zeroed, 2)
            for e in range(2):
                if e:
                    pool.wait_ge(qpad_zeroed, 1)
                pool.memset(qpad[e * DK:(e + 1) * DK, 1 - e:HEADS:2, :], 0.0).then_inc(qpad_zeroed, 1)
            pool.wait_ge(att_done, TT)
            keys(2)
            keys(3)

            def ffn(layer):
                done = FT * layer
                for c, tiles in enumerate(CHUNKS):
                    n0 = BASE[f"gate_up{layer}{c}"]
                    with pool.Fori(0, tiles) as i:
                        pool.wait_ge(silu_done, done + 1 + i)
                        pool.wait_ge(unit_read, reads(n0 + 1) + 2 * i)
                        pool.tensor_tensor(T[1][:, :], T[0][:, :], T[1][:, :], ALU.mult).then_inc(prod_done, 1)
                        pool.wait_ge(act_hi, done + 1 + i)
                        pool.tensor_tensor(pairB[:, i, 1, :], T[1][:, :], pairB[:, i, 0, :].bitcast(F32),
                                           ALU.subtract).then_inc(act_lo, 1)
                    done += tiles

            squares(1, CHAIN["ab"])
            ffn(0)
            squares(2, CHAIN["ffn0"])
            pool.wait_ge(h_lo, KT * 3)
            pool.dma_start(ropes[:, :, :], rope.rearrange("p (a t) -> p a t", a=2)).then_inc(rope_landed, 16)
            pool.wait_ge(rope_landed, 16)
            for i, (_, kind, k) in enumerate(QK):
                pair = kpair[:, k] if kind == "k" else pairB[:, k]
                pool.wait_ge(qk_gain, i + 1)
                if i:
                    pool.wait_ge(qk_lo, i)
                pool.tensor_tensor(T[4][:, :], T[2 + i % 2][:, :], ropes[:, 0, :], ALU.mult).then_inc(qk_cos, 1)
                pool.wait_ge(qk_cos, i + 1)
                pool.wait_ge(rot_read, 2 * i + 2)
                pool.tensor_tensor(T[4][:, :], T[4][:, :], T[1][:, :], ALU.add).then_inc(qk_sum, 1)
                pool.wait_ge(qk_hi, i + 1)
                pool.tensor_tensor(pair[:, 1, :], T[4][:, :], pair[:, 0, :].bitcast(F32), ALU.subtract).then_inc(qk_lo, 1)
            pool.wait_ge(pv_done, len(ITEMS))
            squares(3, CHAIN["c"])
            ffn(1)


def _tables():
    ident = np.eye(P)
    i = np.arange(P)
    same = (i[:, None] // CHUNK) == (i[None, :] // CHUNK)
    forward = same & (i[:, None] <= i[None, :])
    backward = same & (i[:, None] >= i[None, :])
    rot = np.zeros((P, P))
    q = HD // 4
    for half in (0, HD // 2):
        for k in range(q):
            rot[half + q + k, half + k] = -1.0
            rot[half + k, half + q + k] = 1.0
    return np.concatenate([ident, forward, backward, rot], axis=1).astype(np.float32)


def _rope():
    half = HD // 2
    inv = (np.float32(ROPE_THETA) ** (-np.arange(0, half, 2, dtype=np.float32) / np.float32(half))).astype(np.float32)
    t = np.concatenate([np.arange(SEQ), np.arange(DEC)])
    out = []
    for fn in (np.cos, np.sin):
        rows = []
        for d in range(HD):
            pos = (t // GRID_W if d < half else t % GRID_W).astype(np.float32)
            rows.append(fn(pos * inv[d % (half // 2)]))
        out.append(np.stack(rows))
    return np.concatenate(out, axis=1).astype(np.float32)


def _dft():
    def cs(n):
        k = np.outer(np.arange(n), np.arange(n)) % n
        return np.cos(2 * np.pi * k / n), np.sin(2 * np.pi * k / n)

    out = np.zeros((6, P, SLOT))
    out[0, :, 0:2 * FW] = np.concatenate(cs(FW), axis=1)
    c, s = cs(SEQ)
    both = (np.concatenate([c, -s]) / np.sqrt(SEQ * FW)).reshape(8, P, SEQ)
    for j in range(4):
        out[1 + j] = np.concatenate([both[2 * j], both[2 * j + 1]], axis=1)
    c, s = cs(DEC)
    both = (np.concatenate([c, -s]) / np.sqrt(DEC * FW)).reshape(4, P, DEC)
    out[5] = np.concatenate(list(both), axis=1)
    return out.astype(np.float32)


def kernel(x_prompt, x_sample, ab_norm, ab_w_in, gla_up_f, gla_bias_f, gla_up_b, gla_bias_b, gla_out_norm, ab_w_out,
           c_norm, c_w_in, c_q_norm, c_k_norm, c_w_out, ffn_norm, ffn_w_gate, ffn_w_up, ffn_w_down):
    import concourse.bacc as bacc
    from concourse.bass_utils import run_bass_kernel_spmd

    def tiles(v):
        return np.asarray(v).reshape(-1, P).T

    eps = np.full((P, 1), EPS, np.float32)
    columns = np.concatenate([tiles(ab_norm[0]), tiles(ffn_norm[0]), tiles(c_norm[0]), tiles(ffn_norm[1]),
                              tiles(gla_out_norm[0]), tiles(c_q_norm[0]), tiles(c_k_norm[0]), tiles(gla_bias_f[0]),
                              tiles(gla_bias_b[0]), eps], axis=1)
    up_pad = np.zeros((2 * RANK, 4 * P), np.float32)
    up_pad[0:RANK, 0:2 * P] = gla_up_f[0]
    up_pad[RANK:, 2 * P:] = gla_up_b[0]
    arrays = {
        "in_x_prompt": np.asarray(x_prompt)[0], "in_x_sample": np.asarray(x_sample)[0],
        "in_ab_w_in": np.asarray(ab_w_in)[0], "in_ab_w_out": np.asarray(ab_w_out)[0],
        "in_c_w_in": np.asarray(c_w_in)[0], "in_c_w_out": np.asarray(c_w_out)[0],
        "in_w_gate": ffn_w_gate, "in_w_up": ffn_w_up, "in_w_down": ffn_w_down,
        "in_columns": columns, "in_up_pad": up_pad,
        "const_tables": _tables(), "const_rope": _rope(), "const_dft": _dft(),
    }
    arrays = {k: np.ascontiguousarray(v) for k, v in arrays.items()}
    nc = bacc.Bacc("TRN2", target_bir_lowering=False, num_devices=1)
    args = [nc.dram_tensor(k, v.shape, mybir.dt.from_np(v.dtype), kind="ExternalInput").ap() for k, v in arrays.items()]
    for name, n in (("out_prompt", SEQ), ("out_sample", DEC)):
        args.append(nc.dram_tensor(name, (n, D), F32, kind="ExternalOutput").ap())
    trunk_kernel(nc, *args)
    r = run_bass_kernel_spmd(nc, [arrays], core_ids=[0]).results[0]
    return r["out_prompt"][None], r["out_sample"][None]
```
